# Optimizing a Trainium2 kernel written in Bass

```python
import jax, jax.numpy as jnp
from jax import lax
import numpy as np

D_MODEL = 2048
BATCH = 1
SEQ = 256
DEPTH = 1

ATTN_HEAD_DIM = 64
N_Q_HEADS = D_MODEL // 128
N_KV_HEADS = N_Q_HEADS // 4
Q_PER_KV = N_Q_HEADS // N_KV_HEADS
WINDOW = 128
ATTN_BLOCK = WINDOW
ATTN_WIDTH = N_Q_HEADS * ATTN_HEAD_DIM
KV_WIDTH = N_KV_HEADS * ATTN_HEAD_DIM
HGRN_HEAD_DIM = 128
HGRN_HEADS = D_MODEL // 256
HGRN_WIDTH = HGRN_HEADS * HGRN_HEAD_DIM
HGRN_CHUNK = 64
N_BRANCHES = 2
IN_WIDTH = ATTN_WIDTH + 2 * KV_WIDTH + 4 * HGRN_WIDTH + N_BRANCHES * D_MODEL
N_GROUPS = 4
EXPERTS_PER_GROUP = 8
N_EXPERTS = N_GROUPS * EXPERTS_PER_GROUP
TOP_K = 2
D_EXPERT = D_MODEL // 4
MOE_BLOCK = 128
EPS = 1e-6

kernel_name = "hybrid_swa_sink_hgrn2_hmoe_block"

def rmsnorm(x, g):
    x32 = x.astype(jnp.float32)
    y = x32 * lax.rsqrt(jnp.mean(x32 * x32, axis=-1, keepdims=True) + EPS)
    return (y * g.astype(jnp.float32)).astype(x.dtype)

def sliding_window_sink_attention(q, k, v, sinks):
    B, S, _ = q.shape
    nb = S // ATTN_BLOCK
    q = q.reshape(B, nb, ATTN_BLOCK, N_KV_HEADS, Q_PER_KV, ATTN_HEAD_DIM)
    k = k.reshape(B, nb, ATTN_BLOCK, N_KV_HEADS, ATTN_HEAD_DIM)
    v = v.reshape(B, nb, ATTN_BLOCK, N_KV_HEADS, ATTN_HEAD_DIM)

    def band(t):
        prev = jnp.concatenate([jnp.zeros_like(t[:, :1]), t[:, :-1]], axis=1)
        return jnp.concatenate([prev, t], axis=2)

    kb, vb = band(k), band(v)
    scores = jnp.einsum('bnqhgd,bnkhd->bnhgqk', q, kb).astype(jnp.float32) * (ATTN_HEAD_DIM ** -0.5)
    qi = jnp.arange(ATTN_BLOCK)[:, None]
    kj = jnp.arange(2 * ATTN_BLOCK)[None, :]
    rel = ATTN_BLOCK + qi - kj
    in_window = (rel >= 0) & (rel < WINDOW)
    key_exists = (jnp.arange(nb) > 0)[:, None, None] | (kj >= ATTN_BLOCK)[None]
    mask = in_window[None] & key_exists
    scores = jnp.where(mask[None, :, None, None], scores, -jnp.inf)
    sink = sinks.astype(jnp.float32).reshape(N_KV_HEADS, Q_PER_KV)[None, None, :, :, None, None]
    sink = jnp.broadcast_to(sink, scores.shape[:-1] + (1,))
    probs = jax.nn.softmax(jnp.concatenate([scores, sink], axis=-1), axis=-1)[..., :-1]
    out = jnp.einsum('bnhgqk,bnkhd->bnqhgd', probs.astype(v.dtype), vb)
    return out.reshape(B, S, ATTN_WIDTH)

def hgrn2_recurrence(q, f_logit, i, lower_bound):
    B, S, _ = q.shape
    nc = S // HGRN_CHUNK

    def chunks(t):
        t = t.reshape(B, nc, HGRN_CHUNK, HGRN_HEADS, HGRN_HEAD_DIM)
        return t.transpose(1, 0, 3, 2, 4).astype(jnp.float32)

    lb = lower_bound.astype(jnp.float32).reshape(HGRN_HEADS, 1, HGRN_HEAD_DIM)
    f = lb + (1.0 - lb) * jax.nn.sigmoid(chunks(f_logit))
    qh = jax.nn.silu(chunks(q)) * (HGRN_HEAD_DIM ** -0.5)
    kh = 1.0 - f
    vh = chunks(i)
    gh = jnp.log(f)
    causal = jnp.tril(jnp.ones((HGRN_CHUNK, HGRN_CHUNK), dtype=bool))

    def step(state, inp):
        qc, kc, vc, gc = inp
        b = jnp.cumsum(gc, axis=-2)
        diff = b[:, :, :, None, :] - b[:, :, None, :, :]
        decay = jnp.exp(jnp.where(causal[None, None, :, :, None], diff, -jnp.inf))
        attn = jnp.einsum('bhtk,bhsk,bhtsk->bhts', qc, kc, decay)
        o = jnp.einsum('bhts,bhsv->bhtv', attn, vc) + jnp.einsum('bhtk,bhkv->bhtv', qc * jnp.exp(b), state)
        b_last = b[:, :, -1:, :]
        new_state = jnp.exp(b_last[:, :, 0, :])[..., None] * state + \
            jnp.einsum('bhsk,bhsv->bhkv', kc * jnp.exp(b_last - b), vc)
        return new_state, o

    s0 = jnp.zeros((B, HGRN_HEADS, HGRN_HEAD_DIM, HGRN_HEAD_DIM), jnp.float32)
    _, o = lax.scan(step, s0, (qh, kh, vh, gh))
    return o.transpose(1, 0, 3, 2, 4).reshape(B, S, HGRN_HEADS, HGRN_HEAD_DIM)

def hierarchical_moe(xn, w_rg, b_rg, w_re, b_re, w1, w3, w2):
    B, S, D = xn.shape
    T = B * S
    xf = xn.reshape(T, D)
    p_group = jax.nn.softmax((xf @ w_rg).astype(jnp.float32) + b_rg.astype(jnp.float32), axis=-1)
    group = jnp.argmax(p_group, axis=-1)
    p_sel_group = jnp.take_along_axis(p_group, group[:, None], axis=-1)
    e_logits = ((xf @ w_re).astype(jnp.float32) + b_re.astype(jnp.float32)).reshape(T, N_GROUPS, EXPERTS_PER_GROUP)
    e_logits = jnp.take_along_axis(e_logits, group[:, None, None], axis=1)[:, 0]
    top_p, top_i = lax.top_k(jax.nn.softmax(e_logits, axis=-1), TOP_K)
    weights = p_sel_group * top_p / jnp.sum(top_p, axis=-1, keepdims=True)
    expert = group[:, None] * EXPERTS_PER_GROUP + top_i

    n_assign = T * TOP_K
    flat_e = expert.reshape(-1)
    flat_w = weights.reshape(-1)
    flat_tok = jnp.arange(n_assign) // TOP_K
    order = jnp.argsort(flat_e, stable=True)
    sorted_e = flat_e[order]
    sorted_tok = flat_tok[order]
    counts = jnp.bincount(flat_e, length=N_EXPERTS)
    padded = ((counts + MOE_BLOCK - 1) // MOE_BLOCK) * MOE_BLOCK
    pad_end = jnp.cumsum(padded)
    pad_start = pad_end - padded
    start = jnp.cumsum(counts) - counts
    dest = pad_start[sorted_e] + (jnp.arange(n_assign) - start[sorted_e])
    n_blocks = -(-n_assign // MOE_BLOCK) + N_EXPERTS
    block_expert = jnp.clip(jnp.searchsorted(pad_end, jnp.arange(n_blocks) * MOE_BLOCK, side='right'), 0, N_EXPERTS - 1)
    rows = jnp.zeros((n_blocks * MOE_BLOCK, D), xf.dtype).at[dest].set(xf[sorted_tok])

    def expert_block(args):
        xb, e = args
        hb = jax.nn.silu(xb @ w1[e]) * (xb @ w3[e])
        return hb @ w2[e]

    y_rows = lax.map(expert_block, (rows.reshape(n_blocks, MOE_BLOCK, D), block_expert)).reshape(-1, D)
    contrib = y_rows[dest].astype(jnp.float32) * flat_w[order][:, None]
    out = jnp.zeros((T, D), jnp.float32).at[sorted_tok].add(contrib)
    return out.reshape(B, S, D).astype(xn.dtype)

def setup_inputs(seed: int = 0) -> dict:
    key = jax.random.key(seed)
    ks = jax.random.split(key, 18)
    f32 = jnp.float32
    nrm = lambda k, shape, s: jax.random.normal(k, shape, f32) * s
    return {
        "x": nrm(ks[0], (BATCH, SEQ, D_MODEL), 1.0),
        "w_in": nrm(ks[1], (DEPTH, D_MODEL, IN_WIDTH), D_MODEL ** -0.5),
        "attn_sinks": nrm(ks[2], (DEPTH, N_Q_HEADS), 1.0),
        "hgrn_lb_logits": nrm(ks[3], (DEPTH + 1, HGRN_WIDTH), 0.5),
        "hgrn_norm_g": 1.0 + nrm(ks[4], (DEPTH, HGRN_HEAD_DIM), 0.02),
        "w_br_attn": nrm(ks[5], (DEPTH, ATTN_WIDTH, D_MODEL), ATTN_WIDTH ** -0.5),
        "w_br_hgrn": nrm(ks[6], (DEPTH, HGRN_WIDTH, D_MODEL), HGRN_WIDTH ** -0.5),
        "w_out": nrm(ks[7], (DEPTH, D_MODEL, D_MODEL), D_MODEL ** -0.5),
        "mix_norm_g": 1.0 + nrm(ks[8], (DEPTH, D_MODEL), 0.02),
        "moe_norm_g": 1.0 + nrm(ks[9], (DEPTH, D_MODEL), 0.02),
        "w_router_group": nrm(ks[10], (DEPTH, D_MODEL, N_GROUPS), D_MODEL ** -0.5),
        "b_router_group": nrm(ks[11], (DEPTH, N_GROUPS), 0.01),
        "w_router_expert": nrm(ks[12], (DEPTH, D_MODEL, N_EXPERTS), D_MODEL ** -0.5),
        "b_router_expert": nrm(ks[13], (DEPTH, N_EXPERTS), 0.01),
        "w1": nrm(ks[14], (DEPTH, N_EXPERTS, D_MODEL, D_EXPERT), D_MODEL ** -0.5),
        "w3": nrm(ks[15], (DEPTH, N_EXPERTS, D_MODEL, D_EXPERT), D_MODEL ** -0.5),
        "w2": nrm(ks[16], (DEPTH, N_EXPERTS, D_EXPERT, D_MODEL), D_EXPERT ** -0.5),
        "final_norm_g": 1.0 + nrm(ks[17], (D_MODEL,), 0.02),
    }

def reference(x, w_in, attn_sinks, hgrn_lb_logits, hgrn_norm_g, w_br_attn, w_br_hgrn, w_out,
              mix_norm_g, moe_norm_g, w_router_group, b_router_group, w_router_expert,
              b_router_expert, w1, w3, w2, final_norm_g):
    B, S, _ = x.shape
    widths = [ATTN_WIDTH, KV_WIDTH, KV_WIDTH, HGRN_WIDTH, HGRN_WIDTH, HGRN_WIDTH, HGRN_WIDTH, N_BRANCHES * D_MODEL]
    splits = [int(c) for c in np.cumsum(widths)[:-1]]
    lb_table = jnp.cumsum(jax.nn.softmax(hgrn_lb_logits.astype(jnp.float32), axis=0), axis=0)
    h = x
    for l in range(DEPTH):
        xn = rmsnorm(h, mix_norm_g[l])
        proj = xn @ w_in[l]
        q_a, k_a, v_a, q_h, f_h, i_h, og_h, gate_logits = jnp.split(proj, splits, axis=-1)
        o_a = sliding_window_sink_attention(q_a, k_a, v_a, attn_sinks[l])
        o_h = hgrn2_recurrence(q_h, f_h, i_h, lb_table[l])
        o_h = rmsnorm(o_h, hgrn_norm_g[l]) * jax.nn.silu(og_h.astype(jnp.float32).reshape(B, S, HGRN_HEADS, HGRN_HEAD_DIM))
        o_h = o_h.reshape(B, S, HGRN_WIDTH).astype(h.dtype)
        gates = jax.nn.sigmoid(gate_logits.astype(jnp.float32)).reshape(B, S, N_BRANCHES, D_MODEL)
        y_a = o_a @ w_br_attn[l]
        y_h = o_h @ w_br_hgrn[l]
        merged = (gates[:, :, 0] * y_a + gates[:, :, 1] * y_h).astype(h.dtype)
        h = h + merged @ w_out[l]
        hn = rmsnorm(h, moe_norm_g[l])
        h = h + hierarchical_moe(hn, w_router_group[l], b_router_group[l], w_router_expert[l],
                                 b_router_expert[l], w1[l], w3[l], w2[l])
    return rmsnorm(h, final_norm_g)


_drawn_inputs = setup_inputs


def setup_inputs(seed=0):
    import zlib

    import numpy as np

    out = dict(_drawn_inputs(seed))
    spreads = {}
    factors = {'attn_sinks': 3.409,
     'hgrn_norm_g': 3.257,
     'b_router_group': 7.684,
     'final_norm_g': 7.963,
     'b_router_expert': 6.108}
    for name, (base, spread) in spreads.items():
        noise = np.random.default_rng([zlib.crc32(name.encode()), seed]).standard_normal(out[name].shape)
        drawn = base * np.exp(spread * noise) if base else spread * noise
        out[name] = __import__('jax').numpy.asarray(drawn.astype(out[name].dtype))
    for name, factor in factors.items():
        out[name] = (out[name] * factor).astype(out[name].dtype)
    return out
```

```python
from contextlib import ExitStack

import concourse.bass as bass
from concourse import mybir

F32 = mybir.dt.float32
ALU = mybir.AluOpType
ACT = mybir.ActivationFunctionType
AX = mybir.AxisListType

P = 128
D = 2048
T = 256
TB = T // P
KD = D // P
CH = 512
KS = 8
NC = D // CH
HEADS = 8
DH = 64
HW = 128
LEVELS = 7
W_ATT = 1024
KV = 256
C_HGRN = W_ATT + 2 * KV
C_GATE = C_HGRN + 4 * W_ATT
RING = 4
EPS = 1e-6
ONE = 1
NEG = -1e30
NG = 4
EG = 8
NE = NG * EG
NR = NG + NE
FE = 512
SL = 32
CAP = SL
GX = P // SL
GROUPS = NE // GX
LIST = 16
BIG = 1000.0

K_LEV = 0
K_ATT = K_LEV + (LEVELS + 1) * P
K_ID = K_ATT + 3 * P
K_TRI = K_ID + P
K_IOTA = K_TRI + P
K_ONE = K_IOTA + 2 * P
K_EPS = K_ONE + P
K_END = K_EPS + 8


def constants():
    import numpy as np
    s = np.arange(P)[:, None]
    t = np.arange(P)[None, :]
    out = np.zeros((P, K_END), np.float32)
    for lev in range(LEVELS + 1):
        if lev == 0:
            m = s == t
        else:
            half = 1 << (lev - 1)
            m = (s >> lev == t >> lev) & (s & half == 0) & (t & half != 0)
        out[:, K_LEV + lev * P:K_LEV + (lev + 1) * P] = m
    causal = np.where(t <= s, 0.0, NEG)
    out[:, K_ATT:K_ATT + P] = causal
    out[:, K_ATT + P:K_ATT + 2 * P] = np.where(t > s, 0.0, NEG)
    out[:, K_ATT + 2 * P:K_ATT + 3 * P] = causal
    out[:, K_ID:K_ID + P] = s == t
    out[:, K_TRI:K_TRI + P] = s < t
    out[:, K_IOTA:K_IOTA + 2 * P] = np.arange(2 * P)[None, :]
    out[:, K_ONE:K_ONE + P] = 1.0
    out[:, K_EPS] = EPS
    return out


class Chain:

    def __init__(self, eng, sem):
        self.eng, self.sem, self.base, self.n = eng, sem, 0, 0

    def link(self, ins):
        self.n += 1
        ins.then_inc(self.sem, 1)
        self.eng.wait_ge(self.sem, self.base + self.n)

    def enter(self, i, per):
        self.start = self.base + self.n
        self.base, self.n, self.per = self.start + i * per, 0, per

    def leave(self, times):
        assert self.n == self.per, (self.n, self.per)
        self.base, self.n = self.start + times * self.per, 0


def settle(eng, sem):
    eng.wait_ge(sem, 16 * 3)


def bc(ap, shape):
    return ap.broadcast_to(shape)


def hybrid_block(nc, x, w_in, attn_sinks, hgrn_lb_logits, hgrn_norm_g, w_br_attn, w_br_hgrn, w_out,
                 mix_norm_g, moe_norm_g, w_router_group, b_router_group, w_router_expert,
                 b_router_expert, w1, w3, w2, final_norm_g, consts, out):
    ctx = ExitStack()
    with ctx:
        def sb(name, shape, dt=F32):
            return ctx.enter_context(nc.sbuf_tensor(name, shape, dt))

        def ps(name, shape):
            return ctx.enter_context(nc.psum_tensor(name, shape, F32))

        def sem(name):
            return ctx.enter_context(nc.semaphore(name))

        wslot = sb("wslot", [P, 6, KS * CH])
        actT = sb("actT", [P, KD, T])
        resid = sb("resid", [P, TB, D])
        gates = sb("gates", [P, TB, 2 * D])
        norm_g = sb("norm_g", [P, D])
        qa = sb("qa", [P, TB, W_ATT])
        kv = sb("kv", [P, TB, 2 * KV])
        oaT = sb("oaT", [P, HEADS, T])
        ohT = sb("ohT", [P, HEADS, T])
        cst = sb("cst", [P, K_END])
        sinks = sb("sinks", [P, 2 * HEADS])
        hnorm = sb("hnorm", [P, HW])
        lbT = sb("lbT", [P, HEADS])
        stat = sb("stat", [P, 32])
        small = sb("small", [P, 64])
        over_i = sb("over_i", [P, LIST + 1], mybir.dt.int32)
        ident = cst[:, K_ID:K_ID + P]

        work = wslot[:, 4:6, :].rearrange("p a n -> p (a n)")
        at = [0]

        def carve(*shape):
            n = 1
            for s in shape:
                n *= s
            ap = work[:, at[0]:at[0] + n]
            at[0] += n
            assert at[0] <= 2 * KS * CH
            if len(shape) == 2:
                return ap.rearrange("p (a b) -> p a b", a=shape[0])
            if len(shape) == 3:
                return ap.rearrange("p (a b c) -> p a b c", a=shape[0], b=shape[1])
            return ap
        qs = carve(TB, P)
        ks = carve(TB, P)
        vs = carve(TB, DH)
        qkT = carve(2, T)
        prob = carve(2, 3 * P)
        probT = carve(2, 3 * P)
        es = carve(TB, 3 * P)
        qrow = carve(TB, HW)
        frow = carve(TB, HW)
        orow = carve(TB, HW)
        irow = carve(TB, HW)
        qT = carve(T)
        fT = carve(T)
        qp = carve(T)
        kq = carve(T)
        tot = carve(T)
        hatt = carve(T)
        crossT = carve(P)
        oh = carve(TB, HW)
        sk = carve(2, 2)
        lbs = carve(2)
        mx = carve(2, 2)
        mneg = carve(2, 2)
        esink = carve(2, 2)
        psums = carve(2, 2)
        rden = carve(2, 2)
        lbrow = carve(2, P)
        lev = norm_g[:, :].rearrange("p (l t) -> p l t", l=LEVELS + 1)
        merged = norm_g[:, 0:TB * CH].rearrange("p (b n) -> p b n", b=TB)
        merged2 = norm_g[:, TB * CH:2 * TB * CH].rearrange("p (b n) -> p b n", b=TB)

        pair = [ps("pair0", [P, TB, CH]), ps("pair1", [P, TB, CH])]
        four = ps("four", [P, 4, CH])
        flat4 = four[:, :, :].rearrange("p a n -> p (a n)")
        levp = flat4.rearrange("p (l t) -> p l t", l=8)
        bank_t = four[:, 2, :]
        bank_o = four[:, 3, :]

        x_in = sem("x_in")
        g_in = sem("g_in")
        c_in = sem("c_in")
        loaded = [sem(f"loaded{s}") for s in range(6)]
        slot_used = sem("slot_used")
        dve_step = sem("dve_step")
        act_step = sem("act_step")
        rstd_done = sem("rstd_done")
        xn_ready = sem("xn_ready")
        tp_ready = sem("tp_ready")
        tp_copied = sem("tp_copied")
        lb_in = sem("lb_in")
        lb_rows = sem("lb_rows")
        lb_e = sem("lb_e")
        lb_s = sem("lb_s")
        lb_t = sem("lb_t")
        lb_done = sem("lb_done")
        pair0_act = sem("pair0_act")
        pair1_act = sem("pair1_act")
        pair0_dve = sem("pair0_dve")
        staged = sem("staged")
        qkT_ready = sem("qkT_ready")
        qkT_copied = sem("qkT_copied")
        score_ready = sem("score_ready")
        max_ready = sem("max_ready")
        exp_done = sem("exp_done")
        prob_ready = sem("prob_ready")
        probT_ready = sem("probT_ready")
        probT_copied = sem("probT_copied")
        oT_ready = sem("oT_ready")
        oaT_done = sem("oaT_done")
        es_ready = sem("es_ready")
        hg_rows = sem("hg_rows")
        qfT_ready = sem("qfT_ready")
        qT_copied = sem("qT_copied")
        level_ops = sem("level_ops")
        level_mm = sem("level_mm")
        lev_read = sem("lev_read")
        cross_mm = sem("cross_mm")
        cross_copied = sem("cross_copied")
        hatt_ready = sem("hatt_ready")
        ho_ready = sem("ho_ready")
        ho_sq = sem("ho_sq")
        oh_ready = sem("oh_ready")
        ohT_ready = sem("ohT_ready")
        ohT_done = sem("ohT_done")
        y_read = sem("y_read")
        merged_ready = sem("merged_ready")
        mT_ready = sem("mT_ready")
        mT_done = sem("mT_done")
        h_added = sem("h_added")
        g2_in = sem("g2_in")
        g3_in = sem("g3_in")
        r_in = sem("r_in")
        logit_ready = sem("logit_ready")
        logit_read = sem("logit_read")
        r_exp_in = sem("r_exp_in")
        r_exp = sem("r_exp")
        coef_ready = sem("coef_ready")
        gathered = sem("gathered")
        xg_copied = sem("xg_copied")
        swT_ready = sem("swT_ready")
        swT_copied = sem("swT_copied")
        onehot_ready = sem("onehot_ready")
        sw_ready = sem("sw_ready")
        ghid_ready = sem("ghid_ready")
        ge_exp = sem("ge_exp")
        ghT_ready = sem("ghT_ready")
        ghT_copied = sem("ghT_copied")
        yg_act = sem("yg_act")
        yg_dve = sem("yg_dve")
        back_ready = sem("back_ready")
        scattered = sem("scattered")
        quarter_used = sem("quarter_used")
        mask_ready = sem("mask_ready")
        rank_ready = sem("rank_ready")
        rank_read = sem("rank_read")
        over_ready = sem("over_ready")
        over_step = sem("over_step")
        oh13_ready = sem("oh13_ready")
        oy_ready = sem("oy_ready")
        resid_done = sem("resid_done")
        e_exp = sem("e_exp")
        hid_ready = sem("hid_ready")
        hidT_ready = sem("hidT_ready")
        hidT_copied = sem("hidT_copied")
        y_added = sem("y_added")
        o_ready = sem("o_ready")
        stored = sem("stored")

        gflat = gates[:, :, :].rearrange("p a n -> p (a n)")
        hn = gates[:, :, 0:D]
        hid = gates[:, :, D:D + FE]
        ehid = gates[:, :, D + FE:D + 2 * FE]
        xg = gates[:, 0, D:2 * D].rearrange("p (k n) -> p k n", k=KD)
        yg = gates[:, 1, D:2 * D]
        gwork = ohT[:, :, :].rearrange("p a n -> p (a n)")
        gh = gwork[:, 0:T].rearrange("p (b n) -> p b n", b=TB)
        sw = gwork[:, T:2 * T].rearrange("p (b n) -> p b n", b=TB)
        swT = gwork[:, 2 * T:3 * T]
        geh = gwork[:, 3 * T:3 * T + P]
        ghid = gwork[:, 3 * T + P:4 * T]
        ghT = gwork[:, 4 * T:4 * T + P]
        hidT = gates[:, :, D + 2 * FE:D + 4 * FE].rearrange("p b (k t) -> p b k t", k=4)[:, :, :, 0:P]
        wr = qa[:, :, :].rearrange("p a n -> p (a n)")[:, 0:KD * NR].rearrange("p (k n) -> p k n", k=KD)
        br = kv[:, 0, 0:NR]
        rwork = kv[:, :, :].rearrange("p a n -> p (a n)")
        coef = oaT[:, 0, 0:TB * NE].rearrange("p (b e) -> p b e", b=TB)
        rmask = oaT[:, 1, 0:TB * NE].rearrange("p (b e) -> p b e", b=TB)
        place = oaT[:, 2, 0:TB * NE].rearrange("p (b e) -> p b e", b=TB)
        late = oaT[:, 3, 0:TB * NE].rearrange("p (b e) -> p b e", b=TB)
        ocoef = oaT[:, 4, 0:TB * NE].rearrange("p (b e) -> p b e", b=TB)
        lrow = oaT[:, 5, 0:2 * NE + LIST + 1]
        llist = oaT[0:1, 6:8, :].rearrange("p a n -> p (a n)").rearrange("p (j e) -> p j e", j=LIST)

        w_in_k = w_in[0].rearrange("(k p) n -> p k n", p=P)
        w_gather = w_in[0][:, C_HGRN:C_GATE].rearrange("(k p) (j c) -> p k j c", p=P, j=4)
        wa_k = w_br_attn[0].rearrange("(k p) n -> p k n", p=P)
        wh_k = w_br_hgrn[0].rearrange("(k p) n -> p k n", p=P)
        wo_k = w_out[0].rearrange("(k p) n -> p k n", p=P)
        w1_k = w1[0].rearrange("e (p k) f -> e p k f", p=P)
        w3_k = w3[0].rearrange("e (p k) f -> e p k f", p=P)
        w2_k = w2[0].rearrange("e (k p) n -> e p k n", p=P)

        def slot(s):
            return wslot[:, s, :].rearrange("p (k n) -> p k n", k=KS)

        def slot_hg(s):
            return wslot[:, s, :].rearrange("p (k j c) -> p k j c", k=KS, j=4)

        def slot_w2(s):
            return wslot[:, s, :].rearrange("p (k n) -> p k n", k=2)

        PRO = 3
        PRO_SLOTS = [2, 3, 0, 1, 2, 3]
        USES = [PRO_SLOTS.count(s) for s in range(RING)]
        N_HEAD0 = 2 * PRO
        N_BR0 = N_HEAD0 + 4 * HEADS
        N_WO0 = N_BR0 + 2 * NC
        N_ALL = N_WO0 + 2 * NC
        BR_USE = [u + HEADS for u in USES]
        WO_USE = [u + NC // 2 for u in BR_USE]
        MOE_USE = [u + NC // 2 for u in WO_USE] + [0, 0]

        block = ctx.enter_context(nc.Block())

        @block.sync
        def _(sp):
            sp.dma_start(resid[:, :, :], x[0].rearrange("(b p) d -> p b d", p=P)).then_inc(x_in, 16)
            sp.dma_start(norm_g[:, :], mix_norm_g[0:1, :].to_broadcast([P, D])).then_inc(g_in, 16)
            for n in range(2 * PRO):
                c, half = divmod(n, 2)
                if n >= RING:
                    sp.wait_ge(slot_used, n - RING + 1)
                sp.dma_start(slot(PRO_SLOTS[n]), w_in_k[:, half * KS:(half + 1) * KS, c * CH:(c + 1) * CH])\
                    .then_inc(loaded[PRO_SLOTS[n]], 16)
            with sp.Fori(0, HEADS) as i:
                for s in range(RING):
                    sp.wait_ge(slot_used, i * RING + (N_HEAD0 - RING + 1 + s))
                    half = s % 2
                    if s < 2:
                        for k in range(KS):
                            sp.dma_start(slot_hg(s)[:, k], w_gather[:, half * KS + k, :, bass.ts(i, HW)])\
                                .then_inc(loaded[s], 16)
                    else:
                        sp.dma_start(slot(s), w_in_k[:, half * KS:(half + 1) * KS, bass.ds(i * CH + C_GATE, CH)])\
                            .then_inc(loaded[s], 16)
            with sp.Fori(0, NC // 2) as j:
                for s in range(RING):
                    sp.wait_ge(slot_used, j * RING + (N_BR0 - RING + 1 + s))
                    w = (wa_k, wh_k)[s % 2]
                    sp.dma_start(slot(s), w[:, :, bass.ds(j * (2 * CH) + (s // 2) * CH, CH)]).then_inc(loaded[s], 16)
            with sp.Fori(0, NC // 2) as j:
                for s in range(RING):
                    sp.wait_ge(slot_used, j * RING + (N_WO0 - RING + 1 + s))
                    half = s % 2
                    sp.dma_start(slot(s), wo_k[:, half * KS:(half + 1) * KS, bass.ds(j * (2 * CH) + (s // 2) * CH, CH)])\
                        .then_inc(loaded[s], 16)
            sp.wait_ge(merged_ready, NC)
            sp.dma_start(norm_g[:, :], moe_norm_g[0:1, :].to_broadcast([P, D])).then_inc(g2_in, 16)
            sp.wait_ge(staged, 5 * HEADS)
            sp.dma_start(wr[:, :, 0:NG], w_router_group[0].rearrange("(p k) n -> p k n", p=P)).then_inc(r_in, 16)
            sp.dma_start(wr[:, :, NG:NR], w_router_expert[0].rearrange("(p k) n -> p k n", p=P)).then_inc(r_in, 16)
            sp.dma_start(br[:, 0:NG], b_router_group[0:1, :].to_broadcast([P, NG])).then_inc(r_in, 16)
            sp.dma_start(br[:, NG:NR], b_router_expert[0:1, :].to_broadcast([P, NE])).then_inc(r_in, 16)

            def load_expert(e, s):
                if s < 4:
                    src = (w1_k, w3_k)[s % 2][bass.ds(e, 1), :, (s // 2) * KS:(s // 2 + 1) * KS, :]
                    dst = slot(s)
                else:
                    src = w2_k[bass.ds(e, 1), :, 2 * (s % 2):2 * (s % 2) + 2, :]
                    dst = slot_w2(s)
                sp.dma_start(dst, src.rearrange("a p k n -> (a p) k n")).then_inc(loaded[s], 16)

            sp.wait_ge(ohT_done, HEADS + ONE)
            for s in (4, 5):
                load_expert(0, s)
            for s in range(4):
                sp.wait_ge(slot_used, N_ALL - 3 + s)
                load_expert(0, s)
            with sp.Fori(1, NE) as e:
                for s in range(6):
                    sp.wait_ge(quarter_used, e * 4 + ((1, 1, 2, 2, 3, 4)[s] - 4))
                    load_expert(e, s)
            sp.wait_ge(over_ready, 1)
            sp.wait_ge(quarter_used, 4 * NE)
            n_over = sp.value_load(over_i[0:1, LIST:LIST + 1], min_val=0, max_val=LIST)
            with sp.If(n_over > 0):
                with sp.Fori(0, n_over) as j:
                    e = sp.value_load(over_i[0:1, bass.ds(j, 1)], min_val=0, max_val=NE - 1)
                    for s in range(6):
                        if s == 0:
                            sp.wait_ge(oh13_ready, j * TB + ONE)
                        if s == 4:
                            sp.wait_ge(oy_ready, j * 2 * NC + ONE)
                        load_expert(e, s)
            sp.wait_ge(o_ready, TB)
            sp.dma_start(out[0].rearrange("(b p) d -> p b d", p=P), resid[:, :, :]).then_inc(stored, 16)
            sp.wait_ge(stored, 16)

        @block.gpsimd
        def _(pool):
            pool.wait_ge(pair1_act, 2)
            pool.wait_ge(pair0_act, 1)
            pool.wait_ge(c_in, 16 * 3)
            pool.wait_ge(lb_done, 1)
            with pool.Fori(0, HEADS) as i:
                pool.wait_ge(qkT_ready, i + ONE)
                settle(pool, c_in)
                nc.gpsimd.tensor_copy(qs, qa[:, :, bass.ts(i, P)]).then_inc(staged, 1)
                k_cols = kv[:, :, bass.ds((i // 2) * DH, DH)]
                nc.gpsimd.tensor_copy(ks[:, :, 0:DH], k_cols).then_inc(staged, 1)
                nc.gpsimd.tensor_copy(ks[:, :, DH:P], k_cols).then_inc(staged, 1)
                pool.wait_ge(oT_ready, i + ONE)
                settle(pool, c_in)
                nc.gpsimd.tensor_copy(vs, kv[:, :, bass.ds((i // 2) * DH + KV, DH)]).then_inc(staged, 1)
                pool.wait_ge(prob_ready, i * 4 + ONE)
                settle(pool, c_in)
                nc.gpsimd.tensor_copy(sk, bc(sinks[:, bass.ts(i, 2)].unsqueeze(1), [P, 2, 2])).then_inc(staged, 1)

        @block.scalar
        def _(act):
            for ahead in (ohT_done, cross_copied, mT_done, hidT_copied, ghT_copied, yg_act):
                act.sem_inc(ahead, ONE)
            chain = Chain(act, act_step)

            def mean_square(b, dst, src, n, col):
                return nc.scalar.activation(dst, src, ACT.Square, scale=n ** -0.5, accum_out=stat[:, col + b:col + b + 1])

            def rstd(col, done):
                v = stat[:, col:col + TB]
                chain.link(nc.scalar.activation(v, v, ACT.Ln, bias=cst[:, K_EPS:K_EPS + 1]))
                nc.scalar.activation(v, v, ACT.Exp, scale=-0.5).then_inc(done, 1)

            act.dma_start(cst[:, :], consts).then_inc(c_in, 16)
            act.dma_start(sinks[:, :], attn_sinks[0:1, :].to_broadcast([P, 2 * HEADS])).then_inc(c_in, 16)
            act.dma_start(hnorm[:, :], hgrn_norm_g[0:1, :].to_broadcast([P, HW])).then_inc(c_in, 16)
            for r in range(2):
                act.dma_start(lbrow[0:HEADS, r, :], hgrn_lb_logits[r].rearrange("(h c) -> h c", h=HEADS))\
                    .then_inc(lb_in, 16)
            act.wait_ge(x_in, 16)
            for b in range(TB):
                chain.link(mean_square(b, actT[:, b * KS:(b + 1) * KS, :].rearrange("p a b -> p (a b)"), resid[:, b, :], D, 0))
            act.wait_ge(c_in, 16 * 3)
            rstd(0, rstd_done)
            act.wait_ge(lb_rows, 2)
            nc.scalar.activation(lbrow[0:HEADS, :, :], lbrow[0:HEADS, :, :], ACT.Exp).then_inc(lb_e, 1)
            for g in range(4):
                act.wait_ge(tp_ready, g + 1)
                nc.scalar.activation(actT[:, 4 * g:4 * g + 4, :],
                                     levp[:, 4 * (g % 2):4 * (g % 2) + 4, :], ACT.Copy).then_inc(tp_copied, 1)
            act.wait_ge(lb_t, 1)
            nc.scalar.activation(lbT[:, :], flat4[:, 0:HEADS], ACT.Copy).then_inc(lb_done, 1)
            for c in range(PRO):
                act.wait_ge(slot_used, 2 * c + 2)
                dst = qa[:, :, c * CH:(c + 1) * CH] if c < 2 else kv[:, :, :]
                nc.scalar.activation(dst, pair[(c + 1) % 2][:, :, :], ACT.Copy, scale=DH ** -0.5 if c < 2 else 1.0)\
                    .then_inc(pair1_act if c != 1 else pair0_act, 1)
            with act.Fori(0, HEADS) as i:
                chain.enter(i, TB + 1)
                act.wait_ge(qkT_ready, i + 1 + ONE)
                act.wait_ge(score_ready, i + ONE)
                nc.scalar.activation(qkT, bank_t.rearrange("p (a t) -> p a t", a=2), ACT.Copy).then_inc(qkT_copied, 1)
                act.wait_ge(max_ready, i + 1)
                for h in range(2):
                    nc.scalar.activation(prob[:, h, 0:P], prob[:, h, 0:P], ACT.Exp, bias=mneg[:, 0, h:h + 1],
                                         accum_out=psums[:, 0, h:h + 1]).then_inc(exp_done, 1)
                    nc.scalar.activation(prob[:, h, P:3 * P], prob[:, h, P:3 * P], ACT.Exp, bias=mneg[:, 1, h:h + 1],
                                         accum_out=psums[:, 1, h:h + 1]).then_inc(exp_done, 1)
                nc.scalar.activation(esink, esink, ACT.Exp).then_inc(exp_done, 1)
                act.wait_ge(probT_ready, i + 1)
                act.wait_ge(oT_ready, i + ONE)
                nc.scalar.activation(probT[:, 0, :], bank_t[:, 0:3 * P], ACT.Copy).then_inc(probT_copied, 1)
                nc.scalar.activation(probT[:, 1, :], bank_o[:, 0:3 * P], ACT.Copy).then_inc(probT_copied, 1)
                act.wait_ge(oT_ready, i + 1 + ONE)
                settle(act, c_in)
                nc.scalar.activation(oaT[:, bass.ds(i, 1), :].rearrange("p a t -> p (a t)"), four[:, 0, 0:T], ACT.Copy)\
                    .then_inc(oaT_done, 1)
                act.wait_ge(slot_used, i * RING + (N_HEAD0 + 2))
                act.wait_ge(hg_rows, i + ONE)
                nc.scalar.activation(es[:, :, 0:2 * HW], pair[0][:, :, 0:2 * HW], ACT.Exp, scale=-1.0).then_inc(es_ready, 1)
                nc.scalar.activation(es[:, :, 2 * HW:3 * HW], pair[0][:, :, 3 * HW:4 * HW], ACT.Exp, scale=-1.0)\
                    .then_inc(es_ready, 1)
                act.wait_ge(ho_ready, i + ONE)
                nc.scalar.activation(irow, pair[0][:, :, 2 * HW:3 * HW], ACT.Copy).then_inc(pair0_act, 1)
                act.wait_ge(qfT_ready, i + 1)
                act.wait_ge(level_mm, i * 9 + ONE)
                nc.scalar.activation(qT, bank_t[:, 0:T], ACT.Copy).then_inc(qT_copied, 1)
                act.wait_ge(level_mm, i * 9 + 9 + ONE)
                nc.scalar.activation(crossT, four[:, 0, 0:P], ACT.Copy).then_inc(cross_copied, 1)
                act.wait_ge(ho_ready, i + 1 + ONE)
                for b in range(TB):
                    chain.link(mean_square(b, es[:, b, 0:HW], bank_o[:, b * HW:(b + 1) * HW], HW, 4))
                rstd(4, ho_sq)
                act.wait_ge(ohT_ready, i + 1)
                settle(act, c_in)
                nc.scalar.activation(ohT[:, bass.ds(i, 1), :].rearrange("p a t -> p (a t)"), bank_t[:, 0:T], ACT.Copy)\
                    .then_inc(ohT_done, 1)
                act.wait_ge(slot_used, i * RING + (N_HEAD0 + 4))
                settle(act, c_in)
                nc.scalar.activation(gates[:, :, bass.ts(i, CH)], pair[1][:, :, :], ACT.Exp, scale=-1.0)\
                    .then_inc(pair1_act, 1)
            chain.leave(HEADS)
            with act.Fori(0, NC) as c:
                act.wait_ge(mT_ready, c + 1 + ONE)
                settle(act, c_in)
                nc.scalar.activation(actT[:, bass.ds(c * 4, 4), :], levp[:, 0:4, :], ACT.Copy).then_inc(mT_done, 1)
            act.wait_ge(h_added, NC + ONE)
            act.wait_ge(merged_ready, NC)
            for b in range(TB):
                chain.link(mean_square(b, gates[:, b, D:2 * D], resid[:, b, :], D, 8))
            rstd(8, rstd_done)
            for g in range(4):
                act.wait_ge(tp_ready, 4 + g + 1)
                nc.scalar.activation(actT[:, 4 * g:4 * g + 4, :],
                                     levp[:, 4 * (g % 2):4 * (g % 2) + 4, :], ACT.Copy).then_inc(tp_copied, 1)
            act.wait_ge(xn_ready, 2 * TB)
            act.dma_start(norm_g[:, :], final_norm_g.rearrange("(a d) -> a d", a=1).to_broadcast([P, D])).then_inc(g3_in, 16)
            act.wait_ge(r_exp_in, 1)
            nc.scalar.activation(small[:, 0:10], small[:, 0:10], ACT.Exp).then_inc(r_exp, 1)
            with act.Fori(0, GROUPS) as g:
                for half in range(2):
                    act.wait_ge(gathered, g * 2 + (half + 1) + ONE)
                    nc.scalar.activation(xg[:, half * KS:(half + 1) * KS, :],
                                         four[:, 2 * half:2 * half + 2, :].rearrange("p a (k n) -> p (a k) n", n=P),
                                         ACT.Copy).then_inc(xg_copied, 1)
                act.wait_ge(swT_ready, g + 1 + ONE)
                nc.scalar.activation(swT, pair[1][:, 0, 0:T], ACT.Copy).then_inc(swT_copied, 1)
                for q in range(GX):
                    hp = pair[0][:, q % 2, :]
                    yp = pair[1][:, q % 2, :]
                    act.wait_ge(quarter_used, g * (4 * GX) + (4 * q + 2))
                    act.wait_ge(ghid_ready, g * GX + q + ONE)
                    nc.scalar.activation(geh, hp[:, 0:P], ACT.Exp, scale=-1.0).then_inc(ge_exp, 1)
                    act.wait_ge(ghT_ready, g * GX + (q + 1) + ONE)
                    nc.scalar.activation(ghT, hp[:, 2 * P:3 * P], ACT.Copy).then_inc(ghT_copied, 1)
                    act.wait_ge(quarter_used, g * (4 * GX) + (4 * q + 4))
                    for c in (0, 1):
                        nc.scalar.activation(yg[q * SL:(q + 1) * SL, c * CH:(c + 1) * CH], yp[c * SL:(c + 1) * SL, :],
                                             ACT.Copy).then_inc(yg_act, 1)
            act.wait_ge(over_ready, 1)
            act.wait_ge(scattered, GROUPS * 2 * NC + ONE)
            n_over = act.value_load(over_i[0:1, LIST:LIST + 1], min_val=0, max_val=LIST)
            with act.If(n_over > 0):
                with act.Fori(0, n_over) as e:
                    for b in range(TB):
                        act.wait_ge(oh13_ready, e * 2 + (b + 1) + ONE)
                        act.wait_ge(hid_ready, e * 2 + b + ONE)
                        nc.scalar.activation(ehid[:, b, :], pair[b][:, 0, :], ACT.Exp, scale=-1.0).then_inc(e_exp, 1)
                        act.wait_ge(hidT_ready, e * 2 + (b + 1) + ONE)
                        nc.scalar.activation(hidT[:, b], four[:, 3, :].rearrange("p (k t) -> p k t", k=4), ACT.Copy)\
                            .then_inc(hidT_copied, 1)
            act.wait_ge(resid_done, 1)
            for b in range(TB):
                chain.link(mean_square(b, gates[:, b, 0:D], resid[:, b, :], D, 12))
            rstd(12, rstd_done)

        @block.tensor
        def _(pe):
            for ahead in (oh13_ready, oy_ready, gathered, swT_ready, ghT_ready, qkT_ready, oT_ready, score_ready, ho_ready, level_mm, mT_ready, hidT_ready):
                pe.sem_inc(ahead, ONE)
            def transpose_rows(src, first, per_copy):
                for g in range(4):
                    if first + g >= 2:
                        pe.wait_ge(tp_copied, first + g - 1)
                    for k in range(4):
                        for b in range(TB):
                            kk = 4 * g + k
                            last = nc.tensor.transpose(levp[:, 4 * (g % 2) + k, b * P:(b + 1) * P],
                                                       src[:, b, kk * P:(kk + 1) * P], ident)
                    last.then_inc(tp_ready, 1)

            pe.wait_ge(xn_ready, TB)
            pe.wait_ge(c_in, 16 * 3)
            transpose_rows(gates, 0, 4)
            pe.wait_ge(lb_s, 1)
            pe.wait_ge(tp_copied, 4)
            nc.tensor.transpose(flat4[:, 0:HEADS], lbrow[0:HEADS, 0, :], ident[0:HEADS, 0:HEADS]).then_inc(lb_t, 1)

            for n in range(2 * PRO):
                c, half = divmod(n, 2)
                s = PRO_SLOTS[n]
                if c == 2 and half == 0:
                    pe.wait_ge(pair1_act, 1)
                pe.wait_ge(loaded[s], 16 * (PRO_SLOTS[:n + 1].count(s)))
                for k in range(KS):
                    kk = half * KS + k
                    for b in range(TB):
                        last = nc.tensor.matmul(pair[(c + 1) % 2][:, b, :], actT[:, kk, b * P:(b + 1) * P],
                                                slot(s)[:, k, :], start=(kk == 0), stop=(kk == KD - 1))
                last.then_inc(slot_used, 1)

            with pe.Fori(0, HEADS) as i:
                def a_transpose():
                    pe.wait_ge(staged, i * 5 + 5)
                    pe.wait_ge(ohT_done, i + ONE)
                    pe.wait_ge(lb_done, 1)
                    for a, src in enumerate((qs, ks)):
                        for b in range(TB):
                            last = nc.tensor.transpose(bank_t[:, a * T + b * P:a * T + (b + 1) * P], src[:, b, :], ident)
                    last.then_inc(qkT_ready, 1)

                def a_scores():
                    pe.wait_ge(qkT_copied, i + 1)
                    pe.wait_ge(lev_read, i * 2 + ONE)
                    pe.wait_ge(cross_copied, i + ONE)
                    for h in range(2):
                        r = slice(h * DH, (h + 1) * DH)
                        nc.tensor.matmul(four[:, h, 0:P], qkT[r, 0, 0:P], qkT[r, 1, 0:P], start=True, stop=True)
                        last = nc.tensor.matmul(four[:, h, P:3 * P], qkT[r, 0, P:T], qkT[r, 1, :], start=True, stop=True)
                    last.then_inc(score_ready, 1)

                def a_probT():
                    pe.wait_ge(prob_ready, i * 4 + 4 + ONE)
                    pe.wait_ge(oh_ready, i * 2 + ONE)
                    for h in range(2):
                        bank = (bank_t, bank_o)[h]
                        for k in range(3):
                            last = nc.tensor.transpose(bank[:, k * P:(k + 1) * P], prob[:, h, k * P:(k + 1) * P], ident)
                    last.then_inc(probT_ready, 1)

                def a_values():
                    pe.wait_ge(probT_copied, i * 2 + 2)
                    for h in range(2):
                        o = four[h * DH:(h + 1) * DH, 0, :]
                        nc.tensor.matmul(o[:, P:T], vs[:, 0, :], probT[:, h, P:2 * P], start=True, stop=False)
                        nc.tensor.matmul(o[:, P:T], vs[:, 1, :], probT[:, h, 2 * P:3 * P], start=False, stop=True)
                        last = nc.tensor.matmul(o[:, 0:P], vs[:, 0, :], probT[:, h, 0:P], start=True, stop=True)
                    last.then_inc(oT_ready, 1)

                def h_transpose():
                    pe.wait_ge(hg_rows, i + 1 + ONE)
                    for a, src in enumerate((qrow, frow)):
                        for b in range(TB):
                            last = nc.tensor.transpose(bank_t[:, a * T + b * P:a * T + (b + 1) * P], src[:, b, :], ident)
                    last.then_inc(qfT_ready, 1)

                def h_level(lv):
                    def go():
                        if lv == 0:
                            pe.wait_ge(qT_copied, i + 1)
                            pe.wait_ge(oaT_done, i + 1)
                        pe.wait_ge(level_ops, i * 8 + max(lv, 1))
                        if lv == LEVELS + 1:
                            pe.wait_ge(lev_read, i * 2 + 1 + ONE)
                            nc.tensor.matmul(four[:, 0, 0:P], kq[:, 0:P], qp[:, P:T], start=True, stop=True)\
                                .then_inc(level_mm, 1)
                            return
                        for b in range(TB):
                            rhs = (qT if lv == 0 else qp)[:, b * P:(b + 1) * P]
                            last = nc.tensor.matmul(levp[:, lv, b * P:(b + 1) * P], kq[:, b * P:(b + 1) * P], rhs,
                                                    start=True, stop=True)
                        last.then_inc(level_mm, 1)
                    return go

                def h_values():
                    pe.wait_ge(hatt_ready, i + 1)
                    pe.wait_ge(cross_copied, i + 1 + ONE)
                    pe.wait_ge(pair0_act, i + 2)
                    o = [bank_o[:, b * HW:(b + 1) * HW] for b in range(TB)]
                    nc.tensor.matmul(o[0], hatt[:, 0:P], irow[:, 0, :], start=True, stop=True)
                    nc.tensor.matmul(o[1], hatt[:, P:T], irow[:, 1, :], start=True, stop=False)
                    nc.tensor.matmul(o[1], crossT, irow[:, 0, :], start=False, stop=True).then_inc(ho_ready, 1)

                def h_outT():
                    pe.wait_ge(oh_ready, i * 2 + 2 + ONE)
                    for b in range(TB):
                        last = nc.tensor.transpose(bank_t[:, b * P:(b + 1) * P], oh[:, b, :], ident)
                    last.then_inc(ohT_ready, 1)

                tasks = {2: [a_transpose], 4: [a_scores], 10: [a_probT], 13: [a_values],
                         KD + 3: [h_transpose], KD + 6: [h_level(0), h_level(1)], KD + 7: [h_level(2)],
                         KD + 8: [h_level(3)], KD + 9: [h_level(4)], KD + 10: [h_level(5)],
                         KD + 11: [h_level(6)], KD + 12: [h_level(7)], KD + 13: [h_level(8)],
                         KD + 14: [h_values]}
                for s in range(RING):
                    if s == 0:
                        pe.wait_ge(pair0_act, i + 1)
                        pe.wait_ge(pair0_dve, i + ONE)
                    if s == 2:
                        pe.wait_ge(pair1_act, i + 2)
                    pe.wait_ge(loaded[s], (i + 1) * (16 * KS if s < 2 else 16) + 16 * USES[s])
                    for k in range(KS):
                        kk = (s % 2) * KS + k
                        for b in range(TB):
                            last = nc.tensor.matmul(pair[s // 2][:, b, :], actT[:, kk, b * P:(b + 1) * P],
                                                    slot(s)[:, k, :], start=(kk == 0), stop=(kk == KD - 1))
                        if k == KS - 1:
                            last.then_inc(slot_used, 1)
                        for task in tasks.get((s // 2) * KD + kk, ()):
                            task()
                h_outT()

            pe.wait_ge(oaT_done, HEADS)
            pe.wait_ge(ohT_done, HEADS + ONE)
            with pe.Fori(0, NC // 2) as j:
                for u in range(2):
                    for a, src in enumerate((oaT, ohT)):
                        s = 2 * u + a
                        if a == 0 and u == 0:
                            pe.wait_ge(pair0_act, HEADS + 1)
                            pe.wait_ge(pair0_dve, HEADS + ONE)
                            pe.wait_ge(pair1_act, HEADS + 2)
                        pe.wait_ge(y_read, j * 4 + (2 * u + a - 1 if 2 * u + a else 0) + ONE)
                        pe.wait_ge(loaded[s], j * 16 + 16 * (1 + BR_USE[s]) + (16 * (KS - 1) * HEADS if s < 2 else 0))
                        for k in range(KS):
                            for b in range(TB):
                                last = nc.tensor.matmul(pair[a][:, b, :], src[:, k, b * P:(b + 1) * P], slot(s)[:, k, :],
                                                        start=(k == 0), stop=(k == KS - 1))
                        last.then_inc(slot_used, 1)
                    pe.wait_ge(merged_ready, j * 2 + (u + 1))
                    pe.wait_ge(mT_done, j * 2 + u + ONE)
                    for k in range(4):
                        for b in range(TB):
                            last = nc.tensor.transpose(levp[:, k, b * P:(b + 1) * P], merged[:, b, k * P:(k + 1) * P], ident)
                    last.then_inc(mT_ready, 1)
            pe.wait_ge(mT_done, NC + ONE)
            with pe.Fori(0, NC // 2) as j:
                for s in range(RING):
                    if s % 2 == 0:
                        pe.wait_ge(h_added, j * 2 + (s // 2 - 1 if s else 0) + ONE)
                        if s == 0:
                            pe.wait_ge(y_read, 2 * NC + ONE)
                    pe.wait_ge(loaded[s], j * 16 + 16 * (1 + WO_USE[s]) + (16 * (KS - 1) * HEADS if s < 2 else 0))
                    for k in range(KS):
                        kk = (s % 2) * KS + k
                        for b in range(TB):
                            last = nc.tensor.matmul(pair[s // 2][:, b, :], actT[:, kk, b * P:(b + 1) * P],
                                                    slot(s)[:, k, :], start=(kk == 0), stop=(kk == KD - 1))
                    last.then_inc(slot_used, 1)
            pe.wait_ge(xn_ready, 2 * TB)
            transpose_rows(gates, 4, 4)
            pe.wait_ge(tp_copied, 8)
            pe.wait_ge(r_in, 16 * 4)
            pe.wait_ge(h_added, NC + ONE)
            for b in range(TB):
                for k in range(KD):
                    last = nc.tensor.matmul(pair[0][:, b, 0:NR], actT[:, k, b * P:(b + 1) * P], wr[:, k, :],
                                            start=(k == 0), stop=(k == KD - 1))
            last.then_inc(logit_ready, 1)
            pe.wait_ge(logit_read, 1)
            pe.wait_ge(mask_ready, 1)
            tri, ones = cst[:, K_TRI:K_TRI + P], cst[:, K_ONE:K_ONE + P]
            rank = pair[1][:, 0, 0:3 * NE].rearrange("p (b e) -> p b e", b=3)
            nc.tensor.matmul(rank[:, 0, :], tri, rmask[:, 0, :], start=True, stop=True)
            nc.tensor.matmul(rank[:, 1, :], tri, rmask[:, 1, :], start=True, stop=False)
            nc.tensor.matmul(rank[:, 1, :], ones, rmask[:, 0, :], start=False, stop=True)
            nc.tensor.matmul(rank[:, 2, :], ones, rmask[:, 0, :], start=True, stop=False)
            nc.tensor.matmul(rank[:, 2, :], ones, rmask[:, 1, :], start=False, stop=True).then_inc(rank_ready, 1)
            pe.wait_ge(rank_read, 1)
            with pe.Fori(0, GROUPS) as g:
                pe.wait_ge(onehot_ready, g * 2 + 2)
                pe.wait_ge(scattered, g * (2 * NC) + ONE)
                for k in range(KD):
                    for b in range(TB):
                        last = nc.tensor.matmul(flat4[:, k * P:(k + 1) * P], hn[:, b, k * P:(k + 1) * P],
                                                gh[:, b, :], start=(b == 0), stop=(b == TB - 1))
                    if k % KS == KS - 1:
                        last.then_inc(gathered, 1)
                pe.wait_ge(sw_ready, g * 2 + 2)
                pe.wait_ge(yg_act, g * (2 * GX) + ONE)
                pe.wait_ge(yg_dve, g * (2 * GX) + ONE)
                for b in range(TB):
                    last = nc.tensor.transpose(pair[1][:, 0, b * P:(b + 1) * P], sw[:, b, :], ident)
                last.then_inc(swT_ready, 1)
                for q in range(GX):
                    hp = pair[0][:, q % 2, :]
                    yp = pair[1][:, q % 2, :]
                    pe.wait_ge(xg_copied, g * 2 + 2)
                    pe.wait_ge(ghT_copied, g * GX + q + ONE)
                    for half in range(2):
                        for m in range(2):
                            s = 2 * half + m
                            pe.wait_ge(loaded[s], g * (16 * GX) + (16 * (1 + q + MOE_USE[s]) + (16 * (KS - 1) * HEADS if s < 2 else 0)))
                        for k in range(KS):
                            kk = half * KS + k
                            for c in range(4):
                                last = nc.tensor.matmul(
                                    hp[c * SL:(c + 1) * SL, 0:2 * P], xg[:, kk, q * SL:(q + 1) * SL],
                                    wslot[:, 2 * half:2 * half + 2, k * CH + c * P:k * CH + (c + 1) * P],
                                    start=(kk == 0), stop=(kk == KD - 1))
                        last.then_inc(quarter_used, 1)
                    pe.wait_ge(ghid_ready, g * GX + (q + 1) + ONE)
                    nc.tensor.transpose(hp[:, 2 * P:3 * P], ghid, ident).then_inc(ghT_ready, 1)
                    pe.wait_ge(ghT_copied, g * GX + (q + 1) + ONE)
                    pe.wait_ge(swT_copied, g + 1)
                    pe.wait_ge(yg_act, g * (2 * GX) + 2 * q + ONE)
                    pe.wait_ge(yg_dve, g * (2 * GX) + 2 * q + ONE)
                    for k in range(4):
                        if k % 2 == 0:
                            pe.wait_ge(loaded[4 + k // 2], g * (16 * GX) + 16 * (q + 1))
                        for c in range(4):
                            last = nc.tensor.matmul(yp[c * SL:(c + 1) * SL, :], ghT[:, k * SL:(k + 1) * SL],
                                                    slot_w2(4 + k // 2)[:, k % 2, c * CH:(c + 1) * CH],
                                                    start=(k == 0), stop=(k == 3))
                        if k % 2 == 1:
                            last.then_inc(quarter_used, 1)
                pe.wait_ge(yg_act, g * (2 * GX) + 2 * GX + ONE)
                pe.wait_ge(yg_dve, g * (2 * GX) + 2 * GX + ONE)
                for b in range(TB):
                    for c in range(NC):
                        if b == 1:
                            pe.wait_ge(scattered, g * (2 * NC) + (c + 1) + ONE)
                        nc.tensor.matmul(four[:, c, :], swT[:, b * P:(b + 1) * P], yg[:, c * CH:(c + 1) * CH],
                                         start=True, stop=True).then_inc(back_ready, 1)
            pe.wait_ge(over_ready, 1)
            pe.wait_ge(scattered, GROUPS * 2 * NC + ONE)
            n_over = pe.value_load(over_i[0:1, LIST:LIST + 1], min_val=0, max_val=LIST)
            with pe.If(n_over > 0):
                with pe.Fori(0, n_over) as e:
                    for b in range(TB):
                        pe.wait_ge(hid_ready, e * 2 + b + ONE)
                        for half in range(2):
                            for m in range(2):
                                s = 2 * half + m
                                if b == 0:
                                    pe.wait_ge(loaded[s], e * 16 + 16 * (1 + NE + MOE_USE[s]) + (16 * (KS - 1) * HEADS if s < 2 else 0))
                                for k in range(KS):
                                    kk = half * KS + k
                                    last = nc.tensor.matmul(pair[b][:, m, :], actT[:, kk, b * P:(b + 1) * P], slot(s)[:, k, :],
                                                            start=(kk == 0), stop=(kk == KD - 1))
                        last.then_inc(oh13_ready, 1)
                    for b in range(TB):
                        pe.wait_ge(hid_ready, e * 2 + (b + 1) + ONE)
                        pe.wait_ge(y_added, e * 8 + b * 4 + ONE)
                        pe.wait_ge(hidT_copied, e * 2 + b + ONE)
                        for k in range(4):
                            last = nc.tensor.transpose(four[:, 3, k * P:(k + 1) * P], hid[:, b, k * P:(k + 1) * P], ident)
                        last.then_inc(hidT_ready, 1)
                        pe.wait_ge(hidT_copied, e * 2 + (b + 1) + ONE)
                        for half in range(2):
                            if b == 0:
                                pe.wait_ge(loaded[4 + half], e * 16 + 16 * (1 + NE))
                        for c in range(NC):
                            for k in range(4):
                                last = nc.tensor.matmul(four[:, c, :], hidT[:, b, k, :],
                                                        slot_w2(4 + k // 2)[:, k % 2, c * CH:(c + 1) * CH],
                                                        start=(k == 0), stop=(k == 3))
                            last.then_inc(oy_ready, 1)

        @block.vector
        def _(dve):
            for ahead in (prob_ready, hg_rows, hid_ready, lev_read, oh_ready, pair0_dve, y_read, h_added, y_added, scattered, ghid_ready, yg_dve):
                dve.sem_inc(ahead, ONE)
            chain = Chain(dve, dve_step)
            link = chain.link

            dve.wait_ge(rstd_done, 1)
            dve.wait_ge(g_in, 16)
            for b in range(TB):
                nc.vector.scalar_tensor_tensor(gates[:, b, 0:D], resid[:, b, :], stat[:, b:b + 1], norm_g[:, :],
                                               ALU.mult, ALU.mult).then_inc(xn_ready, 1)
            dve.wait_ge(lb_in, 32)
            r0, r1 = lbrow[0:HEADS, 0, :], lbrow[0:HEADS, 1, :]
            top = es[0:HEADS, 0, 0:P]
            link(nc.vector.tensor_tensor(top, r0, r1, ALU.max))
            nc.vector.tensor_tensor(r0, r0, top, ALU.subtract).then_inc(lb_rows, 1)
            nc.vector.tensor_tensor(r1, r1, top, ALU.subtract).then_inc(lb_rows, 1)
            dve.wait_ge(lb_e, 1)
            link(nc.vector.tensor_tensor(r1, r0, r1, ALU.add))
            link(nc.vector.reciprocal(r1, r1))
            nc.vector.tensor_tensor(r0, r0, r1, ALU.mult).then_inc(lb_s, 1)
            dve.wait_ge(lb_done, 1)
            dve.wait_ge(c_in, 16 * 3)

            att_mask = cst[:, K_ATT:K_ATT + 3 * P]
            lev_mask = cst[:, K_LEV:K_LEV + 8 * P].rearrange("p (l t) -> p l t", l=8)
            with dve.Fori(0, HEADS) as i:
                chain.enter(i, 31)
                dve.wait_ge(staged, i * 5 + 5)
                dve.wait_ge(score_ready, i + 1 + ONE)
                for h in range(2):
                    link(nc.vector.tensor_tensor(prob[:, h, :], four[:, h, 0:3 * P], att_mask, ALU.add))
                link(nc.vector.tensor_reduce(mx[:, 0, :], prob[:, :, 0:P], AX.X, ALU.max))
                link(nc.vector.tensor_reduce(mx[:, 1, :], prob[:, :, P:3 * P], AX.X, ALU.max))
                link(nc.vector.tensor_tensor(mx, mx, sk, ALU.max))
                link(nc.vector.tensor_tensor(esink, sk, mx, ALU.subtract))
                nc.vector.tensor_scalar(mneg, mx, -1.0, None, ALU.mult).then_inc(max_ready, 1)
                dve.wait_ge(exp_done, i * 5 + 5)
                link(nc.vector.tensor_tensor(rden, psums, esink, ALU.add))
                link(nc.vector.reciprocal(rden, rden))
                for h in range(2):
                    nc.vector.tensor_scalar(prob[:, h, 0:P], prob[:, h, 0:P], rden[:, 0, h:h + 1], None, ALU.mult)\
                        .then_inc(prob_ready, 1)
                    nc.vector.tensor_scalar(prob[:, h, P:3 * P], prob[:, h, P:3 * P], rden[:, 1, h:h + 1], None, ALU.mult)\
                        .then_inc(prob_ready, 1)
                dve.wait_ge(es_ready, i * 2 + 2)
                dve.wait_ge(pair0_act, i + 2)
                link(nc.vector.tensor_scalar(es, es, 1.0, None, ALU.add))
                link(nc.vector.reciprocal(es, es))
                link(nc.vector.scalar_tensor_tensor(qrow, es[:, :, 0:HW], HW ** -0.5, pair[0][:, :, 0:HW], ALU.mult, ALU.mult))
                link(nc.vector.tensor_tensor(orow, es[:, :, 2 * HW:3 * HW], pair[0][:, :, 3 * HW:4 * HW], ALU.mult))
                nc.vector.tensor_tensor(orow, orow, bc(hnorm[:, :].unsqueeze(1), [P, TB, HW]), ALU.mult).then_inc(pair0_dve, 1)
                nc.vector.tensor_copy(frow, es[:, :, HW:2 * HW]).then_inc(hg_rows, 1)
                settle(dve, c_in)
                link(nc.vector.tensor_copy(lbs[:, 0:1], lbT[:, bass.ds(i, 1)]))
                link(nc.vector.tensor_scalar(lbs[:, 1:2], lbs[:, 0:1], -1.0, 1.0, ALU.mult, ALU.add))
                dve.wait_ge(qT_copied, i + 1)
                link(nc.vector.tensor_scalar(fT, bank_t[:, T:2 * T], lbs[:, 1:2], lbs[:, 0:1], ALU.mult, ALU.add))
                link(nc.vector.tensor_tensor(qp, fT, bank_t[:, 0:T], ALU.mult))
                nc.vector.tensor_scalar(kq, fT, -1.0, 1.0, ALU.mult, ALU.add).then_inc(level_ops, 1)
                totals = fT
                off = 0
                for lv in range(1, LEVELS + 1):
                    size = 1 << (lv - 1)
                    blocks = T // size
                    pairs = totals.rearrange("p (n a) -> p n a", a=2)
                    q_odd = qp.rearrange("p (n a s) -> p n a s", a=2, s=size)[:, :, 1, :]
                    k_even = kq.rearrange("p (n a s) -> p n a s", a=2, s=size)[:, :, 0, :]
                    dve.wait_ge(level_mm, i * 9 + (lv + 1) + ONE)
                    if lv == 1:
                        dve.wait_ge(level_ops, i * 8 + 1)
                    link(nc.vector.tensor_tensor(q_odd, q_odd, bc(pairs[:, :, 0:1], [P, blocks // 2, size]), ALU.mult))
                    if lv < LEVELS:
                        nxt = tot[:, off:off + blocks // 2]
                        link(nc.vector.tensor_tensor(nxt, pairs[:, :, 0], pairs[:, :, 1], ALU.mult))
                        off += blocks // 2
                    nc.vector.tensor_tensor(k_even, k_even, bc(pairs[:, :, 1:2], [P, blocks // 2, size]), ALU.mult)\
                        .then_inc(level_ops, 1)
                    totals = nxt
                    dve.wait_ge(level_ops, i * 8 + (lv + 1))
                for half in range(2):
                    dst = lev[:, 4 * half:4 * half + 4, :].rearrange("p l (b t) -> p l b t", b=TB)
                    src = levp[:, 4 * half:4 * half + 4, :].rearrange("p l (b t) -> p l b t", b=TB)
                    for b in range(TB):
                        ins = nc.vector.tensor_tensor(dst[:, :, b, :], src[:, :, b, :],
                                                      lev_mask[:, 4 * half:4 * half + 4, :], ALU.mult)
                        if b == TB - 1:
                            ins.then_inc(lev_read, 1)
                        else:
                            link(ins)
                dve.wait_ge(lev_read, i * 2 + 2 + ONE)
                nc.vector.tensor_reduce(hatt, lev.rearrange("p l t -> p t l"), AX.X, ALU.add).then_inc(hatt_ready, 1)
                dve.wait_ge(ho_sq, i + 1)
                for b in range(TB):
                    nc.vector.scalar_tensor_tensor(oh[:, b, :], bank_o[:, b * HW:(b + 1) * HW], stat[:, 4 + b:5 + b],
                                                   orow[:, b, :], ALU.mult, ALU.mult).then_inc(oh_ready, 1)
            chain.leave(HEADS)
            dve.wait_ge(pair1_act, HEADS + 2)
            with dve.Fori(0, NC) as c:
                chain.enter(c, 4)
                dve.wait_ge(mT_ready, c + ONE)
                for m, first in ((merged, 0), (merged2, D)):
                    link(nc.vector.tensor_scalar(m, gates[:, :, bass.ds(c * CH + first, CH)], 1.0, None, ALU.add))
                    link(nc.vector.reciprocal(m, m))
                for a, m in enumerate((merged, merged2)):
                    dve.wait_ge(slot_used, c * 2 + (N_BR0 + 1 + a))
                    nc.vector.tensor_tensor(m, pair[a][:, :, :], m, ALU.mult).then_inc(y_read, 1)
                dve.wait_ge(y_read, c * 2 + 2 + ONE)
                nc.vector.tensor_tensor(merged, merged, merged2, ALU.add).then_inc(merged_ready, 1)
            chain.leave(NC)
            with dve.Fori(0, NC // 2) as j:
                for u in range(2):
                    dve.wait_ge(slot_used, j * RING + (N_WO0 + 2 * u + 2))
                    h_c = resid[:, :, bass.ds(j * (2 * CH) + u * CH, CH)]
                    nc.vector.tensor_tensor(h_c, h_c, pair[u][:, :, :], ALU.add).then_inc(h_added, 1)
            dve.wait_ge(rstd_done, 2)
            dve.wait_ge(g2_in, 16)
            for b in range(TB):
                nc.vector.scalar_tensor_tensor(
                    gates[:, b, 0:D].rearrange("p (k c) -> p k c", k=KD),
                    resid[:, b, :].rearrange("p (c k) -> p k c", k=KD), stat[:, 8 + b:9 + b],
                    norm_g[:, :].rearrange("p (c k) -> p k c", k=KD), ALU.mult, ALU.mult).then_inc(xn_ready, 1)

            off = [NR]

            def rw(*shape):
                n = 1
                for s in shape:
                    n *= s
                ap = rwork[:, off[0]:off[0] + n]
                off[0] += n
                return ap.rearrange("p (a b) -> p a b", a=shape[0]) if len(shape) == 2 else ap
            lg = rw(TB, NR)
            oneg = rw(TB, NG)
            me = rw(TB, NE)
            oh1 = rw(TB, NE)
            oh2 = rw(TB, NE)
            t32 = rw(TB, NE)
            t4 = rw(TB, NG)
            m_g, i_g, m_1, i_1, m_2, i_2, psel, w_1, w_2, s1 = (rw(TB, 1) for _ in range(10))
            iota = cst[:, K_IOTA:K_IOTA + NE]
            dve.wait_ge(logit_ready, 1)
            nc.vector.tensor_tensor(lg, pair[0][:, :, 0:NR], bc(br.unsqueeze(1), [P, TB, NR]), ALU.add).then_inc(logit_read, 1)
            dve.wait_ge(logit_read, 1)

            def first_max(v, m, idx, onehot, tmp, n):
                it = bc(iota[:, 0:n].unsqueeze(1), [P, TB, n])
                link(nc.vector.tensor_reduce(m, v, AX.X, ALU.max))
                link(nc.vector.tensor_tensor(tmp, v, bc(m, [P, TB, n]), ALU.is_lt))
                link(nc.vector.scalar_tensor_tensor(tmp, tmp, 1000.0, it, ALU.mult, ALU.add))
                link(nc.vector.tensor_reduce(idx, tmp, AX.X, ALU.min))
                link(nc.vector.tensor_tensor(onehot, it, bc(idx, [P, TB, n]), ALU.is_equal))

            lgg = lg[:, :, 0:NG]
            first_max(lgg, m_g, i_g, oneg, t4, NG)
            ex = small[:, 0:TB * NG].rearrange("p (b g) -> p b g", b=TB)
            link(nc.vector.tensor_tensor(ex, lgg, bc(m_g, [P, TB, NG]), ALU.subtract))
            for b in range(TB):
                gm = bc(oneg[:, b, :].unsqueeze(2), [P, NG, EG])
                me_b = me[:, b, :].rearrange("p (g e) -> p g e", g=NG)
                link(nc.vector.tensor_tensor(me_b, lg[:, b, NG:NR].rearrange("p (g e) -> p g e", g=NG), gm, ALU.mult))
                link(nc.vector.tensor_scalar(t32[:, b, :].rearrange("p (g e) -> p g e", g=NG), gm, 1.0, -NEG,
                                             ALU.subtract, ALU.mult))
            link(nc.vector.tensor_tensor(me, me, t32, ALU.add))
            first_max(me, m_1, i_1, oh1, t32, NE)
            link(nc.vector.scalar_tensor_tensor(me, oh1, 4 * NEG, me, ALU.mult, ALU.add))
            first_max(me, m_2, i_2, oh2, t32, NE)
            d12 = small[:, 8:10].rearrange("p (b o) -> p b o", b=TB)
            nc.vector.tensor_tensor(d12, m_2, m_1, ALU.subtract).then_inc(r_exp_in, 1)
            dve.wait_ge(r_exp, 1)
            link(nc.vector.tensor_reduce(psel, ex, AX.X, ALU.add))
            link(nc.vector.tensor_scalar(s1, d12, 1.0, None, ALU.add))
            link(nc.vector.tensor_tensor(s1, s1, psel, ALU.mult))
            link(nc.vector.reciprocal(w_1, s1))
            link(nc.vector.tensor_tensor(w_2, w_1, d12, ALU.mult))
            nc.vector.tensor_tensor(rmask, oh1, oh2, ALU.add).then_inc(mask_ready, 1)
            link(nc.vector.tensor_tensor(oh1, oh1, bc(w_1, [P, TB, NE]), ALU.mult))
            link(nc.vector.tensor_tensor(oh2, oh2, bc(w_2, [P, TB, NE]), ALU.mult))
            link(nc.vector.tensor_tensor(coef, oh1, oh2, ALU.add))
            dve.wait_ge(rank_ready, 1)
            dve.wait_ge(mask_ready, 1)
            rank = pair[1][:, 0, 0:3 * NE].rearrange("p (b e) -> p b e", b=3)
            link(nc.vector.tensor_scalar(late, rank[:, 0:TB, :], CAP - 0.5, BIG, ALU.is_gt, ALU.mult))
            link(nc.vector.tensor_scalar(place, rmask, -BIG, BIG, ALU.mult, ALU.add))
            link(nc.vector.tensor_tensor(place, place, late, ALU.add))
            link(nc.vector.tensor_tensor(place, place, rank[:, 0:TB, :], ALU.add))
            link(nc.vector.scalar_tensor_tensor(ocoef, late, 1.0 / BIG, coef, ALU.mult, ALU.mult))
            over, upto, idx = lrow[0:1, 0:NE], lrow[0:1, NE:2 * NE], lrow[0:1, 2 * NE:2 * NE + LIST + 1]
            link(nc.vector.tensor_scalar(over, rank[0:1, 2, :], CAP + 0.5, None, ALU.is_gt))
            link(nc.vector.tensor_tensor_scan(upto, cst[0:1, K_ONE:K_ONE + NE], over, 0.0, ALU.mult, ALU.add))
            link(nc.vector.tensor_tensor(llist, bc(cst[0:1, K_IOTA + 1:K_IOTA + 1 + LIST].unsqueeze(2), [1, LIST, NE]),
                                         bc(upto.unsqueeze(1), [1, LIST, NE]), ALU.is_equal))
            link(nc.vector.tensor_tensor(over, over, iota[0:1, :], ALU.mult))
            link(nc.vector.tensor_tensor(llist, llist, bc(over.unsqueeze(1), [1, LIST, NE]), ALU.mult))
            link(nc.vector.tensor_reduce(idx[:, 0:LIST], llist, AX.X, ALU.add))
            link(nc.vector.tensor_copy(idx[:, LIST:LIST + 1], upto[:, NE - 1:NE]))
            nc.vector.tensor_copy(over_i[0:1, :], idx).then_inc(over_ready, 1)
            nc.vector.tensor_copy(lrow[0:1, 0:1], rank[0:1, 2, 0:1]).then_inc(rank_read, 1)
            it4 = bc(iota.unsqueeze(1), [P, GX, SL])
            with dve.Fori(0, GROUPS) as g:
                chain.enter(g, 3 * GX)
                dve.wait_ge(gathered, g * 2 + ONE)
                dve.wait_ge(swT_ready, g + ONE)
                dve.wait_ge(rank_read, 1)
                for b in range(TB):
                    pl = place[:, b, bass.ts(g, GX)]
                    nc.vector.tensor_tensor(gh[:, b, :].rearrange("p (q s) -> p q s", q=GX), it4,
                                            bc(pl.unsqueeze(2), [P, GX, SL]), ALU.is_equal).then_inc(onehot_ready, 1)
                dve.wait_ge(onehot_ready, g * 2 + 2)
                for b in range(TB):
                    cf = coef[:, b, bass.ts(g, GX)]
                    nc.vector.tensor_tensor(sw[:, b, :].rearrange("p (q s) -> p q s", q=GX),
                                            gh[:, b, :].rearrange("p (q s) -> p q s", q=GX),
                                            bc(cf.unsqueeze(2), [P, GX, SL]), ALU.mult).then_inc(sw_ready, 1)
                for q in range(GX):
                    hp = pair[0][:, q % 2, :]
                    yp = pair[1][:, q % 2, :]
                    dve.wait_ge(ge_exp, g * GX + (q + 1))
                    link(nc.vector.tensor_scalar(geh, geh, 1.0, None, ALU.add))
                    link(nc.vector.reciprocal(geh, geh))
                    dve.wait_ge(ghT_ready, g * GX + q + ONE)
                    link(nc.vector.tensor_tensor(ghid, geh, hp[:, 0:P], ALU.mult))
                    nc.vector.tensor_tensor(ghid, ghid, hp[:, P:2 * P], ALU.mult).then_inc(ghid_ready, 1)
                    dve.wait_ge(quarter_used, g * (4 * GX) + (4 * q + 4))
                    for c in (2, 3):
                        nc.vector.tensor_copy(yg[q * SL:(q + 1) * SL, c * CH:(c + 1) * CH], yp[c * SL:(c + 1) * SL, :])\
                            .then_inc(yg_dve, 1)
                for b in range(TB):
                    for c in range(NC):
                        dve.wait_ge(back_ready, g * (2 * NC) + (b * NC + c + 1))
                        h_c = resid[:, b, c * CH:(c + 1) * CH]
                        nc.vector.tensor_tensor(h_c, h_c, four[:, c, :], ALU.add).then_inc(scattered, 1)
            chain.leave(GROUPS)
            dve.wait_ge(scattered, GROUPS * 2 * NC + ONE)
            dve.wait_ge(over_ready, 1)
            n_over = dve.value_load(over_i[0:1, LIST:LIST + 1], min_val=0, max_val=LIST)
            with dve.If(n_over > 0):
                with dve.Fori(0, n_over) as e:
                    ex_e = dve.value_load(over_i[0:1, bass.ds(e, 1)], min_val=0, max_val=NE - 1)
                    chain_o = Chain(dve, over_step)
                    chain_o.enter(e, 2 * 3 + 1)
                    dve.wait_ge(y_added, e * 2 * NC + ONE)
                    chain_o.link(nc.vector.tensor_scalar(small[:, 16:18].rearrange("p (b o) -> p b o", b=TB),
                                                         ocoef[:, :, bass.ds(ex_e, 1)], 1.0, None, ALU.mult))
                    for b in range(TB):
                        dve.wait_ge(e_exp, e * 2 + (b + 1))
                        dve.wait_ge(hidT_ready, e * 2 + b + ONE)
                        chain_o.link(nc.vector.tensor_scalar(ehid[:, b, :], ehid[:, b, :], 1.0, None, ALU.add))
                        chain_o.link(nc.vector.reciprocal(ehid[:, b, :], ehid[:, b, :]))
                        chain_o.link(nc.vector.tensor_tensor(hid[:, b, :], ehid[:, b, :], pair[b][:, 0, :], ALU.mult))
                        nc.vector.tensor_tensor(hid[:, b, :], hid[:, b, :], pair[b][:, 1, :], ALU.mult).then_inc(hid_ready, 1)
                    for b in range(TB):
                        for c in range(NC):
                            dve.wait_ge(oy_ready, e * 8 + (b * 4 + c + 1) + ONE)
                            h_c = resid[:, b, c * CH:(c + 1) * CH]
                            nc.vector.scalar_tensor_tensor(h_c, four[:, c, :], small[:, 16 + b:17 + b], h_c,
                                                           ALU.mult, ALU.add).then_inc(y_added, 1)
            nc.vector.tensor_copy(small[:, 20:21], small[:, 0:1]).then_inc(resid_done, 1)
            dve.wait_ge(rstd_done, 3)
            dve.wait_ge(g3_in, 16)
            for b in range(TB):
                nc.vector.scalar_tensor_tensor(resid[:, b, :], resid[:, b, :], stat[:, 12 + b:13 + b], norm_g[:, :],
                                               ALU.mult, ALU.mult).then_inc(o_ready, 1)


_INS = ["x", "w_in", "attn_sinks", "hgrn_lb_logits", "hgrn_norm_g", "w_br_attn", "w_br_hgrn", "w_out",
        "mix_norm_g", "moe_norm_g", "w_router_group", "b_router_group", "w_router_expert",
        "b_router_expert", "w1", "w3", "w2", "final_norm_g"]


def kernel(**inputs):
    import numpy as np
    import concourse.bacc as bacc
    from concourse.bass_utils import run_bass_kernel_spmd as run

    nc = bacc.Bacc("TRN2", target_bir_lowering=False, num_devices=1)
    arrays, args = {}, []
    for name in _INS + ["consts"]:
        a = constants() if name == "consts" else np.ascontiguousarray(inputs[name])
        arrays[f"in_{name}"] = a
        args.append(nc.dram_tensor(f"in_{name}", a.shape, mybir.dt.from_np(a.dtype), kind="ExternalInput").ap())
    res = nc.dram_tensor("result", (1, T, D), F32, kind="ExternalOutput").ap()
    hybrid_block(nc, *args, res)
    r = run(nc, [arrays], core_ids=[0])
    return r.results[0]["result"]
```

```python
from contextlib import ExitStack

import concourse.bass as bass
from concourse import mybir

F32 = mybir.dt.float32
F32R = mybir.dt.float32r
I32 = mybir.dt.int32
ALU = mybir.AluOpType
ACT = mybir.ActivationFunctionType
AX = mybir.AxisListType

P = 128
D = 2048
T = 256
TB = T // P
KD = D // P
CH = 512
KS = 8
KU = 4
UNITS = 4
NC = D // CH
HEADS = 8
DH = 64
HW = 128
LEVELS = 7
W_ATT = 1024
KV = 256
C_HGRN = W_ATT + 2 * KV
C_GATE = C_HGRN + 4 * W_ATT
EPS = 1e-6
ONE = 1
Q_SCALE = 0.5 * HW ** -0.5
NEG = -1e30
NG = 4
EG = 8
NE = NG * EG
NR = NG + NE
FE = 512
SL = 32
CAP = SL
GX = P // SL
GROUPS = NE // GX
LIST = 16
BIG = 1000.0

K_LEV = 0
K_ATT = K_LEV + (LEVELS + 1) * P
K_ID = K_ATT + 3 * P
K_TRI = K_ID + P
K_IOTA = K_TRI + P
K_ONE = K_IOTA + 2 * P
K_EPS = K_ONE + P
K_END = K_EPS + 8


def constants():
    import numpy as np
    s = np.arange(P)[:, None]
    t = np.arange(P)[None, :]
    out = np.zeros((P, K_END), np.float32)
    for lev in range(LEVELS + 1):
        if lev == 0:
            m = s == t
        else:
            half = 1 << (lev - 1)
            m = (s >> lev == t >> lev) & (s & half == 0) & (t & half != 0)
        out[:, K_LEV + lev * P:K_LEV + (lev + 1) * P] = m
    causal = np.where(t <= s, 0.0, NEG)
    out[:, K_ATT:K_ATT + P] = causal
    out[:, K_ATT + P:K_ATT + 2 * P] = np.where(t > s, 0.0, NEG)
    out[:, K_ATT + 2 * P:K_ATT + 3 * P] = causal
    out[:, K_ID:K_ID + P] = s == t
    out[:, K_TRI:K_TRI + P] = s < t
    out[:, K_IOTA:K_IOTA + 2 * P] = np.arange(2 * P)[None, :]
    out[:, K_ONE:K_ONE + P] = 1.0
    out[:, K_EPS] = EPS
    return out


class Chain:

    def __init__(self, eng, sem):
        self.eng, self.sem, self.base, self.n = eng, sem, 0, 0

    def link(self, ins):
        self.n += 1
        ins.then_inc(self.sem, 1)
        self.eng.wait_ge(self.sem, self.base + self.n)

    def enter(self, i, per):
        self.start = self.base + self.n
        self.base, self.n, self.per = self.start + i * per, 0, per

    def leave(self, times):
        assert self.n == self.per, (self.n, self.per)
        self.base, self.n = self.start + times * self.per, 0


def settle(eng, sem):
    eng.wait_ge(sem, 16 * 3)


def bc(ap, shape):
    return ap.broadcast_to(shape)


def hybrid_block(nc, x, w_in, attn_sinks, hgrn_lb_logits, hgrn_norm_g, w_br_attn, w_br_hgrn, w_out,
                 mix_norm_g, moe_norm_g, w_router_group, b_router_group, w_router_expert,
                 b_router_expert, w1, w3, w2, final_norm_g, consts, out):
    ctx = ExitStack()
    with ctx:
        def sb(name, shape, dt=F32):
            return ctx.enter_context(nc.sbuf_tensor(name, shape, dt))

        def ps(name, shape):
            return ctx.enter_context(nc.psum_tensor(name, shape, F32))

        def sem(name):
            return ctx.enter_context(nc.semaphore(name))

        def another_name(name, shape, offset):
            return nc.alloc_sbuf_tensor_at(name, shape, F32R, offset=offset)

        w_at = -(-nc.sbuf_base // 32) * 32
        wslot = sb("wslot", [P, 6, KS * CH])
        act_at = w_at + 6 * KS * CH * 4
        actT = sb("actT", [P, KD, T])
        resid_at = act_at + KD * T * 4
        resid = sb("resid", [P, TB, D])
        assert nc.sbuf_base == resid_at + TB * D * 4 and nc.sbuf_base % 32 == 0
        unit_bytes = KU * CH * 4
        w_lo = another_name("w_lo", [P, UNITS, KU, CH], w_at)
        w_hi = another_name("w_hi", [P, UNITS, KU, CH], w_at + UNITS * unit_bytes)
        act_hi = another_name("act_hi", [P, KD, T], act_at)
        act_lo = another_name("act_lo", [P, KD, T], resid_at)
        w_raw = wslot[:, 0:2, :].rearrange("p a n -> p (a n)").rearrange("p (u k n) -> p u k n", u=UNITS, k=KU)
        gates_at = nc.sbuf_base
        gates = sb("gates", [P, TB, 2 * D])
        m_lo = another_name("m_lo", [P, TB, 2 * D], gates_at)
        norm_g = sb("norm_g", [P, D])
        qa = sb("qa", [P, TB, W_ATT])
        kv = sb("kv", [P, TB, 2 * KV])
        o_at = nc.sbuf_base
        oT = sb("oT", [P, KD, T])
        m_hi = another_name("m_hi", [P, KD, T], o_at)
        oaT, ohT = oT[:, 0:HEADS, :], oT[:, HEADS:KD, :]
        hT = actT
        cst = sb("cst", [P, K_END])
        sinks = sb("sinks", [P, 2 * HEADS])
        hnorm = sb("hnorm", [P, HW])
        lbT = sb("lbT", [P, 2, HEADS])
        stat = sb("stat", [P, 32])
        small = sb("small", [P, 64])
        msq = small[:, 24:24 + TB * NC].rearrange("p (b c) -> p b c", b=TB)
        half_rstd = small[:, 32:32 + TB]
        nwt = small[:, 40:40 + 2 * TB]
        over_i = sb("over_i", [P, LIST + 1], mybir.dt.int32)
        ident = cst[:, K_ID:K_ID + P]

        work = wslot[:, 4:6, :].rearrange("p a n -> p (a n)")
        square_scratch = qa[:, 1, 0:CH]
        at = [0]

        def carve(*shape):
            n = 1
            for s in shape:
                n *= s
            ap = work[:, at[0]:at[0] + n]
            at[0] += n
            assert at[0] <= 2 * KS * CH
            if len(shape) == 2:
                return ap.rearrange("p (a b) -> p a b", a=shape[0])
            if len(shape) == 3:
                return ap.rearrange("p (a b c) -> p a b c", a=shape[0], b=shape[1])
            return ap
        qs = carve(TB, P)
        ks = carve(TB, P)
        vs = carve(TB, DH)
        qkT = carve(2, T)
        prob = carve(2, 3 * P)
        probT = carve(2, 3 * P)
        es = carve(TB, 3 * P)
        qrow = carve(TB, HW)
        orow = carve(TB, HW)
        irow = carve(TB, HW)
        qT = carve(T)
        fT = carve(T)
        qp = carve(T)
        kq = carve(T)
        tot = carve(T)
        hatt = carve(T)
        crossT = carve(P)
        oh = carve(TB, HW)
        sk = carve(2, 2)
        lbs = carve(2)
        mx = carve(2, 2)
        mneg = carve(2, 2)
        esink = carve(2, 2)
        psums = carve(2, 2)
        rden = carve(2, 2)
        lbrow = carve(2, P)
        lev = norm_g[:, :].rearrange("p (l t) -> p l t", l=LEVELS + 1)
        merged = norm_g[:, 0:TB * CH].rearrange("p (b n) -> p b n", b=TB)
        merged2 = norm_g[:, TB * CH:2 * TB * CH].rearrange("p (b n) -> p b n", b=TB)

        pair = [ps("pair0", [P, TB, CH]), ps("pair1", [P, TB, CH])]
        four = ps("four", [P, 4, CH])
        flat4 = four[:, :, :].rearrange("p a n -> p (a n)")
        levp = flat4.rearrange("p (l t) -> p l t", l=8)
        bank_t = four[:, 2, :]
        bank_o = four[:, 3, :]

        x_in = [sem(f"x_in{b}") for b in range(TB)]
        ms_done = sem("ms_done")
        hg_ready = sem("hg_ready")
        g_in = sem("g_in")
        c_in = sem("c_in")
        loaded = [sem(f"loaded{s}") for s in range(6)]
        o_hi_ready = sem("o_hi_ready")
        o_lo_ready = sem("o_lo_ready")
        m_lo_ready = sem("m_lo_ready")
        unit_in = [sem(f"unit_in{u}") for u in range(UNITS)]
        hi_ready = sem("hi_ready")
        lo_ready = sem("lo_ready")
        xl_ready = sem("xl_ready")
        unit_used = sem("unit_used")
        dve_step = sem("dve_step")
        act_step = sem("act_step")
        rstd_done = sem("rstd_done")
        xn_ready = sem("xn_ready")
        tp_ready = sem("tp_ready")
        tp_copied = sem("tp_copied")
        lb_in = sem("lb_in")
        lb_rows = sem("lb_rows")
        lb_e = sem("lb_e")
        lb_s = sem("lb_s")
        lb_t = sem("lb_t")
        lb_done = sem("lb_done")
        pair0_act = sem("pair0_act")
        pair1_act = sem("pair1_act")
        pair0_dve = sem("pair0_dve")
        staged = sem("staged")
        qkT_ready = sem("qkT_ready")
        qkT_copied = sem("qkT_copied")
        score_ready = sem("score_ready")
        max_ready = sem("max_ready")
        exp_done = sem("exp_done")
        prob_ready = sem("prob_ready")
        probT_ready = sem("probT_ready")
        probT_copied = sem("probT_copied")
        oT_ready = sem("oT_ready")
        oaT_done = sem("oaT_done")
        es_ready = sem("es_ready")
        hg_rows = sem("hg_rows")
        qfT_ready = sem("qfT_ready")
        qT_copied = sem("qT_copied")
        level_ops = sem("level_ops")
        level_mm = sem("level_mm")
        lev_read = sem("lev_read")
        cross_mm = sem("cross_mm")
        cross_copied = sem("cross_copied")
        hatt_ready = sem("hatt_ready")
        ho_ready = sem("ho_ready")
        ho_sq = sem("ho_sq")
        oh_ready = sem("oh_ready")
        ohT_ready = sem("ohT_ready")
        ohT_done = sem("ohT_done")
        y_read = sem("y_read")
        merged_ready = sem("merged_ready")
        mT_ready = sem("mT_ready")
        mT_done = sem("mT_done")
        h_added = sem("h_added")
        g2_in = sem("g2_in")
        g3_in = sem("g3_in")
        r_in = sem("r_in")
        logit_ready = sem("logit_ready")
        logit_read = sem("logit_read")
        r_exp_in = sem("r_exp_in")
        r_exp = sem("r_exp")
        coef_ready = sem("coef_ready")
        gathered = sem("gathered")
        xg_copied = sem("xg_copied")
        swT_ready = sem("swT_ready")
        swT_copied = sem("swT_copied")
        onehot_ready = sem("onehot_ready")
        sw_ready = sem("sw_ready")
        ghid_ready = sem("ghid_ready")
        ge_exp = sem("ge_exp")
        ghT_ready = sem("ghT_ready")
        ghT_copied = sem("ghT_copied")
        yg_act = sem("yg_act")
        yg_dve = sem("yg_dve")
        back_ready = sem("back_ready")
        scattered = sem("scattered")
        quarter_used = sem("quarter_used")
        mask_ready = sem("mask_ready")
        rank_ready = sem("rank_ready")
        rank_read = sem("rank_read")
        over_ready = sem("over_ready")
        over_step = sem("over_step")
        oh13_ready = sem("oh13_ready")
        oy_ready = sem("oy_ready")
        resid_done = sem("resid_done")
        e_exp = sem("e_exp")
        hid_ready = sem("hid_ready")
        hidT_ready = sem("hidT_ready")
        hidT_copied = sem("hidT_copied")
        y_added = sem("y_added")
        o_ready = sem("o_ready")
        stored = sem("stored")

        gflat = gates[:, :, :].rearrange("p a n -> p (a n)")
        hn = gates[:, :, 0:D]
        hid = gates[:, :, D:D + FE]
        ehid = gates[:, :, D + FE:D + 2 * FE]
        xg = gates[:, 0, D:2 * D].rearrange("p (k n) -> p k n", k=KD)
        yg = gates[:, 1, D:2 * D]
        gwork = oT[:, KS:KD, :].rearrange("p a n -> p (a n)")
        gh = gwork[:, 0:T].rearrange("p (b n) -> p b n", b=TB)
        sw = gwork[:, T:2 * T].rearrange("p (b n) -> p b n", b=TB)
        swT = gwork[:, 2 * T:3 * T]
        geh = gwork[:, 3 * T:3 * T + P]
        ghid = gwork[:, 3 * T + P:4 * T]
        ghT = gwork[:, 4 * T:4 * T + P]
        hidT = gates[:, :, D + 2 * FE:D + 4 * FE].rearrange("p b (k t) -> p b k t", k=4)[:, :, :, 0:P]
        wr = qa[:, :, :].rearrange("p a n -> p (a n)")[:, 0:KD * NR].rearrange("p (k n) -> p k n", k=KD)
        br = kv[:, 0, 0:NR]
        rwork = kv[:, :, :].rearrange("p a n -> p (a n)")
        coef = oT[:, 0, 0:TB * NE].rearrange("p (b e) -> p b e", b=TB)
        rmask = oT[:, 1, 0:TB * NE].rearrange("p (b e) -> p b e", b=TB)
        place = oT[:, 2, 0:TB * NE].rearrange("p (b e) -> p b e", b=TB)
        late = oT[:, 3, 0:TB * NE].rearrange("p (b e) -> p b e", b=TB)
        ocoef = oT[:, 4, 0:TB * NE].rearrange("p (b e) -> p b e", b=TB)
        lrow = oT[:, 5, 0:2 * NE + LIST + 1]
        llist = oT[0:1, 6:8, :].rearrange("p a n -> p (a n)").rearrange("p (j e) -> p j e", j=LIST)

        w_in_k = w_in[0].rearrange("(k p) n -> p k n", p=P)
        w_gather = w_in[0][:, C_HGRN:C_GATE].rearrange("(k p) (j c) -> p k j c", p=P, j=4)
        wa_k = w_br_attn[0].rearrange("(k p) n -> p k n", p=P)
        wh_k = w_br_hgrn[0].rearrange("(k p) n -> p k n", p=P)
        wo_k = w_out[0].rearrange("(k p) n -> p k n", p=P)
        w1_k = w1[0].rearrange("e (k p) f -> e p k f", p=P)
        w3_k = w3[0].rearrange("e (k p) f -> e p k f", p=P)
        w2_k = w2[0].rearrange("e (k p) n -> e p k n", p=P)

        def slot(s):
            return wslot[:, s, :].rearrange("p (k n) -> p k n", k=KS)

        def slot_w2(s):
            return wslot[:, s, :].rearrange("p (k n) -> p k n", k=2)

        PRO = 3
        CU = KD // KU
        N_PRO = PRO * CU
        HU = 2 * CU
        N_UNITS = N_PRO + HEADS * HU
        HU_IN = 16 * KU + 16
        N_WO = N_UNITS + NC * CU
        N_ALL = N_WO + NC * CU

        def unit_loaded(i, u):
            i, u = i + u // HU, u % HU
            return i * HU_IN + (16 * N_PRO // UNITS + (16 * KU if u < CU else HU_IN))

        def later_loaded(c, u):
            return c * 16 + (16 * N_PRO // UNITS + HEADS * HU_IN + 16 * (u // CU + 1))

        block = ctx.enter_context(nc.Block())

        @block.sync
        def _(sp):
            for b in range(TB):
                sp.dma_start(resid[:, b, :], x[0, b * P:(b + 1) * P, :]).then_inc(x_in[b], 16)
            sp.dma_start(norm_g[:, :], mix_norm_g[0:1, :].to_broadcast([P, D])).then_inc(g_in, 16)
            for n in range(N_PRO):
                c, part = divmod(n, CU)
                if n >= UNITS:
                    sp.wait_ge(unit_used, n - UNITS + 1)
                sp.dma_start(w_raw[:, n % UNITS], w_in_k[:, part * KU:(part + 1) * KU, c * CH:(c + 1) * CH])\
                    .then_inc(unit_in[n % UNITS], 16)
            with sp.Fori(0, HEADS) as i:
                for u in range(HU):
                    part = u % CU
                    sp.wait_ge(unit_used, i * HU + (N_PRO + u - UNITS + 1))
                    if u < CU:
                        for k in range(KU):
                            sp.dma_start(w_raw[:, u % UNITS, k].rearrange("p (j c) -> p j c", j=4),
                                         w_gather[:, part * KU + k, :, bass.ts(i, HW)]).then_inc(unit_in[u % UNITS], 16)
                    else:
                        sp.dma_start(w_raw[:, u % UNITS], w_in_k[:, part * KU:(part + 1) * KU, bass.ds(i * CH + C_GATE, CH)])\
                            .then_inc(unit_in[u % UNITS], 16)
            with sp.Fori(0, NC) as c:
                for u in range(CU):
                    sp.wait_ge(unit_used, c * CU + (N_UNITS + u - UNITS + 1))
                    w, part = (wa_k, wh_k)[u // 2], u % 2
                    sp.dma_start(w_raw[:, u % UNITS], w[:, part * KU:(part + 1) * KU, bass.ds(c * CH, CH)])\
                        .then_inc(unit_in[u % UNITS], 16)
            for n in range(NC * CU):
                c, part = divmod(n, CU)
                sp.wait_ge(unit_used, N_WO + n - UNITS + 1)
                sp.dma_start(w_raw[:, n % UNITS], wo_k[:, part * KU:(part + 1) * KU, c * CH:(c + 1) * CH])\
                    .then_inc(unit_in[n % UNITS], 16)
                if n == CU - 1:
                    for b in range(TB):
                        sp.dma_start(resid[:, b, :], x[0, b * P:(b + 1) * P, :]).then_inc(x_in[b], 16)

            def load_expert(e, s):
                if s < 4:
                    src = (w1_k, w3_k)[s % 2][bass.ds(e, 1), :, (s // 2) * KS:(s // 2 + 1) * KS, :]
                    dst = slot(s)
                else:
                    src = w2_k[bass.ds(e, 1), :, 2 * (s % 2):2 * (s % 2) + 2, :]
                    dst = slot_w2(s)
                sp.dma_start(dst, src.rearrange("a p k n -> (a p) k n")).then_inc(loaded[s], 16)

            sp.wait_ge(ohT_done, HEADS + ONE)
            for s in (4, 5):
                load_expert(0, s)
            for s in range(4):
                sp.wait_ge(unit_used, N_ALL - (2 if s == 0 else 0))
                load_expert(0, s)
            with sp.Fori(1, NE) as e:
                for s in range(6):
                    sp.wait_ge(quarter_used, e * 4 + ((1, 1, 2, 2, 3, 4)[s] - 4))
                    load_expert(e, s)
            sp.wait_ge(over_ready, 1)
            sp.wait_ge(quarter_used, 4 * NE)
            n_over = sp.value_load(over_i[0:1, LIST:LIST + 1], min_val=0, max_val=LIST)
            with sp.If(n_over > 0):
                with sp.Fori(0, n_over) as j:
                    e = sp.value_load(over_i[0:1, bass.ds(j, 1)], min_val=0, max_val=NE - 1)
                    for s in range(6):
                        if s == 0:
                            sp.wait_ge(oh13_ready, j * TB + ONE)
                        if s == 4:
                            sp.wait_ge(oy_ready, j * 2 * NC + ONE)
                        load_expert(e, s)
            for b in range(TB):
                sp.wait_ge(o_ready, b + 1)
                sp.dma_start(out[0, b * P:(b + 1) * P, :], resid[:, b, :]).then_inc(stored, 16)
            sp.wait_ge(stored, 16 * TB)

        @block.gpsimd
        def _(pool):
            def split_lo(n, u):
                pool.wait_ge(hi_ready, n)
                nc.gpsimd.tensor_tensor(w_lo[:, u % UNITS], w_raw[:, u % UNITS], w_hi[:, u % UNITS].bitcast(F32), ALU.subtract)\
                    .then_inc(lo_ready, 1)

            def stage_qk(i):
                nc.gpsimd.tensor_copy(qs, qa[:, :, bass.ts(i, P)]).then_inc(staged, 1)
                k_cols = kv[:, :, bass.ds((i // 2) * DH, DH)]
                nc.gpsimd.tensor_copy(ks[:, :, 0:DH], k_cols).then_inc(staged, 1)
                nc.gpsimd.tensor_copy(ks[:, :, DH:P], k_cols).then_inc(staged, 1)

            def stage_v(i):
                nc.gpsimd.tensor_copy(vs, kv[:, :, bass.ds((i // 2) * DH + KV, DH)]).then_inc(staged, 1)

            def stage_sinks(i):
                nc.gpsimd.tensor_copy(sk, bc(sinks[:, bass.ts(i, 2)].unsqueeze(1), [P, 2, 2])).then_inc(staged, 1)

            for n in range(N_PRO + 2):
                split_lo(n + 1, n)
            pool.wait_ge(pair1_act, 2)
            pool.wait_ge(pair0_act, 1)
            pool.wait_ge(c_in, 16 * 3)
            pool.wait_ge(lb_done, 1)
            stage_qk(0)
            stage_v(0)
            stage_sinks(0)

            def head(i, last):
                for u in range(2, HU + 2):
                    split_lo(i * HU + (N_PRO + u + 1), u)
                    if u == 3 and not last:
                        pool.wait_ge(qkT_ready, i + 1 + ONE)
                        settle(pool, c_in)
                        stage_qk(i + 1)
                    if u == 5 and not last:
                        pool.wait_ge(oT_ready, i + 1 + ONE)
                        settle(pool, c_in)
                        stage_v(i + 1)
                        pool.wait_ge(prob_ready, i * 4 + 4 + ONE)
                        settle(pool, c_in)
                        stage_sinks(i + 1)
            with pool.Fori(0, HEADS - 1) as i:
                head(i, False)
            head(HEADS - 1, True)
            with pool.Fori(0, 2 * NC - 1) as c:
                for u in range(2, CU + 2):
                    split_lo(c * CU + (N_UNITS + u + 1), u)
            for u in range(2, CU):
                split_lo(N_ALL - CU + u + 1, u)

        @block.scalar
        def _(act):
            for ahead in (ohT_done, cross_copied, mT_done, hidT_copied, ghT_copied, yg_act):
                act.sem_inc(ahead, ONE)
            def h_copy(c):
                act.wait_ge(tp_ready, 4 + c + 1)
                nc.scalar.activation(hT[:, 4 * c:4 * c + 4, :], levp[:, 4 * (c % 2):4 * (c % 2) + 4, :], ACT.Copy)\
                    .then_inc(tp_copied, 1)

            def mean_square(b, dst, src, n, col):
                return nc.scalar.activation(dst, src, ACT.Square, scale=n ** -0.5, accum_out=stat[:, col + b:col + b + 1])

            def split_hi(u, there):
                act.wait_ge(unit_in[u % UNITS], there)
                nc.scalar.activation(w_hi[:, u % UNITS], w_raw[:, u % UNITS], ACT.Copy).then_inc(hi_ready, 1)

            act.dma_start(cst[:, :], consts).then_inc(c_in, 16)
            act.dma_start(sinks[:, :], attn_sinks[0:1, :].to_broadcast([P, 2 * HEADS])).then_inc(c_in, 16)
            act.dma_start(hnorm[:, :], hgrn_norm_g[0:1, :].to_broadcast([P, HW])).then_inc(c_in, 16)
            for r in range(2):
                act.dma_start(lbrow[0:HEADS, r, :], hgrn_lb_logits[r].rearrange("(h c) -> h c", h=HEADS))\
                    .then_inc(lb_in, 16)
            act.wait_ge(x_in[0], 16)
            mean_square(0, actT[:, 0:KS, :].rearrange("p a b -> p (a b)"), resid[:, 0, :], D, 0).then_inc(ms_done, 1)
            act.wait_ge(lb_rows, 2)
            nc.scalar.activation(lbrow[0:HEADS, :, :], lbrow[0:HEADS, :, :], ACT.Exp).then_inc(lb_e, 1)
            for n in range(2):
                split_hi(n, 16)
            for g in range(4):
                act.wait_ge(tp_ready, g + 1)
                nc.scalar.activation(act_hi[:, 4 * g:4 * g + 4, :],
                                     levp[:, 4 * (g % 2):4 * (g % 2) + 4, :], ACT.Copy).then_inc(tp_copied, 1)
            act.wait_ge(lb_t, 1)
            nc.scalar.activation(lbT[:, :, :], flat4[:, 0:2 * HEADS].rearrange("p (a h) -> p a h", a=2), ACT.Copy).then_inc(lb_done, 1)
            for n in range(2, N_PRO + 3):
                if n % CU == 2 and n > 2:
                    c = n // CU - 1
                    act.wait_ge(unit_used, c * CU + CU)
                    dst = qa[:, :, c * CH:(c + 1) * CH] if c < 2 else kv[:, :, :]
                    nc.scalar.activation(dst, pair[(c + 1) % 2][:, :, :], ACT.Copy, scale=DH ** -0.5 if c < 2 else 1.0)\
                        .then_inc(pair1_act if c != 1 else pair0_act, 1)
                if n < N_PRO + 2:
                    split_hi(n, 16 * (n // UNITS + 1) if n < N_PRO else unit_loaded(0, n - N_PRO))

            def o_split_hi(g):
                if g == 0:
                    act.wait_ge(unit_used, N_UNITS)
                    act.wait_ge(oaT_done, HEADS)
                if g == 2:
                    act.wait_ge(ohT_done, HEADS + ONE)
                nc.scalar.activation(act_hi[:, 4 * g:4 * g + 4, :], oT[:, 4 * g:4 * g + 4, :], ACT.Copy).then_inc(o_hi_ready, 1)

            def head(i, last):
                def hi(u):
                    split_hi(u, later_loaded(0, u - HU) if last and u >= HU else unit_loaded(i, u))

                act.wait_ge(qkT_ready, i + 1 + ONE)
                act.wait_ge(score_ready, i + ONE)
                nc.scalar.activation(qkT, bank_t.rearrange("p (a t) -> p a t", a=2), ACT.Copy).then_inc(qkT_copied, 1)
                hi(2)
                hi(3)
                act.wait_ge(max_ready, i + 1)
                for h in range(2):
                    nc.scalar.activation(prob[:, h, 0:P], prob[:, h, 0:P], ACT.Exp, bias=mneg[:, 0, h:h + 1],
                                         accum_out=psums[:, 0, h:h + 1]).then_inc(exp_done, 1)
                    nc.scalar.activation(prob[:, h, P:3 * P], prob[:, h, P:3 * P], ACT.Exp, bias=mneg[:, 1, h:h + 1],
                                         accum_out=psums[:, 1, h:h + 1]).then_inc(exp_done, 1)
                nc.scalar.activation(esink, esink, ACT.Exp).then_inc(exp_done, 1)
                hi(4)
                act.wait_ge(probT_ready, i + 1)
                act.wait_ge(oT_ready, i + ONE)
                nc.scalar.activation(probT[:, 0, :], bank_t[:, 0:3 * P], ACT.Copy).then_inc(probT_copied, 1)
                nc.scalar.activation(probT[:, 1, :], bank_o[:, 0:3 * P], ACT.Copy).then_inc(probT_copied, 1)
                act.wait_ge(oT_ready, i + 1 + ONE)
                settle(act, c_in)
                nc.scalar.activation(oaT[:, bass.ds(i, 1), :].rearrange("p a t -> p (a t)"), four[:, 0, 0:T], ACT.Copy)\
                    .then_inc(oaT_done, 1)
                hi(5)
                act.wait_ge(unit_used, i * HU + (N_PRO + CU))
                act.wait_ge(pair0_dve, i + ONE)
                nc.scalar.activation(es[:, :, 0:2 * HW], pair[0][:, :, 0:2 * HW], ACT.Tanh, scale=0.5).then_inc(es_ready, 1)
                nc.scalar.activation(es[:, :, 2 * HW:3 * HW], pair[0][:, :, 3 * HW:4 * HW], ACT.Tanh, scale=0.5)\
                    .then_inc(es_ready, 1)
                act.wait_ge(ho_ready, i + ONE)
                nc.scalar.activation(irow, pair[0][:, :, 2 * HW:3 * HW], ACT.Copy).then_inc(pair0_act, 1)
                hi(6)
                act.wait_ge(qfT_ready, i + 1)
                act.wait_ge(level_mm, i * 9 + ONE)
                nc.scalar.activation(qT, bank_t[:, 0:T], ACT.Copy, scale=Q_SCALE).then_inc(qT_copied, 1)
                hi(7)
                hi(8)
                act.wait_ge(level_mm, i * 9 + 9 + ONE)
                nc.scalar.activation(crossT, four[:, 0, 0:P], ACT.Copy).then_inc(cross_copied, 1)
                hi(9)
                act.wait_ge(ho_ready, i + 1 + ONE)
                for b in range(TB):
                    mean_square(b, es[:, b, 0:HW], bank_o[:, b * HW:(b + 1) * HW], HW, 4).then_inc(ho_sq, 1)
                if last:
                    o_split_hi(0)
                    o_split_hi(1)
                act.wait_ge(ohT_ready, i + 1)
                settle(act, c_in)
                nc.scalar.activation(ohT[:, bass.ds(i, 1), :].rearrange("p a t -> p (a t)"), bank_t[:, 0:T], ACT.Copy)\
                    .then_inc(ohT_done, 1)
                act.wait_ge(unit_used, i * HU + (N_PRO + HU))
                settle(act, c_in)
                nc.scalar.activation(gates[:, :, bass.ts(i, CH)], pair[1][:, :, :], ACT.Tanh, scale=0.5)\
                    .then_inc(pair1_act, 1)
            with act.Fori(0, HEADS - 1) as i:
                head(i, False)
            head(HEADS - 1, True)
            o_split_hi(2)
            o_split_hi(3)

            def m_split_hi(c):
                act.wait_ge(mT_ready, c + 1 + ONE)
                settle(act, c_in)
                dst = m_hi[:, bass.ds(c * 4, 4), :]
                nc.scalar.activation(dst, levp[:, 0:4, :], ACT.Copy, scale=0.5).then_inc(mT_done, 1)

            def branch_chunk(c, first):
                split_hi(2, later_loaded(c, 2))
                split_hi(3, later_loaded(c, 3))
                if not first:
                    m_split_hi(c - 1)
                split_hi(4, later_loaded(c, 4))
                split_hi(5, later_loaded(c, 5))
            branch_chunk(0, True)
            with act.Fori(1, NC) as c:
                branch_chunk(c, False)
            def square_sums(c):
                act.wait_ge(h_added, c + 1 + ONE)
                for b in range(TB):
                    nc.scalar.activation(square_scratch, resid[:, b, c * CH:(c + 1) * CH], ACT.Square, scale=D ** -0.5,
                                         accum_out=msq[:, b, c:c + 1]).then_inc(act_step, 1)
                    act.wait_ge(act_step, c * TB + b + 1)
            for c in range(NC):
                split_hi(2, later_loaded(NC + c, 2))
                if c == 0:
                    m_split_hi(NC - 1)
                split_hi(3, later_loaded(NC + c, 3))
                if c == 0:
                    act.dma_start(norm_g[:, :], moe_norm_g[0:1, :].to_broadcast([P, D])).then_inc(g2_in, 16)
                    act.wait_ge(staged, 5 * HEADS)
                    act.dma_start(wr[:, :, 0:NG], w_router_group[0].rearrange("(k p) n -> p k n", p=P)).then_inc(r_in, 16)
                    act.dma_start(wr[:, :, NG:NR], w_router_expert[0].rearrange("(k p) n -> p k n", p=P)).then_inc(r_in, 16)
                    act.dma_start(br[:, 0:NG], b_router_group[0:1, :].to_broadcast([P, NG])).then_inc(r_in, 16)
                    act.dma_start(br[:, NG:NR], b_router_expert[0:1, :].to_broadcast([P, NE])).then_inc(r_in, 16)
                else:
                    square_sums(c - 1)
                if c < NC - 1:
                    split_hi(4, later_loaded(NC + c, 4))
                if c:
                    h_copy(c - 1)
                if c < NC - 1:
                    split_hi(5, later_loaded(NC + c, 5))
            square_sums(NC - 1)
            h_copy(NC - 1)
            act.wait_ge(xn_ready, 2 * TB)
            act.dma_start(norm_g[:, :], final_norm_g.rearrange("(a d) -> a d", a=1).to_broadcast([P, D])).then_inc(g3_in, 16)
            act.wait_ge(r_exp_in, 1)
            nc.scalar.activation(small[:, 0:10], small[:, 0:10], ACT.Exp).then_inc(r_exp, 1)
            with act.Fori(0, GROUPS) as g:
                for half in range(2):
                    act.wait_ge(gathered, g * 2 + (half + 1) + ONE)
                    nc.scalar.activation(xg[:, half * KS:(half + 1) * KS, :],
                                         four[:, 2 * half:2 * half + 2, :].rearrange("p a (k n) -> p (a k) n", n=P),
                                         ACT.Copy).then_inc(xg_copied, 1)
                act.wait_ge(swT_ready, g + 1 + ONE)
                nc.scalar.activation(swT, pair[1][:, 0, 0:T], ACT.Copy).then_inc(swT_copied, 1)
                for q in range(GX):
                    hp = pair[0][:, q % 2, :]
                    yp = pair[1][:, q % 2, :]
                    act.wait_ge(quarter_used, g * (4 * GX) + (4 * q + 2))
                    act.wait_ge(ghid_ready, g * GX + q + ONE)
                    nc.scalar.activation(geh, hp[:, 0:P], ACT.Tanh, scale=0.5).then_inc(ge_exp, 1)
                    act.wait_ge(ghT_ready, g * GX + (q + 1) + ONE)
                    nc.scalar.activation(ghT, hp[:, 2 * P:3 * P], ACT.Copy, scale=0.5).then_inc(ghT_copied, 1)
                    act.wait_ge(quarter_used, g * (4 * GX) + (4 * q + 4))
                    for c in (0, 1):
                        nc.scalar.activation(yg[q * SL:(q + 1) * SL, c * CH:(c + 1) * CH], yp[c * SL:(c + 1) * SL, :],
                                             ACT.Copy).then_inc(yg_act, 1)
            act.wait_ge(over_ready, 1)
            act.wait_ge(scattered, GROUPS * 2 * NC + ONE)
            n_over = act.value_load(over_i[0:1, LIST:LIST + 1], min_val=0, max_val=LIST)
            with act.If(n_over > 0):
                with act.Fori(0, n_over) as e:
                    for b in range(TB):
                        act.wait_ge(oh13_ready, e * 2 + (b + 1) + ONE)
                        act.wait_ge(hid_ready, e * 2 + b + ONE)
                        nc.scalar.activation(ehid[:, b, :], pair[b][:, 0, :], ACT.Tanh, scale=half_rstd[:, b:b + 1]).then_inc(e_exp, 1)
                        act.wait_ge(hidT_ready, e * 2 + (b + 1) + ONE)
                        nc.scalar.activation(hidT[:, b], four[:, 3, :].rearrange("p (k t) -> p k t", k=4), ACT.Copy)\
                            .then_inc(hidT_copied, 1)
            act.wait_ge(resid_done, 1)
            mean_square(0, gates[:, 0, 0:D], resid[:, 0, :], D, 12).then_inc(ms_done, 1)

        @block.tensor
        def _(pe):
            for ahead in (oh13_ready, oy_ready, gathered, swT_ready, ghT_ready, qkT_ready, oT_ready, score_ready, ho_ready, level_mm, mT_ready, hidT_ready):
                pe.sem_inc(ahead, ONE)
            def transpose_rows(src, first, per_copy):
                for g in range(4):
                    if first + g >= 2:
                        pe.wait_ge(xl_ready, first + g - 1)
                    for k in range(4):
                        for b in range(TB):
                            kk = 4 * g + k
                            last = nc.tensor.transpose(levp[:, 4 * (g % 2) + k, b * P:(b + 1) * P],
                                                       src[:, b, kk * P:(kk + 1) * P], ident)
                    last.then_inc(tp_ready, 1)

            pe.wait_ge(xn_ready, TB)
            pe.wait_ge(c_in, 16 * 3)
            transpose_rows(gates, 0, 4)
            pe.wait_ge(lb_s, 2)
            pe.wait_ge(xl_ready, 4)
            for a in range(2):
                last = nc.tensor.transpose(flat4[:, a * HEADS:(a + 1) * HEADS], lbrow[0:HEADS, a, :], ident[0:HEADS, 0:HEADS])
            last.then_inc(lb_t, 1)

            def project(dst, u, k, hi=act_hi, lo=act_lo, first=0, end=KD):
                wh, wl = w_hi[:, u % UNITS, k % KU, :], w_lo[:, u % UNITS, k % KU, :]
                for b in range(TB):
                    xh = hi[:, k, b * P:(b + 1) * P]
                    xl = m_lo[:, b, D + k * P:D + (k + 1) * P] if lo is m_lo else lo[:, k, b * P:(b + 1) * P]
                    nc.tensor.matmul(dst[:, b, :], xh, wh, start=(k == first), stop=False)
                    nc.tensor.matmul(dst[:, b, :], xh, wl, start=False, stop=False)
                    last = nc.tensor.matmul(dst[:, b, :], xl, wh, start=False, stop=(k == end - 1))
                if k % KU == KU - 1:
                    last.then_inc(unit_used, 1)

            for n in range(N_PRO):
                c = n // CU
                if n == 2 * CU:
                    pe.wait_ge(pair1_act, 1)
                pe.wait_ge(lo_ready, n + 1)
                for k in range((n % CU) * KU, (n % CU + 1) * KU):
                    project(pair[(c + 1) % 2], n, k)

            with pe.Fori(0, HEADS) as i:
                def a_transpose():
                    pe.wait_ge(staged, i * 5 + 5)
                    pe.wait_ge(ohT_done, i + ONE)
                    pe.wait_ge(lb_done, 1)
                    for a, src in enumerate((qs, ks)):
                        for b in range(TB):
                            last = nc.tensor.transpose(bank_t[:, a * T + b * P:a * T + (b + 1) * P], src[:, b, :], ident)
                    last.then_inc(qkT_ready, 1)

                def a_scores():
                    pe.wait_ge(qkT_copied, i + 1)
                    pe.wait_ge(lev_read, i * 2 + ONE)
                    pe.wait_ge(cross_copied, i + ONE)
                    for h in range(2):
                        r = slice(h * DH, (h + 1) * DH)
                        nc.tensor.matmul(four[:, h, 0:P], qkT[r, 0, 0:P], qkT[r, 1, 0:P], start=True, stop=True)
                        last = nc.tensor.matmul(four[:, h, P:3 * P], qkT[r, 0, P:T], qkT[r, 1, :], start=True, stop=True)
                    last.then_inc(score_ready, 1)

                def a_probT():
                    pe.wait_ge(prob_ready, i * 4 + 4 + ONE)
                    pe.wait_ge(oh_ready, i * 2 + ONE)
                    for h in range(2):
                        bank = (bank_t, bank_o)[h]
                        for k in range(3):
                            last = nc.tensor.transpose(bank[:, k * P:(k + 1) * P], prob[:, h, k * P:(k + 1) * P], ident)
                    last.then_inc(probT_ready, 1)

                def a_values():
                    pe.wait_ge(probT_copied, i * 2 + 2)
                    for h in range(2):
                        o = four[h * DH:(h + 1) * DH, 0, :]
                        nc.tensor.matmul(o[:, P:T], vs[:, 0, :], probT[:, h, P:2 * P], start=True, stop=False)
                        nc.tensor.matmul(o[:, P:T], vs[:, 1, :], probT[:, h, 2 * P:3 * P], start=False, stop=True)
                        last = nc.tensor.matmul(o[:, 0:P], vs[:, 0, :], probT[:, h, 0:P], start=True, stop=True)
                    last.then_inc(oT_ready, 1)

                def h_transpose():
                    pe.wait_ge(hg_rows, i + 1 + ONE)
                    for a, src in enumerate((qrow, es[:, :, HW:2 * HW])):
                        for b in range(TB):
                            last = nc.tensor.transpose(bank_t[:, a * T + b * P:a * T + (b + 1) * P], src[:, b, :], ident)
                    last.then_inc(qfT_ready, 1)

                def h_level(lv):
                    def go():
                        if lv == 0:
                            pe.wait_ge(qT_copied, i + 1)
                            pe.wait_ge(oaT_done, i + 1)
                        pe.wait_ge(level_ops, i * 8 + max(lv, 1))
                        if lv == LEVELS + 1:
                            pe.wait_ge(lev_read, i * 2 + 1 + ONE)
                            nc.tensor.matmul(four[:, 0, 0:P], kq[:, 0:P], qp[:, P:T], start=True, stop=True)\
                                .then_inc(level_mm, 1)
                            return
                        for b in range(TB):
                            rhs = (qT if lv == 0 else qp)[:, b * P:(b + 1) * P]
                            last = nc.tensor.matmul(levp[:, lv, b * P:(b + 1) * P], kq[:, b * P:(b + 1) * P], rhs,
                                                    start=True, stop=True)
                        last.then_inc(level_mm, 1)
                    return go

                def h_values():
                    pe.wait_ge(hatt_ready, i + 1)
                    pe.wait_ge(cross_copied, i + 1 + ONE)
                    pe.wait_ge(pair0_act, i + 2)
                    o = [bank_o[:, b * HW:(b + 1) * HW] for b in range(TB)]
                    nc.tensor.matmul(o[0], hatt[:, 0:P], irow[:, 0, :], start=True, stop=True)
                    nc.tensor.matmul(o[1], hatt[:, P:T], irow[:, 1, :], start=True, stop=False)
                    nc.tensor.matmul(o[1], crossT, irow[:, 0, :], start=False, stop=True).then_inc(ho_ready, 1)

                def h_outT():
                    pe.wait_ge(oh_ready, i * 2 + 2 + ONE)
                    for b in range(TB):
                        last = nc.tensor.transpose(bank_t[:, b * P:(b + 1) * P], oh[:, b, :], ident)
                    last.then_inc(ohT_ready, 1)

                tasks = {0: [a_transpose], 1: [a_scores], 8: [a_probT], 10: [a_values],
                         KD + 1: [h_transpose], KD + 3: [h_level(0), h_level(1)], KD + 4: [h_level(2)],
                         KD + 5: [h_level(3)], KD + 6: [h_level(4)], KD + 7: [h_level(5)],
                         KD + 8: [h_level(6)], KD + 9: [h_level(7)], KD + 10: [h_level(8)],
                         KD + 13: [h_values]}
                for u in range(HU):
                    if u == 0:
                        pe.wait_ge(pair0_act, i + 1)
                        pe.wait_ge(pair0_dve, i + ONE)
                    if u == CU:
                        pe.wait_ge(pair1_act, i + 2)
                    pe.wait_ge(lo_ready, i * HU + (N_PRO + u + 1))
                    for k in range((u % CU) * KU, (u % CU + 1) * KU):
                        project(pair[u // CU], u, k)
                        for task in tasks.get((u // CU) * KD + k, ()):
                            task()
                h_outT()

            def turn_merged(c):
                pe.wait_ge(merged_ready, c + 1)
                pe.wait_ge(m_lo_ready, TB * c)
                for k in range(4):
                    for b in range(TB):
                        last = nc.tensor.transpose(levp[:, k, b * P:(b + 1) * P], merged[:, b, k * P:(k + 1) * P], ident)
                last.then_inc(mT_ready, 1)

            def branch_chunk(c, first):
                for u in range(CU):
                    if first:
                        pe.wait_ge(o_lo_ready, u + 1)
                        if u == 0:
                            pe.wait_ge(pair0_act, HEADS + 1)
                            pe.wait_ge(pair0_dve, HEADS + ONE)
                        if u == CU // 2:
                            pe.wait_ge(pair1_act, HEADS + 2)
                    elif u % 2 == 0:
                        pe.wait_ge(y_read, c * 2 + (u // 2 - 1) + ONE)
                    pe.wait_ge(lo_ready, c * CU + (N_UNITS + u + 1))
                    for k in range(u * KU, (u + 1) * KU):
                        project(pair[u // 2], u, k, first=u // 2 * KS, end=u // 2 * KS + KS)
                    if u == 0 and not first:
                        turn_merged(c - 1)
            branch_chunk(0, True)
            with pe.Fori(1, NC) as c:
                branch_chunk(c, False)
            def h_transpose_chunk(c):
                pe.wait_ge(hg_ready, c + 1)
                pe.wait_ge(tp_copied, 4 + c - 1)
                for k in range(4):
                    for b in range(TB):
                        kk = 4 * c + k
                        last = nc.tensor.transpose(levp[:, 4 * (c % 2) + k, b * P:(b + 1) * P],
                                                   hn[:, b, kk * P:(kk + 1) * P], ident)
                last.then_inc(tp_ready, 1)

            for c in range(NC):
                if c < 2:
                    pe.wait_ge(y_read, 2 * NC - 1 + c + ONE)
                else:
                    pe.wait_ge(h_added, c - 1 + ONE)
                for u in range(CU):
                    if c == 0:
                        pe.wait_ge(m_lo_ready, TB * max(u + 1, NC - 1))
                    pe.wait_ge(lo_ready, N_WO + c * CU + u + 1)
                    for k in range(u * KU, (u + 1) * KU):
                        project(pair[c % 2], u, k, m_hi, m_lo)
                    if c == 0 and u == 0:
                        turn_merged(NC - 1)
                    if c and u == 1:
                        h_transpose_chunk(c - 1)
            pe.wait_ge(r_in, 16 * 4)
            pe.wait_ge(h_added, NC + ONE)
            h_transpose_chunk(NC - 1)
            pe.wait_ge(tp_copied, 8)
            for b in range(TB):
                for k in range(KD):
                    last = nc.tensor.matmul(pair[0][:, b, 0:NR], hT[:, k, b * P:(b + 1) * P], wr[:, k, :],
                                            start=(k == 0), stop=(k == KD - 1))
            last.then_inc(logit_ready, 1)
            pe.wait_ge(logit_read, 2)
            pe.wait_ge(mask_ready, 1)
            tri, ones = cst[:, K_TRI:K_TRI + P], cst[:, K_ONE:K_ONE + P]
            rank = pair[1][:, 0, 0:3 * NE].rearrange("p (b e) -> p b e", b=3)
            nc.tensor.matmul(rank[:, 0, :], tri, rmask[:, 0, :], start=True, stop=True)
            nc.tensor.matmul(rank[:, 1, :], tri, rmask[:, 1, :], start=True, stop=False)
            nc.tensor.matmul(rank[:, 1, :], ones, rmask[:, 0, :], start=False, stop=True)
            nc.tensor.matmul(rank[:, 2, :], ones, rmask[:, 0, :], start=True, stop=False)
            nc.tensor.matmul(rank[:, 2, :], ones, rmask[:, 1, :], start=False, stop=True).then_inc(rank_ready, 1)
            pe.wait_ge(rank_read, 1)
            with pe.Fori(0, GROUPS) as g:
                pe.wait_ge(onehot_ready, g * 2 + 2)
                pe.wait_ge(scattered, g * (2 * NC) + ONE)
                for k in range(KD):
                    for b in range(TB):
                        last = nc.tensor.matmul(flat4[:, k * P:(k + 1) * P], hn[:, b, k * P:(k + 1) * P],
                                                gh[:, b, :], start=(b == 0), stop=(b == TB - 1))
                    if k % KS == KS - 1:
                        last.then_inc(gathered, 1)
                pe.wait_ge(sw_ready, g * 2 + 2)
                pe.wait_ge(yg_act, g * (2 * GX) + ONE)
                pe.wait_ge(yg_dve, g * (2 * GX) + ONE)
                for b in range(TB):
                    last = nc.tensor.transpose(pair[1][:, 0, b * P:(b + 1) * P], sw[:, b, :], ident)
                last.then_inc(swT_ready, 1)
                for q in range(GX):
                    hp = pair[0][:, q % 2, :]
                    yp = pair[1][:, q % 2, :]
                    pe.wait_ge(xg_copied, g * 2 + 2)
                    pe.wait_ge(ghT_copied, g * GX + q + ONE)
                    for half in range(2):
                        for m in range(2):
                            s = 2 * half + m
                            pe.wait_ge(loaded[s], g * (16 * GX) + 16 * (q + 1))
                        for k in range(KS):
                            kk = half * KS + k
                            for c in range(4):
                                last = nc.tensor.matmul(
                                    hp[c * SL:(c + 1) * SL, 0:2 * P], xg[:, kk, q * SL:(q + 1) * SL],
                                    wslot[:, 2 * half:2 * half + 2, k * CH + c * P:k * CH + (c + 1) * P],
                                    start=(kk == 0), stop=(kk == KD - 1))
                        last.then_inc(quarter_used, 1)
                    pe.wait_ge(ghid_ready, g * GX + (q + 1) + ONE)
                    nc.tensor.transpose(hp[:, 2 * P:3 * P], ghid, ident).then_inc(ghT_ready, 1)
                    pe.wait_ge(ghT_copied, g * GX + (q + 1) + ONE)
                    pe.wait_ge(swT_copied, g + 1)
                    pe.wait_ge(yg_act, g * (2 * GX) + 2 * q + ONE)
                    pe.wait_ge(yg_dve, g * (2 * GX) + 2 * q + ONE)
                    for k in range(4):
                        if k % 2 == 0:
                            pe.wait_ge(loaded[4 + k // 2], g * (16 * GX) + 16 * (q + 1))
                        for c in range(4):
                            last = nc.tensor.matmul(yp[c * SL:(c + 1) * SL, :], ghT[:, k * SL:(k + 1) * SL],
                                                    slot_w2(4 + k // 2)[:, k % 2, c * CH:(c + 1) * CH],
                                                    start=(k == 0), stop=(k == 3))
                        if k % 2 == 1:
                            last.then_inc(quarter_used, 1)
                pe.wait_ge(yg_act, g * (2 * GX) + 2 * GX + ONE)
                pe.wait_ge(yg_dve, g * (2 * GX) + 2 * GX + ONE)
                for b in range(TB):
                    for c in range(NC):
                        if b == 1:
                            pe.wait_ge(scattered, g * (2 * NC) + (c + 1) + ONE)
                        nc.tensor.matmul(four[:, c, :], swT[:, b * P:(b + 1) * P], yg[:, c * CH:(c + 1) * CH],
                                         start=True, stop=True).then_inc(back_ready, 1)
            pe.wait_ge(over_ready, 1)
            pe.wait_ge(scattered, GROUPS * 2 * NC + ONE)
            n_over = pe.value_load(over_i[0:1, LIST:LIST + 1], min_val=0, max_val=LIST)
            with pe.If(n_over > 0):
                with pe.Fori(0, n_over) as e:
                    for b in range(TB):
                        pe.wait_ge(hid_ready, e * 2 + b + ONE)
                        for half in range(2):
                            for m in range(2):
                                s = 2 * half + m
                                if b == 0:
                                    pe.wait_ge(loaded[s], e * 16 + 16 * (1 + NE))
                                for k in range(KS):
                                    kk = half * KS + k
                                    last = nc.tensor.matmul(pair[b][:, m, :], hT[:, kk, b * P:(b + 1) * P], slot(s)[:, k, :],
                                                            start=(kk == 0), stop=(kk == KD - 1))
                        last.then_inc(oh13_ready, 1)
                    for b in range(TB):
                        pe.wait_ge(hid_ready, e * 2 + (b + 1) + ONE)
                        pe.wait_ge(y_added, e * 8 + b * 4 + ONE)
                        pe.wait_ge(hidT_copied, e * 2 + b + ONE)
                        for k in range(4):
                            last = nc.tensor.transpose(four[:, 3, k * P:(k + 1) * P], hid[:, b, k * P:(k + 1) * P], ident)
                        last.then_inc(hidT_ready, 1)
                        pe.wait_ge(hidT_copied, e * 2 + (b + 1) + ONE)
                        for half in range(2):
                            if b == 0:
                                pe.wait_ge(loaded[4 + half], e * 16 + 16 * (1 + NE))
                        for c in range(NC):
                            for k in range(4):
                                last = nc.tensor.matmul(four[:, c, :], hidT[:, b, k, :],
                                                        slot_w2(4 + k // 2)[:, k % 2, c * CH:(c + 1) * CH],
                                                        start=(k == 0), stop=(k == 3))
                            last.then_inc(oy_ready, 1)

        @block.vector
        def _(dve):
            for ahead in (prob_ready, hg_rows, hid_ready, lev_read, oh_ready, pair0_dve, y_read, h_added, y_added, scattered, ghid_ready, yg_dve):
                dve.sem_inc(ahead, ONE)
            chain = Chain(dve, dve_step)
            link = chain.link

            def mean_square_dve(b, dst, src, col):
                return nc.vector.tensor_tensor_reduce(out=dst, in0=src, in1=src, scale=1.0 / D, scalar=0.0, op0=ALU.mult,
                                                      op1=ALU.add, accum_out=stat[:, col + b:col + b + 1])

            def rstd(v):
                y, t = nwt[:, 0:TB], nwt[:, TB:2 * TB]
                link(nc.vector.tensor_scalar(v, v, EPS, None, ALU.add))
                link(nc.vector.tensor_scalar(y.bitcast(I32), v.bitcast(I32), -0.5, float(0x5F3759DF), ALU.mult, ALU.add))
                for step in range(4):
                    link(nc.vector.tensor_tensor(t, y, y, ALU.mult))
                    link(nc.vector.scalar_tensor_tensor(t, t, -0.5, v, ALU.mult, ALU.mult))
                    link(nc.vector.scalar_tensor_tensor(v if step == 3 else y, t, 1.5, y, ALU.add, ALU.mult))

            dve.wait_ge(x_in[1], 16)
            link(mean_square_dve(1, actT[:, KS:KD, :].rearrange("p a b -> p (a b)"), resid[:, 1, :], 0))
            dve.wait_ge(ms_done, 1)
            dve.wait_ge(g_in, 16)
            rstd(stat[:, 0:2])
            for b in range(TB):
                nc.vector.scalar_tensor_tensor(gates[:, b, 0:D], resid[:, b, :], stat[:, b:b + 1], norm_g[:, :],
                                               ALU.mult, ALU.mult).then_inc(xn_ready, 1)
            def xl(g):
                dve.wait_ge(tp_copied, g + 1)
                nc.vector.tensor_tensor(act_lo[:, 4 * g:4 * g + 4, :], levp[:, 4 * (g % 2):4 * (g % 2) + 4, :],
                                        act_hi[:, 4 * g:4 * g + 4, :].bitcast(F32), ALU.subtract).then_inc(xl_ready, 1)
            dve.wait_ge(lb_in, 32)
            dve.wait_ge(c_in, 16 * 3)
            r0, r1 = lbrow[0:HEADS, 0, :], lbrow[0:HEADS, 1, :]
            top = es[0:HEADS, 0, 0:P]
            link(nc.vector.tensor_tensor(top, r0, r1, ALU.max))
            nc.vector.tensor_tensor(r0, r0, top, ALU.subtract).then_inc(lb_rows, 1)
            nc.vector.tensor_tensor(r1, r1, top, ALU.subtract).then_inc(lb_rows, 1)
            for g in range(4):
                xl(g)
            dve.wait_ge(lb_e, 1)
            link(nc.vector.tensor_tensor(r1, r0, r1, ALU.add))
            link(nc.vector.reciprocal(r1, r1))
            link(nc.vector.tensor_tensor(r0, r0, r1, ALU.mult))
            nc.vector.tensor_scalar(r1, r0, -0.5, 0.5, ALU.mult, ALU.add).then_inc(lb_s, 1)
            nc.vector.tensor_scalar(r0, r0, 0.5, 0.5, ALU.mult, ALU.add).then_inc(lb_s, 1)
            nc.vector.tensor_scalar(hnorm[:, :], hnorm[:, :], 0.5, None, ALU.mult).then_inc(lb_s, 1)
            dve.wait_ge(lb_s, 3)
            dve.wait_ge(lb_done, 1)
            dve.wait_ge(c_in, 16 * 3)

            att_mask = cst[:, K_ATT:K_ATT + 3 * P]
            lev_mask = cst[:, K_LEV:K_LEV + 8 * P].rearrange("p (l t) -> p l t", l=8)
            def head(i):
                dve.wait_ge(staged, i * 5 + 5)
                dve.wait_ge(score_ready, i + 1 + ONE)
                for h in range(2):
                    link(nc.vector.tensor_tensor(prob[:, h, :], four[:, h, 0:3 * P], att_mask, ALU.add))
                link(nc.vector.tensor_reduce(mx[:, 0, :], prob[:, :, 0:P], AX.X, ALU.max))
                link(nc.vector.tensor_reduce(mx[:, 1, :], prob[:, :, P:3 * P], AX.X, ALU.max))
                link(nc.vector.tensor_tensor(mx, mx, sk, ALU.max))
                link(nc.vector.tensor_tensor(esink, sk, mx, ALU.subtract))
                nc.vector.tensor_scalar(mneg, mx, -1.0, None, ALU.mult).then_inc(max_ready, 1)
                dve.wait_ge(exp_done, i * 5 + 5)
                link(nc.vector.tensor_tensor(rden, psums, esink, ALU.add))
                link(nc.vector.reciprocal(rden, rden))
                for h in range(2):
                    nc.vector.tensor_scalar(prob[:, h, 0:P], prob[:, h, 0:P], rden[:, 0, h:h + 1], None, ALU.mult)\
                        .then_inc(prob_ready, 1)
                    nc.vector.tensor_scalar(prob[:, h, P:3 * P], prob[:, h, P:3 * P], rden[:, 1, h:h + 1], None, ALU.mult)\
                        .then_inc(prob_ready, 1)
                dve.wait_ge(es_ready, i * 2 + 2)
                dve.wait_ge(pair0_act, i + 2)
                link(nc.vector.scalar_tensor_tensor(orow, es[:, :, 2 * HW:3 * HW], 1.0, pair[0][:, :, 3 * HW:4 * HW], ALU.add, ALU.mult))
                nc.vector.scalar_tensor_tensor(qrow, es[:, :, 0:HW], 1.0, pair[0][:, :, 0:HW], ALU.add, ALU.mult).then_inc(hg_rows, 1)
                nc.vector.tensor_tensor(orow, orow, bc(hnorm[:, :].unsqueeze(1), [P, TB, HW]), ALU.mult).then_inc(pair0_dve, 1)
                settle(dve, c_in)
                link(nc.vector.tensor_copy(lbs, lbT[:, :, bass.ds(i, 1)].rearrange("p a o -> p (a o)")))
                dve.wait_ge(qT_copied, i + 1)
                link(nc.vector.tensor_scalar(fT, bank_t[:, T:2 * T], lbs[:, 1:2], lbs[:, 0:1], ALU.mult, ALU.add))
                link(nc.vector.scalar_tensor_tensor(qp, bank_t[:, 0:T], Q_SCALE, fT, ALU.mult, ALU.mult))
                nc.vector.tensor_scalar(kq, fT, -1.0, 1.0, ALU.mult, ALU.add).then_inc(level_ops, 1)
                totals = fT
                off = 0
                for lv in range(1, LEVELS + 1):
                    size = 1 << (lv - 1)
                    blocks = T // size
                    pairs = totals.rearrange("p (n a) -> p n a", a=2)
                    q_odd = qp.rearrange("p (n a s) -> p n a s", a=2, s=size)[:, :, 1, :]
                    k_even = kq.rearrange("p (n a s) -> p n a s", a=2, s=size)[:, :, 0, :]
                    dve.wait_ge(level_mm, i * 9 + (lv + 1) + ONE)
                    if lv == 1:
                        dve.wait_ge(level_ops, i * 8 + 1)
                    link(nc.vector.tensor_tensor(q_odd, q_odd, bc(pairs[:, :, 0:1], [P, blocks // 2, size]), ALU.mult))
                    if lv < LEVELS:
                        nxt = tot[:, off:off + blocks // 2]
                        link(nc.vector.tensor_tensor(nxt, pairs[:, :, 0], pairs[:, :, 1], ALU.mult))
                        off += blocks // 2
                    nc.vector.tensor_tensor(k_even, k_even, bc(pairs[:, :, 1:2], [P, blocks // 2, size]), ALU.mult)\
                        .then_inc(level_ops, 1)
                    totals = nxt
                    dve.wait_ge(level_ops, i * 8 + (lv + 1))
                for half in range(2):
                    dst = lev[:, 4 * half:4 * half + 4, :].rearrange("p l (b t) -> p l b t", b=TB)
                    src = levp[:, 4 * half:4 * half + 4, :].rearrange("p l (b t) -> p l b t", b=TB)
                    for b in range(TB):
                        ins = nc.vector.tensor_tensor(dst[:, :, b, :], src[:, :, b, :],
                                                      lev_mask[:, 4 * half:4 * half + 4, :], ALU.mult)
                        if b == TB - 1:
                            ins.then_inc(lev_read, 1)
                        else:
                            link(ins)
                dve.wait_ge(lev_read, i * 2 + 2 + ONE)
                nc.vector.tensor_reduce(hatt, lev.rearrange("p l t -> p t l"), AX.X, ALU.add).then_inc(hatt_ready, 1)
                dve.wait_ge(ho_sq, i * 2 + 2)
                rstd(stat[:, 4:6])
                for b in range(TB):
                    nc.vector.scalar_tensor_tensor(oh[:, b, :], bank_o[:, b * HW:(b + 1) * HW], stat[:, 4 + b:5 + b],
                                                   orow[:, b, :], ALU.mult, ALU.mult).then_inc(oh_ready, 1)
            with dve.Fori(0, HEADS) as i:
                chain.enter(i, 41)
                head(i)
            chain.leave(HEADS)
            for g in range(4):
                dve.wait_ge(o_hi_ready, g + 1)
                nc.vector.tensor_tensor(act_lo[:, 4 * g:4 * g + 4, :], oT[:, 4 * g:4 * g + 4, :],
                                        act_hi[:, 4 * g:4 * g + 4, :].bitcast(F32), ALU.subtract).then_inc(o_lo_ready, 1)

            def m_split_lo(c):
                dve.wait_ge(mT_done, c + 1 + ONE)
                for b in range(TB):
                    t = slice(b * P, (b + 1) * P)
                    nc.vector.scalar_tensor_tensor(m_lo[:, b, bass.ds(c * CH + D, CH)].rearrange("p (k t) -> p k t", t=P),
                                                   levp[:, 0:4, t], 0.5, m_hi[:, bass.ds(c * 4, 4), t].bitcast(F32),
                                                   ALU.mult, ALU.subtract).then_inc(m_lo_ready, 1)

            def merge_chunk(c, first):
                if not first:
                    m_split_lo(c - 1)
                for a, m in enumerate((merged, merged2)):
                    dve.wait_ge(unit_used, c * CU + (N_UNITS + CU // 2 * (a + 1)))
                    nc.vector.scalar_tensor_tensor(m, gates[:, :, bass.ds(c * CH + a * D, CH)], 1.0, pair[a][:, :, :],
                                                   ALU.add, ALU.mult).then_inc(y_read, 1)
                dve.wait_ge(y_read, c * 2 + 2 + ONE)
                nc.vector.tensor_tensor(merged, merged, merged2, ALU.add).then_inc(merged_ready, 1)
            dve.wait_ge(pair1_act, HEADS + 2)
            merge_chunk(0, True)
            with dve.Fori(1, NC) as c:
                merge_chunk(c, False)
            m_split_lo(NC - 1)
            dve.wait_ge(g2_in, 16)
            for b in range(TB):
                dve.wait_ge(x_in[b], 32)
            for c in range(NC):
                dve.wait_ge(unit_used, N_WO + CU * (c + 1))
                h_c = resid[:, :, c * CH:(c + 1) * CH]
                nc.vector.tensor_tensor(h_c, h_c, pair[c % 2][:, :, :], ALU.add).then_inc(h_added, 1)
                dve.wait_ge(h_added, c + 1 + ONE)
                nc.vector.tensor_tensor(hn[:, :, c * CH:(c + 1) * CH], h_c,
                                        bc(norm_g[:, c * CH:(c + 1) * CH].unsqueeze(1), [P, TB, CH]), ALU.mult)\
                    .then_inc(hg_ready, 1)
            dve.wait_ge(act_step, NC * TB)
            link(nc.vector.tensor_reduce(stat[:, 8:10], msq, AX.X, ALU.add))
            rstd(stat[:, 8:10])
            link(nc.vector.tensor_scalar(half_rstd, stat[:, 8:10], 0.5, None, ALU.mult))
            dve.wait_ge(tp_ready, 8)
            for b in range(TB):
                nc.vector.tensor_scalar(hn[:, b, :], hn[:, b, :], stat[:, 8 + b:9 + b], None, ALU.mult).then_inc(xn_ready, 1)

            off = [NR]

            def rw(*shape):
                n = 1
                for s in shape:
                    n *= s
                ap = rwork[:, off[0]:off[0] + n]
                off[0] += n
                return ap.rearrange("p (a b) -> p a b", a=shape[0]) if len(shape) == 2 else ap
            lg = rw(TB, NR)
            oneg = rw(TB, NG)
            me = rw(TB, NE)
            oh1 = rw(TB, NE)
            oh2 = rw(TB, NE)
            t32 = rw(TB, NE)
            t4 = rw(TB, NG)
            m_g, i_g, m_1, i_1, m_2, i_2, psel, w_1, w_2, s1 = (rw(TB, 1) for _ in range(10))
            iota = cst[:, K_IOTA:K_IOTA + NE]
            dve.wait_ge(logit_ready, 1)
            for b in range(TB):
                nc.vector.scalar_tensor_tensor(lg[:, b, :], pair[0][:, b, 0:NR], stat[:, 8 + b:9 + b], br, ALU.mult, ALU.add)\
                    .then_inc(logit_read, 1)
            dve.wait_ge(logit_read, 2)

            def first_max(v, m, idx, onehot, tmp, n):
                it = bc(iota[:, 0:n].unsqueeze(1), [P, TB, n])
                link(nc.vector.tensor_reduce(m, v, AX.X, ALU.max))
                link(nc.vector.tensor_tensor(tmp, v, bc(m, [P, TB, n]), ALU.is_lt))
                link(nc.vector.scalar_tensor_tensor(tmp, tmp, 1000.0, it, ALU.mult, ALU.add))
                link(nc.vector.tensor_reduce(idx, tmp, AX.X, ALU.min))
                link(nc.vector.tensor_tensor(onehot, it, bc(idx, [P, TB, n]), ALU.is_equal))

            lgg = lg[:, :, 0:NG]
            first_max(lgg, m_g, i_g, oneg, t4, NG)
            ex = small[:, 0:TB * NG].rearrange("p (b g) -> p b g", b=TB)
            link(nc.vector.tensor_tensor(ex, lgg, bc(m_g, [P, TB, NG]), ALU.subtract))
            for b in range(TB):
                gm = bc(oneg[:, b, :].unsqueeze(2), [P, NG, EG])
                me_b = me[:, b, :].rearrange("p (g e) -> p g e", g=NG)
                link(nc.vector.tensor_tensor(me_b, lg[:, b, NG:NR].rearrange("p (g e) -> p g e", g=NG), gm, ALU.mult))
                link(nc.vector.tensor_scalar(t32[:, b, :].rearrange("p (g e) -> p g e", g=NG), gm, 1.0, -NEG,
                                             ALU.subtract, ALU.mult))
            link(nc.vector.tensor_tensor(me, me, t32, ALU.add))
            first_max(me, m_1, i_1, oh1, t32, NE)
            link(nc.vector.scalar_tensor_tensor(me, oh1, 4 * NEG, me, ALU.mult, ALU.add))
            first_max(me, m_2, i_2, oh2, t32, NE)
            d12 = small[:, 8:10].rearrange("p (b o) -> p b o", b=TB)
            nc.vector.tensor_tensor(d12, m_2, m_1, ALU.subtract).then_inc(r_exp_in, 1)
            dve.wait_ge(r_exp, 1)
            link(nc.vector.tensor_reduce(psel, ex, AX.X, ALU.add))
            link(nc.vector.tensor_scalar(s1, d12, 1.0, None, ALU.add))
            link(nc.vector.tensor_tensor(s1, s1, psel, ALU.mult))
            link(nc.vector.reciprocal(w_1, s1))
            link(nc.vector.tensor_tensor(w_2, w_1, d12, ALU.mult))
            nc.vector.tensor_tensor(rmask, oh1, oh2, ALU.add).then_inc(mask_ready, 1)
            link(nc.vector.tensor_tensor(oh1, oh1, bc(w_1, [P, TB, NE]), ALU.mult))
            link(nc.vector.tensor_tensor(oh2, oh2, bc(w_2, [P, TB, NE]), ALU.mult))
            link(nc.vector.tensor_tensor(coef, oh1, oh2, ALU.add))
            dve.wait_ge(rank_ready, 1)
            dve.wait_ge(mask_ready, 1)
            rank = pair[1][:, 0, 0:3 * NE].rearrange("p (b e) -> p b e", b=3)
            link(nc.vector.tensor_scalar(late, rank[:, 0:TB, :], CAP - 0.5, BIG, ALU.is_gt, ALU.mult))
            link(nc.vector.tensor_scalar(place, rmask, -BIG, BIG, ALU.mult, ALU.add))
            link(nc.vector.tensor_tensor(place, place, late, ALU.add))
            link(nc.vector.tensor_tensor(place, place, rank[:, 0:TB, :], ALU.add))
            link(nc.vector.scalar_tensor_tensor(ocoef, late, 1.0 / BIG, coef, ALU.mult, ALU.mult))
            over, upto, idx = lrow[0:1, 0:NE], lrow[0:1, NE:2 * NE], lrow[0:1, 2 * NE:2 * NE + LIST + 1]
            link(nc.vector.tensor_scalar(over, rank[0:1, 2, :], CAP + 0.5, None, ALU.is_gt))
            link(nc.vector.tensor_tensor_scan(upto, cst[0:1, K_ONE:K_ONE + NE], over, 0.0, ALU.mult, ALU.add))
            link(nc.vector.tensor_tensor(llist, bc(cst[0:1, K_IOTA + 1:K_IOTA + 1 + LIST].unsqueeze(2), [1, LIST, NE]),
                                         bc(upto.unsqueeze(1), [1, LIST, NE]), ALU.is_equal))
            link(nc.vector.tensor_tensor(over, over, iota[0:1, :], ALU.mult))
            link(nc.vector.tensor_tensor(llist, llist, bc(over.unsqueeze(1), [1, LIST, NE]), ALU.mult))
            link(nc.vector.tensor_reduce(idx[:, 0:LIST], llist, AX.X, ALU.add))
            link(nc.vector.tensor_copy(idx[:, LIST:LIST + 1], upto[:, NE - 1:NE]))
            nc.vector.tensor_copy(over_i[0:1, :], idx).then_inc(over_ready, 1)
            nc.vector.tensor_copy(lrow[0:1, 0:1], rank[0:1, 2, 0:1]).then_inc(rank_read, 1)
            it4 = bc(iota.unsqueeze(1), [P, GX, SL])
            with dve.Fori(0, GROUPS) as g:
                chain.enter(g, GX)
                dve.wait_ge(gathered, g * 2 + ONE)
                dve.wait_ge(swT_ready, g + ONE)
                dve.wait_ge(rank_read, 1)
                for b in range(TB):
                    pl = place[:, b, bass.ts(g, GX)]
                    nc.vector.tensor_tensor(gh[:, b, :].rearrange("p (q s) -> p q s", q=GX), it4,
                                            bc(pl.unsqueeze(2), [P, GX, SL]), ALU.is_equal).then_inc(onehot_ready, 1)
                dve.wait_ge(onehot_ready, g * 2 + 2)
                for b in range(TB):
                    cf = coef[:, b, bass.ts(g, GX)]
                    nc.vector.tensor_tensor(sw[:, b, :].rearrange("p (q s) -> p q s", q=GX),
                                            gh[:, b, :].rearrange("p (q s) -> p q s", q=GX),
                                            bc(cf.unsqueeze(2), [P, GX, SL]), ALU.mult).then_inc(sw_ready, 1)
                for q in range(GX):
                    hp = pair[0][:, q % 2, :]
                    yp = pair[1][:, q % 2, :]
                    dve.wait_ge(ge_exp, g * GX + (q + 1))
                    dve.wait_ge(ghT_ready, g * GX + q + ONE)
                    link(nc.vector.scalar_tensor_tensor(ghid, geh, 1.0, hp[:, 0:P], ALU.add, ALU.mult))
                    nc.vector.tensor_tensor(ghid, ghid, hp[:, P:2 * P], ALU.mult).then_inc(ghid_ready, 1)
                    dve.wait_ge(quarter_used, g * (4 * GX) + (4 * q + 4))
                    for c in (2, 3):
                        nc.vector.tensor_copy(yg[q * SL:(q + 1) * SL, c * CH:(c + 1) * CH], yp[c * SL:(c + 1) * SL, :])\
                            .then_inc(yg_dve, 1)
                for b in range(TB):
                    for c in range(NC):
                        dve.wait_ge(back_ready, g * (2 * NC) + (b * NC + c + 1))
                        h_c = resid[:, b, c * CH:(c + 1) * CH]
                        nc.vector.tensor_tensor(h_c, h_c, four[:, c, :], ALU.add).then_inc(scattered, 1)
            chain.leave(GROUPS)
            dve.wait_ge(scattered, GROUPS * 2 * NC + ONE)
            dve.wait_ge(over_ready, 1)
            n_over = dve.value_load(over_i[0:1, LIST:LIST + 1], min_val=0, max_val=LIST)
            with dve.If(n_over > 0):
                with dve.Fori(0, n_over) as e:
                    ex_e = dve.value_load(over_i[0:1, bass.ds(e, 1)], min_val=0, max_val=NE - 1)
                    chain_o = Chain(dve, over_step)
                    chain_o.enter(e, 2 * 2 + 1)
                    dve.wait_ge(y_added, e * 2 * NC + ONE)
                    chain_o.link(nc.vector.tensor_scalar(small[:, 16:18].rearrange("p (b o) -> p b o", b=TB),
                                                         ocoef[:, :, bass.ds(ex_e, 1)], 1.0, None, ALU.mult))
                    for b in range(TB):
                        dve.wait_ge(e_exp, e * 2 + (b + 1))
                        dve.wait_ge(hidT_ready, e * 2 + b + ONE)
                        chain_o.link(nc.vector.tensor_scalar(ehid[:, b, :], ehid[:, b, :], 1.0, stat[:, 8 + b:9 + b], ALU.add, ALU.mult))
                        chain_o.link(nc.vector.tensor_tensor(hid[:, b, :], ehid[:, b, :], pair[b][:, 0, :], ALU.mult))
                        nc.vector.scalar_tensor_tensor(hid[:, b, :], pair[b][:, 1, :], half_rstd[:, b:b + 1], hid[:, b, :],
                                                       ALU.mult, ALU.mult).then_inc(hid_ready, 1)
                    for b in range(TB):
                        for c in range(NC):
                            dve.wait_ge(oy_ready, e * 8 + (b * 4 + c + 1) + ONE)
                            h_c = resid[:, b, c * CH:(c + 1) * CH]
                            nc.vector.scalar_tensor_tensor(h_c, four[:, c, :], small[:, 16 + b:17 + b], h_c,
                                                           ALU.mult, ALU.add).then_inc(y_added, 1)
            nc.vector.tensor_copy(small[:, 20:21], small[:, 0:1]).then_inc(resid_done, 1)
            dve.wait_ge(resid_done, 1)
            link(mean_square_dve(1, gates[:, 1, 0:D], resid[:, 1, :], 12))
            dve.wait_ge(ms_done, 2)
            dve.wait_ge(g3_in, 16)
            rstd(stat[:, 12:14])
            for b in range(TB):
                nc.vector.scalar_tensor_tensor(resid[:, b, :], resid[:, b, :], stat[:, 12 + b:13 + b], norm_g[:, :],
                                               ALU.mult, ALU.mult).then_inc(o_ready, 1)


_INS = ["x", "w_in", "attn_sinks", "hgrn_lb_logits", "hgrn_norm_g", "w_br_attn", "w_br_hgrn", "w_out",
        "mix_norm_g", "moe_norm_g", "w_router_group", "b_router_group", "w_router_expert",
        "b_router_expert", "w1", "w3", "w2", "final_norm_g"]


def kernel(**inputs):
    import numpy as np
    import concourse.bacc as bacc
    from concourse.bass_utils import run_bass_kernel_spmd as run

    nc = bacc.Bacc("TRN2", target_bir_lowering=False, num_devices=1)
    arrays, args = {}, []
    for name in _INS + ["consts"]:
        a = constants() if name == "consts" else np.ascontiguousarray(inputs[name])
        arrays[f"in_{name}"] = a
        args.append(nc.dram_tensor(f"in_{name}", a.shape, mybir.dt.from_np(a.dtype), kind="ExternalInput").ap())
    res = nc.dram_tensor("result", (1, T, D), F32, kind="ExternalOutput").ap()
    hybrid_block(nc, *args, res)
    r = run(nc, [arrays], core_ids=[0])
    return r.results[0]["result"]
```

```python
from contextlib import ExitStack

import concourse.bass as bass
from concourse import mybir

F32 = mybir.dt.float32
F32R = mybir.dt.float32r
I32 = mybir.dt.int32
ALU = mybir.AluOpType
ACT = mybir.ActivationFunctionType
AX = mybir.AxisListType

P = 128
D = 2048
T = 256
TB = T // P
KD = D // P
CH = 512
KS = 8
KU = 4
UNITS = 4
NC = D // CH
HEADS = 8
DH = 64
HW = 128
LEVELS = 7
HB = P // 2
W_ATT = 1024
KV = 256
C_HGRN = W_ATT + 2 * KV
C_GATE = C_HGRN + 4 * W_ATT
EPS = 1e-6
ONE = 1
Q_SCALE = 0.5 * HW ** -0.5
NEG = -1e30
NG = 4
EG = 8
NE = NG * EG
NR = NG + NE
FE = 512
SL = 32
CAP = SL
GX = P // SL
GROUPS = NE // GX
LIST = 16
BIG = 1000.0

K_ID = 0
K_LEV = P
K_TOP = K_LEV + LEVELS * HB
K_ATT = K_TOP + P
K_TRI = K_ATT + 3 * P
K_IOTA = K_TRI + P
K_ONE = K_IOTA + 2 * P
K_EPS = K_ONE + P
K_END = K_EPS + 8


def constants():
    import numpy as np
    s = np.arange(P)[:, None]
    t = np.arange(P)[None, :]
    out = np.zeros((P, K_END), np.float32)
    for lev in range(LEVELS):
        ss, tt = s % HB, t[:, 0:HB]
        if lev == 0:
            m = ss == tt
        else:
            half = 1 << (lev - 1)
            m = (ss >> lev == tt >> lev) & (ss & half == 0) & (tt & half != 0)
        out[:, K_LEV + lev * HB:K_LEV + (lev + 1) * HB] = m
    out[:, K_TOP:K_TOP + P] = (s < HB) & (t >= HB)
    causal = np.where(t <= s, 0.0, NEG)
    out[:, K_ATT:K_ATT + P] = causal
    out[:, K_ATT + P:K_ATT + 2 * P] = np.where(t > s, 0.0, NEG)
    out[:, K_ATT + 2 * P:K_ATT + 3 * P] = causal
    out[:, K_ID:K_ID + P] = s == t
    out[:, K_TRI:K_TRI + P] = s < t
    out[:, K_IOTA:K_IOTA + 2 * P] = np.arange(2 * P)[None, :]
    out[:, K_ONE:K_ONE + P] = 1.0
    out[:, K_EPS] = EPS
    return out


class Chain:

    def __init__(self, eng, sem):
        self.eng, self.sem, self.base, self.n = eng, sem, 0, 0

    def link(self, ins):
        self.n += 1
        ins.then_inc(self.sem, 1)
        self.eng.wait_ge(self.sem, self.base + self.n)

    def enter(self, i, per):
        self.start = self.base + self.n
        self.base, self.n, self.per = self.start + i * per, 0, per

    def leave(self, times):
        assert self.n == self.per, (self.n, self.per)
        self.base, self.n = self.start + times * self.per, 0


def settle(eng, sem):
    eng.wait_ge(sem, 16 * 3)


def bc(ap, shape):
    return ap.broadcast_to(shape)


def hybrid_block(nc, x, w_in, attn_sinks, hgrn_lb_logits, hgrn_norm_g, w_br_attn, w_br_hgrn, w_out,
                 mix_norm_g, moe_norm_g, w_router_group, b_router_group, w_router_expert,
                 b_router_expert, w1, w3, w2, final_norm_g, consts, out):
    ctx = ExitStack()
    with ctx:
        def sb(name, shape, dt=F32):
            return ctx.enter_context(nc.sbuf_tensor(name, shape, dt))

        def ps(name, shape):
            return ctx.enter_context(nc.psum_tensor(name, shape, F32))

        def sem(name):
            return ctx.enter_context(nc.semaphore(name))

        def another_name(name, shape, offset):
            return nc.alloc_sbuf_tensor_at(name, shape, F32R, offset=offset)

        w_at = -(-nc.sbuf_base // 32) * 32
        wslot = sb("wslot", [P, 6, KS * CH])
        act_at = w_at + 6 * KS * CH * 4
        actT = sb("actT", [P, KD, T])
        resid_at = act_at + KD * T * 4
        resid = sb("resid", [P, TB, D])
        assert nc.sbuf_base == resid_at + TB * D * 4 and nc.sbuf_base % 32 == 0
        unit_bytes = KU * CH * 4
        w_lo = another_name("w_lo", [P, UNITS, KU, CH], w_at)
        w_hi = another_name("w_hi", [P, UNITS, KU, CH], w_at + UNITS * unit_bytes)
        act_hi = another_name("act_hi", [P, KD, T], act_at)
        act_lo = another_name("act_lo", [P, KD, T], resid_at)
        w_raw = wslot[:, 0:2, :].rearrange("p a n -> p (a n)").rearrange("p (u k n) -> p u k n", u=UNITS, k=KU)
        gates_at = nc.sbuf_base
        gates = sb("gates", [P, TB, 2 * D])
        m_lo = another_name("m_lo", [P, TB, 2 * D], gates_at)
        norm_g = sb("norm_g", [P, D])
        qa = sb("qa", [P, TB, W_ATT])
        kv = sb("kv", [P, TB, 2 * KV])
        o_at = nc.sbuf_base
        oT = sb("oT", [P, KD, T])
        m_hi = another_name("m_hi", [P, KD, T], o_at)
        oaT, ohT = oT[:, 0:HEADS, :], oT[:, HEADS:KD, :]
        hT = actT
        cst = sb("cst", [P, K_END])
        sinks = sb("sinks", [P, 2 * HEADS])
        hnorm = sb("hnorm", [P, HW])
        lbT = sb("lbT", [P, 2, HEADS])
        stat = sb("stat", [P, 32])
        small = sb("small", [P, 64])
        msq = small[:, 24:24 + TB * NC].rearrange("p (b c) -> p b c", b=TB)
        half_rstd = small[:, 32:32 + TB]
        nwt = small[:, 40:40 + 2 * TB]
        over_i = sb("over_i", [P, LIST + 1], mybir.dt.int32)
        ident = cst[:, K_ID:K_ID + P]

        work = wslot[:, 4:6, :].rearrange("p a n -> p (a n)")
        square_scratch = qa[:, 1, 0:CH]
        at = [0]

        def carve(*shape):
            n = 1
            for s in shape:
                n *= s
            ap = work[:, at[0]:at[0] + n]
            at[0] += n
            assert at[0] <= 2 * KS * CH
            if len(shape) == 2:
                return ap.rearrange("p (a b) -> p a b", a=shape[0])
            if len(shape) == 3:
                return ap.rearrange("p (a b c) -> p a b c", a=shape[0], b=shape[1])
            return ap
        qs = carve(TB, P)
        ks = carve(TB, P)
        vs = carve(TB, DH)
        qkT = carve(2, T)
        prob = carve(2, 3 * P)
        probT = carve(2, 3 * P)
        es = carve(TB, 3 * P)
        qrow = carve(TB, HW)
        orow = carve(TB, HW)
        irow = carve(TB, HW)
        qT = carve(T)
        fT = carve(T)
        qp = carve(T)
        kq = carve(T)
        tot = carve(T)
        hatt = carve(T)
        crossT = carve(P)
        oh = carve(TB, HW)
        sk = carve(2, 2)
        lbs = carve(2)
        mx = carve(2, 2)
        mneg = carve(2, 2)
        esink = carve(2, 2)
        psums = carve(2, 2)
        rden = carve(2, 2)
        lbrow = carve(2, P)
        lev = norm_g[:, 0:LEVELS * P].rearrange("p (l t) -> p l t", l=LEVELS)
        diag = norm_g[:, LEVELS * P:(LEVELS + 1) * P].rearrange("p (b t) -> p b t", b=TB)
        merged = norm_g[:, 0:TB * CH].rearrange("p (b n) -> p b n", b=TB)
        merged2 = norm_g[:, TB * CH:2 * TB * CH].rearrange("p (b n) -> p b n", b=TB)

        pair = [ps("pair0", [P, TB, CH]), ps("pair1", [P, TB, CH])]
        four = ps("four", [P, 4, CH])
        flat4 = four[:, :, :].rearrange("p a n -> p (a n)")
        levp = flat4.rearrange("p (l t) -> p l t", l=8)
        levh = flat4[:, 0:LEVELS * P].rearrange("p (l t) -> p l t", l=LEVELS)
        bank_t = four[:, 2, :]
        bank_o = four[:, 3, :]

        x_in = [sem(f"x_in{b}") for b in range(TB)]
        ms_done = sem("ms_done")
        hg_ready = sem("hg_ready")
        g_in = sem("g_in")
        c_in = sem("c_in")
        id_in = sem("id_in")
        loaded = [sem(f"loaded{s}") for s in range(6)]
        o_hi_ready = sem("o_hi_ready")
        o_lo_ready = sem("o_lo_ready")
        m_lo_ready = sem("m_lo_ready")
        unit_in = [sem(f"unit_in{u}") for u in range(UNITS)]
        hi_ready = sem("hi_ready")
        lo_pool = sem("lo_pool")
        lo_dve = sem("lo_dve")
        xl_ready = sem("xl_ready")
        unit_used = sem("unit_used")
        dve_step = sem("dve_step")
        act_step = sem("act_step")
        xn_ready = sem("xn_ready")
        tp_ready = sem("tp_ready")
        tp_copied = sem("tp_copied")
        lb_in = sem("lb_in")
        lb_rows = sem("lb_rows")
        lb_e = sem("lb_e")
        lb_s = sem("lb_s")
        lb_t = sem("lb_t")
        lb_done = sem("lb_done")
        pair0_act = sem("pair0_act")
        pair1_act = sem("pair1_act")
        pair0_dve = sem("pair0_dve")
        staged = sem("staged")
        qkT_ready = sem("qkT_ready")
        qkT_copied = sem("qkT_copied")
        score_ready = sem("score_ready")
        max_ready = sem("max_ready")
        exp_done = sem("exp_done")
        prob_ready = sem("prob_ready")
        probT_ready = sem("probT_ready")
        probT_copied = sem("probT_copied")
        oT_ready = sem("oT_ready")
        oaT_done = sem("oaT_done")
        es_ready = sem("es_ready")
        hg_rows = sem("hg_rows")
        qfT_ready = sem("qfT_ready")
        qT_copied = sem("qT_copied")
        level_ops = sem("level_ops")
        level_mm = sem("level_mm")
        lev_read = sem("lev_read")
        cross_copied = sem("cross_copied")
        hatt_ready = sem("hatt_ready")
        ho_ready = sem("ho_ready")
        ho_sq = sem("ho_sq")
        oh_ready = sem("oh_ready")
        ohT_ready = sem("ohT_ready")
        ohT_done = sem("ohT_done")
        y_read = sem("y_read")
        merged_ready = sem("merged_ready")
        mT_ready = sem("mT_ready")
        mT_done = sem("mT_done")
        h_added = sem("h_added")
        g2_in = sem("g2_in")
        g3_in = sem("g3_in")
        r_in = sem("r_in")
        lgT_ready = sem("lgT_ready")
        lgT_copied = sem("lgT_copied")
        logit_ready = sem("logit_ready")
        logit_read = sem("logit_read")
        r_exp_in = sem("r_exp_in")
        r_exp = sem("r_exp")
        gathered = sem("gathered")
        xg_copied = sem("xg_copied")
        swT_ready = sem("swT_ready")
        swT_copied = sem("swT_copied")
        onehot_ready = sem("onehot_ready")
        sw_ready = sem("sw_ready")
        ghid_ready = sem("ghid_ready")
        ge_exp = sem("ge_exp")
        ghT_ready = sem("ghT_ready")
        ghT_copied = sem("ghT_copied")
        yg_act = sem("yg_act")
        yg_dve = sem("yg_dve")
        back_ready = sem("back_ready")
        scattered = sem("scattered")
        quarter_used = sem("quarter_used")
        mask_ready = sem("mask_ready")
        rank_ready = sem("rank_ready")
        rank_read = sem("rank_read")
        over_ready = sem("over_ready")
        over_step = sem("over_step")
        oh13_ready = sem("oh13_ready")
        oy_ready = sem("oy_ready")
        resid_done = sem("resid_done")
        e_exp = sem("e_exp")
        hid_ready = sem("hid_ready")
        hidT_ready = sem("hidT_ready")
        hidT_copied = sem("hidT_copied")
        y_added = sem("y_added")
        o_ready = sem("o_ready")
        stored = sem("stored")

        hn = gates[:, :, 0:D]
        hid = gates[:, :, D:D + FE]
        ehid = gates[:, :, D + FE:D + 2 * FE]
        xg = gates[:, 0, D:2 * D].rearrange("p (k n) -> p k n", k=KD)
        yg = gates[:, 1, D:2 * D]
        gwork = oT[:, KS:KD, :].rearrange("p a n -> p (a n)")
        gh = gwork[:, 0:T].rearrange("p (b n) -> p b n", b=TB)
        sw = gwork[:, T:2 * T].rearrange("p (b n) -> p b n", b=TB)
        swT = gwork[:, 2 * T:3 * T]
        geh = gwork[:, 3 * T:3 * T + P]
        ghid = gwork[:, 3 * T + P:4 * T]
        ghT = gwork[:, 4 * T:4 * T + P]
        hidT = gates[:, :, D + 2 * FE:D + 4 * FE].rearrange("p b (k t) -> p b k t", k=4)[:, :, :, 0:P]
        wr = qa[:, :, :].rearrange("p a n -> p (a n)")[:, 0:KD * NR].rearrange("p (k n) -> p k n", k=KD)
        br = kv[:, 0, 0:NR]
        lgT = qa[0:NR, 1, CH:CH + T]
        rwork = kv[:, :, :].rearrange("p a n -> p (a n)")
        coef = oT[:, 0, 0:TB * NE].rearrange("p (b e) -> p b e", b=TB)
        rmask = oT[:, 1, 0:TB * NE].rearrange("p (b e) -> p b e", b=TB)
        place = oT[:, 2, 0:TB * NE].rearrange("p (b e) -> p b e", b=TB)
        late = oT[:, 3, 0:TB * NE].rearrange("p (b e) -> p b e", b=TB)
        ocoef = oT[:, 4, 0:TB * NE].rearrange("p (b e) -> p b e", b=TB)
        lrow = oT[:, 5, 0:2 * NE + LIST + 1]
        llist = oT[0:1, 6:8, :].rearrange("p a n -> p (a n)").rearrange("p (j e) -> p j e", j=LIST)

        w_in_k = w_in[0].rearrange("(k p) n -> p k n", p=P)
        w_gather = w_in[0][:, C_HGRN:C_GATE].rearrange("(k p) (j c) -> p k j c", p=P, j=4)
        wa_k = w_br_attn[0].rearrange("(k p) n -> p k n", p=P)
        wh_k = w_br_hgrn[0].rearrange("(k p) n -> p k n", p=P)
        wo_k = w_out[0].rearrange("(k p) n -> p k n", p=P)
        w1_k = w1[0].rearrange("e (k p) f -> e p k f", p=P)
        w3_k = w3[0].rearrange("e (k p) f -> e p k f", p=P)
        w2_k = w2[0].rearrange("e (k p) n -> e p k n", p=P)

        def slot(s):
            return wslot[:, s, :].rearrange("p (k n) -> p k n", k=KS)

        def slot_w2(s):
            return wslot[:, s, :].rearrange("p (k n) -> p k n", k=2)

        PRO = 3
        CU = KD // KU
        N_PRO = PRO * CU
        HU = 2 * CU
        N_UNITS = N_PRO + HEADS * HU
        HU_IN = 16 * KU + 16
        N_WO = N_UNITS + NC * CU
        N_ALL = N_WO + NC * CU

        def unit_loaded(i, u):
            i, u = i + u // HU, u % HU
            return i * HU_IN + (16 * N_PRO // UNITS + (16 * KU if u < CU else HU_IN))

        HEAD_DVE = (4, 5)
        PRO_DVE = N_PRO // 2

        def wait_lo(eng, i, u):
            if u in HEAD_DVE:
                eng.wait_ge(lo_dve, i * 2 + (PRO_DVE + u - HEAD_DVE[0] + 1))
            else:
                eng.wait_ge(lo_pool, i * (HU - 2) + (PRO_DVE + u + 1 - (2 if u > HEAD_DVE[1] else 0)))

        def wait_later_lo(eng, c, u):
            if u < 2:
                eng.wait_ge(lo_pool, c * 2 + (PRO_DVE + HEADS * (HU - 2) + u + 1))
            else:
                eng.wait_ge(lo_dve, c * 2 + (PRO_DVE + HEADS * 2 + u - 1))

        def later_loaded(c, u):
            return c * 16 + (16 * N_PRO // UNITS + HEADS * HU_IN + 16 * (u // CU + 1))

        block = ctx.enter_context(nc.Block())

        @block.sync
        def _(sp):
            for b in range(TB):
                sp.dma_start(resid[:, b, :], x[0, b * P:(b + 1) * P, :]).then_inc(x_in[b], 16)
            sp.dma_start(norm_g[:, :], mix_norm_g[0:1, :].to_broadcast([P, D])).then_inc(g_in, 16)
            sp.dma_start(cst[:, 0:P], consts[:, 0:P]).then_inc(id_in, 16)
            for n in range(N_PRO):
                c, part = divmod(n, CU)
                if n >= UNITS:
                    sp.wait_ge(unit_used, n - UNITS + 1)
                sp.dma_start(w_raw[:, n % UNITS], w_in_k[:, part * KU:(part + 1) * KU, c * CH:(c + 1) * CH])\
                    .then_inc(unit_in[n % UNITS], 16)
                if n == 1:
                    sp.dma_start(cst[:, P:], consts[:, P:]).then_inc(c_in, 16)
            with sp.Fori(0, HEADS) as i:
                for u in range(HU):
                    part = u % CU
                    sp.wait_ge(unit_used, i * HU + (N_PRO + u - UNITS + 1))
                    if u < CU:
                        for k in range(KU):
                            sp.dma_start(w_raw[:, u % UNITS, k].rearrange("p (j c) -> p j c", j=4),
                                         w_gather[:, part * KU + k, :, bass.ts(i, HW)]).then_inc(unit_in[u % UNITS], 16)
                    else:
                        sp.dma_start(w_raw[:, u % UNITS], w_in_k[:, part * KU:(part + 1) * KU, bass.ds(i * CH + C_GATE, CH)])\
                            .then_inc(unit_in[u % UNITS], 16)
            with sp.Fori(0, NC) as c:
                for u in range(CU):
                    sp.wait_ge(unit_used, c * CU + (N_UNITS + u - UNITS + 1))
                    w, part = (wa_k, wh_k)[u // 2], u % 2
                    sp.dma_start(w_raw[:, u % UNITS], w[:, part * KU:(part + 1) * KU, bass.ds(c * CH, CH)])\
                        .then_inc(unit_in[u % UNITS], 16)
            for n in range(NC * CU):
                c, part = divmod(n, CU)
                sp.wait_ge(unit_used, N_WO + n - UNITS + 1)
                sp.dma_start(w_raw[:, n % UNITS], wo_k[:, part * KU:(part + 1) * KU, c * CH:(c + 1) * CH])\
                    .then_inc(unit_in[n % UNITS], 16)
                if n in (CU - 1, CU):
                    b = n - CU + 1
                    sp.dma_start(resid[:, b, :], x[0, b * P:(b + 1) * P, :]).then_inc(x_in[b], 16)

            def load_expert(e, s):
                if s < 4:
                    src = (w1_k, w3_k)[s % 2][bass.ds(e, 1), :, (s // 2) * KS:(s // 2 + 1) * KS, :]
                    dst = slot(s)
                else:
                    src = w2_k[bass.ds(e, 1), :, 2 * (s % 2):2 * (s % 2) + 2, :]
                    dst = slot_w2(s)
                sp.dma_start(dst, src.rearrange("a p k n -> (a p) k n")).then_inc(loaded[s], 16)

            sp.wait_ge(ohT_done, HEADS + ONE)
            for s in (4, 5):
                load_expert(0, s)
            for s in range(4):
                sp.wait_ge(unit_used, N_ALL - (2 if s == 0 else 0))
                load_expert(0, s)
            with sp.Fori(1, NE) as e:
                for s in range(6):
                    sp.wait_ge(quarter_used, e * 4 + ((1, 1, 2, 2, 3, 4)[s] - 4))
                    load_expert(e, s)
            sp.wait_ge(over_ready, 1)
            sp.wait_ge(quarter_used, 4 * NE)
            n_over = sp.value_load(over_i[0:1, LIST:LIST + 1], min_val=0, max_val=LIST)
            with sp.If(n_over > 0):
                with sp.Fori(0, n_over) as j:
                    e = sp.value_load(over_i[0:1, bass.ds(j, 1)], min_val=0, max_val=NE - 1)
                    for s in range(6):
                        if s == 0:
                            sp.wait_ge(oh13_ready, j * TB + ONE)
                        if s == 4:
                            sp.wait_ge(oy_ready, j * 2 * NC + ONE)
                        load_expert(e, s)
            for n in range(2 * TB):
                b, cols = n // 2, slice(n % 2 * (D // 2), (n % 2 + 1) * (D // 2))
                sp.wait_ge(o_ready, n + 1)
                sp.dma_start(out[0, b * P:(b + 1) * P, cols], resid[:, b, cols]).then_inc(stored, 16)
            sp.wait_ge(stored, 16 * 2 * TB)

        @block.gpsimd
        def _(pool):
            def split_lo(n, u):
                pool.wait_ge(hi_ready, n)
                nc.gpsimd.tensor_tensor(w_lo[:, u % UNITS], w_raw[:, u % UNITS], w_hi[:, u % UNITS].bitcast(F32), ALU.subtract)\
                    .then_inc(lo_pool, 1)

            def stage_qk(i):
                nc.gpsimd.tensor_copy(qs, qa[:, :, bass.ts(i, P)]).then_inc(staged, 1)
                k_cols = kv[:, :, bass.ds((i // 2) * DH, DH)]
                nc.gpsimd.tensor_copy(ks[:, :, 0:DH], k_cols).then_inc(staged, 1)
                nc.gpsimd.tensor_copy(ks[:, :, DH:P], k_cols).then_inc(staged, 1)

            def stage_v(i):
                nc.gpsimd.tensor_copy(vs, kv[:, :, bass.ds((i // 2) * DH + KV, DH)]).then_inc(staged, 1)

            def stage_sinks(i):
                nc.gpsimd.tensor_copy(sk, bc(sinks[:, bass.ts(i, 2)].unsqueeze(1), [P, 2, 2])).then_inc(staged, 1)

            for n in range(N_PRO + 2):
                if n % 2 == 0 or n >= N_PRO:
                    split_lo(n + 1, n)
            pool.wait_ge(pair0_act, 1)
            pool.wait_ge(pair1_act, 2)
            pool.wait_ge(c_in, 16 * 3)
            pool.wait_ge(lb_done, 1)
            stage_qk(0)
            stage_v(0)
            stage_sinks(0)

            def head(i, last):
                for u in range(2, HU + 2):
                    if u not in HEAD_DVE:
                        split_lo(i * HU + (N_PRO + u + 1), u)
                    if u == 3 and not last:
                        pool.wait_ge(qkT_ready, i + 1 + ONE)
                        settle(pool, c_in)
                        stage_qk(i + 1)
                    if u == 5 and not last:
                        pool.wait_ge(oT_ready, i + 1 + ONE)
                        settle(pool, c_in)
                        stage_v(i + 1)
                        pool.wait_ge(prob_ready, i * 4 + 4 + ONE)
                        settle(pool, c_in)
                        stage_sinks(i + 1)
            with pool.Fori(0, HEADS - 1) as i:
                head(i, False)
            head(HEADS - 1, True)
            with pool.Fori(0, 2 * NC - 1) as c:
                for u in range(CU, CU + 2):
                    split_lo(c * CU + (N_UNITS + u + 1), u)

        @block.scalar
        def _(act):
            for ahead in (ohT_done, cross_copied, mT_done, hidT_copied, ghT_copied, yg_act):
                act.sem_inc(ahead, ONE)
            def h_copy(c):
                act.wait_ge(tp_ready, 4 + c + 1)
                nc.scalar.activation(hT[:, 4 * c:4 * c + 4, :], levp[:, 4 * (c % 2):4 * (c % 2) + 4, :], ACT.Copy)\
                    .then_inc(tp_copied, 1)

            def mean_square(b, dst, src, n, col):
                return nc.scalar.activation(dst, src, ACT.Square, scale=n ** -0.5, accum_out=stat[:, col + b:col + b + 1])

            def split_hi(u, there):
                act.wait_ge(unit_in[u % UNITS], there)
                nc.scalar.activation(w_hi[:, u % UNITS], w_raw[:, u % UNITS], ACT.Copy).then_inc(hi_ready, 1)

            act.dma_start(sinks[:, :], attn_sinks[0:1, :].to_broadcast([P, 2 * HEADS])).then_inc(c_in, 16)
            act.dma_start(hnorm[:, :], hgrn_norm_g[0:1, :].to_broadcast([P, HW])).then_inc(c_in, 16)
            for r in range(2):
                act.dma_start(lbrow[0:HEADS, r, :], hgrn_lb_logits[r].rearrange("(h c) -> h c", h=HEADS))\
                    .then_inc(lb_in, 16)
            act.wait_ge(x_in[0], 16)
            mean_square(0, actT[:, 0:KS, :].rearrange("p a b -> p (a b)"), resid[:, 0, :], D, 0).then_inc(ms_done, 1)
            split_hi(0, 16)
            for g in range(4):
                if g == 2:
                    split_hi(1, 16)
                act.wait_ge(tp_ready, g + 1)
                nc.scalar.activation(act_hi[:, 4 * g:4 * g + 4, :],
                                     levp[:, 4 * (g % 2):4 * (g % 2) + 4, :], ACT.Copy).then_inc(tp_copied, 1)
            act.wait_ge(lb_rows, 2)
            nc.scalar.activation(lbrow[0:HEADS, :, :], lbrow[0:HEADS, :, :], ACT.Exp).then_inc(lb_e, 1)
            for n in range(2, N_PRO + 3):
                if n % CU == 2 and n > 2:
                    c = n // CU - 1
                    act.wait_ge(unit_used, c * CU + CU)
                    dst = qa[:, :, c * CH:(c + 1) * CH] if c < 2 else kv[:, :, :]
                    nc.scalar.activation(dst, pair[(c + 1) % 2][:, :, :], ACT.Copy, scale=DH ** -0.5 if c < 2 else 1.0)\
                        .then_inc(pair1_act if c != 1 else pair0_act, 1)
                if n == CU + 2:
                    act.wait_ge(lb_t, 1)
                    nc.scalar.activation(lbT[:, :, :], flat4[:, 0:2 * HEADS].rearrange("p (a h) -> p a h", a=2), ACT.Copy)\
                        .then_inc(lb_done, 1)
                if n < N_PRO + 2:
                    split_hi(n, 16 * (n // UNITS + 1) if n < N_PRO else unit_loaded(0, n - N_PRO))

            def o_split_hi(g):
                if g == 0:
                    act.wait_ge(unit_used, N_UNITS)
                    act.wait_ge(oaT_done, HEADS)
                if g == 2:
                    act.wait_ge(ohT_done, HEADS + ONE)
                nc.scalar.activation(act_hi[:, 4 * g:4 * g + 4, :], oT[:, 4 * g:4 * g + 4, :], ACT.Copy).then_inc(o_hi_ready, 1)

            def head(i, last):
                def hi(u):
                    split_hi(u, later_loaded(0, u - HU) if last and u >= HU else unit_loaded(i, u))

                act.wait_ge(qkT_ready, i + 1 + ONE)
                act.wait_ge(score_ready, i + ONE)
                nc.scalar.activation(qkT, bank_t.rearrange("p (a t) -> p a t", a=2), ACT.Copy).then_inc(qkT_copied, 1)
                hi(2)
                hi(3)
                act.wait_ge(max_ready, i + 1)
                for h in range(2):
                    nc.scalar.activation(prob[:, h, 0:P], prob[:, h, 0:P], ACT.Exp, bias=mneg[:, 0, h:h + 1],
                                         accum_out=psums[:, 0, h:h + 1]).then_inc(exp_done, 1)
                    nc.scalar.activation(prob[:, h, P:3 * P], prob[:, h, P:3 * P], ACT.Exp, bias=mneg[:, 1, h:h + 1],
                                         accum_out=psums[:, 1, h:h + 1]).then_inc(exp_done, 1)
                nc.scalar.activation(esink, esink, ACT.Exp).then_inc(exp_done, 1)
                hi(4)
                act.wait_ge(probT_ready, i + 1)
                act.wait_ge(oT_ready, i + ONE)
                nc.scalar.activation(probT[:, 0, :], bank_t[:, 0:3 * P], ACT.Copy).then_inc(probT_copied, 1)
                nc.scalar.activation(probT[:, 1, :], bank_o[:, 0:3 * P], ACT.Copy).then_inc(probT_copied, 1)
                act.wait_ge(oT_ready, i + 1 + ONE)
                settle(act, c_in)
                nc.scalar.activation(oaT[:, bass.ds(i, 1), :].rearrange("p a t -> p (a t)"), four[:, 0, 0:T], ACT.Copy)\
                    .then_inc(oaT_done, 1)
                hi(5)
                act.wait_ge(unit_used, i * HU + (N_PRO + CU))
                act.wait_ge(pair0_dve, i + ONE)
                nc.scalar.activation(es[:, :, 0:2 * HW], pair[0][:, :, 0:2 * HW], ACT.Tanh, scale=0.5).then_inc(es_ready, 1)
                nc.scalar.activation(es[:, :, 2 * HW:3 * HW], pair[0][:, :, 3 * HW:4 * HW], ACT.Tanh, scale=0.5)\
                    .then_inc(es_ready, 1)
                act.wait_ge(ho_ready, i + ONE)
                nc.scalar.activation(irow, pair[0][:, :, 2 * HW:3 * HW], ACT.Copy).then_inc(pair0_act, 1)
                hi(6)
                act.wait_ge(qfT_ready, i + 1)
                act.wait_ge(level_mm, i * 9 + ONE)
                nc.scalar.activation(qT, bank_t[:, 0:T], ACT.Copy, scale=Q_SCALE).then_inc(qT_copied, 1)
                hi(7)
                hi(8)
                act.wait_ge(level_mm, i * 9 + 9 + ONE)
                nc.scalar.activation(crossT, bank_t[:, 0:P], ACT.Copy).then_inc(cross_copied, 1)
                hi(9)
                act.wait_ge(ho_ready, i + 1 + ONE)
                for b in range(TB):
                    mean_square(b, es[:, b, 0:HW], bank_o[:, b * HW:(b + 1) * HW], HW, 4).then_inc(ho_sq, 1)
                if last:
                    o_split_hi(0)
                    o_split_hi(1)
                act.wait_ge(ohT_ready, i + 1)
                settle(act, c_in)
                nc.scalar.activation(ohT[:, bass.ds(i, 1), :].rearrange("p a t -> p (a t)"), bank_t[:, 0:T], ACT.Copy)\
                    .then_inc(ohT_done, 1)
                act.wait_ge(unit_used, i * HU + (N_PRO + HU))
                settle(act, c_in)
                nc.scalar.activation(gates[:, :, bass.ts(i, CH)], pair[1][:, :, :], ACT.Tanh, scale=0.5)\
                    .then_inc(pair1_act, 1)
            with act.Fori(0, HEADS - 1) as i:
                head(i, False)
            head(HEADS - 1, True)
            o_split_hi(2)
            o_split_hi(3)

            def m_split_hi(c):
                act.wait_ge(mT_ready, c + 1 + ONE)
                settle(act, c_in)
                dst = m_hi[:, bass.ds(c * 4, 4), :]
                nc.scalar.activation(dst, levp[:, 0:4, :], ACT.Copy, scale=0.5).then_inc(mT_done, 1)

            def branch_chunk(c, first):
                split_hi(2, later_loaded(c, 2))
                split_hi(3, later_loaded(c, 3))
                if not first:
                    m_split_hi(c - 1)
                split_hi(4, later_loaded(c, 4))
                split_hi(5, later_loaded(c, 5))
            branch_chunk(0, True)
            act.wait_ge(staged, 5 * HEADS)
            act.dma_start(wr[:, :, 0:NG], w_router_group[0].rearrange("(k p) n -> p k n", p=P)).then_inc(r_in, 16)
            act.dma_start(wr[:, :, NG:NR], w_router_expert[0].rearrange("(k p) n -> p k n", p=P)).then_inc(r_in, 16)
            act.dma_start(br[:, 0:NG], b_router_group[0:1, :].to_broadcast([P, NG])).then_inc(r_in, 16)
            act.dma_start(br[:, NG:NR], b_router_expert[0:1, :].to_broadcast([P, NE])).then_inc(r_in, 16)
            with act.Fori(1, NC) as c:
                branch_chunk(c, False)
            def square_sums(c):
                act.wait_ge(h_added, c + 1 + ONE)
                for b in range(TB):
                    nc.scalar.activation(square_scratch, resid[:, b, c * CH:(c + 1) * CH], ACT.Square, scale=D ** -0.5,
                                         accum_out=msq[:, b, c:c + 1]).then_inc(act_step, 1)
                    act.wait_ge(act_step, c * TB + b + 1)
            for c in range(NC):
                split_hi(2, later_loaded(NC + c, 2))
                if c == 0:
                    m_split_hi(NC - 1)
                split_hi(3, later_loaded(NC + c, 3))
                if c == 0:
                    act.dma_start(norm_g[:, :], moe_norm_g[0:1, :].to_broadcast([P, D])).then_inc(g2_in, 16)
                else:
                    square_sums(c - 1)
                if c < NC - 1:
                    split_hi(4, later_loaded(NC + c, 4))
                if c:
                    h_copy(c - 1)
                if c < NC - 1:
                    split_hi(5, later_loaded(NC + c, 5))
            square_sums(NC - 1)
            h_copy(NC - 1)
            act.wait_ge(lgT_ready, 1)
            nc.scalar.activation(lgT, pair[0][0:NR, 0, 0:T], ACT.Copy).then_inc(lgT_copied, 1)
            act.wait_ge(xn_ready, 3 * TB)
            act.dma_start(norm_g[:, :], final_norm_g.rearrange("(a d) -> a d", a=1).to_broadcast([P, D])).then_inc(g3_in, 16)
            act.wait_ge(r_exp_in, 1)
            nc.scalar.activation(small[:, 0:10], small[:, 0:10], ACT.Exp).then_inc(r_exp, 1)
            with act.Fori(0, GROUPS) as g:
                for half in range(2):
                    act.wait_ge(gathered, g * 2 + (half + 1) + ONE)
                    nc.scalar.activation(xg[:, half * KS:(half + 1) * KS, :],
                                         four[:, 2 * half:2 * half + 2, :].rearrange("p a (k n) -> p (a k) n", n=P),
                                         ACT.Copy).then_inc(xg_copied, 1)
                act.wait_ge(swT_ready, g + 1 + ONE)
                nc.scalar.activation(swT, pair[1][:, 0, 0:T], ACT.Copy).then_inc(swT_copied, 1)
                for q in range(GX):
                    hp = pair[0][:, q % 2, :]
                    yp = pair[1][:, q % 2, :]
                    act.wait_ge(quarter_used, g * (4 * GX) + (4 * q + 2))
                    act.wait_ge(ghid_ready, g * GX + q + ONE)
                    nc.scalar.activation(geh, hp[:, 0:P], ACT.Tanh, scale=0.5).then_inc(ge_exp, 1)
                    act.wait_ge(ghT_ready, g * GX + (q + 1) + ONE)
                    nc.scalar.activation(ghT, hp[:, 2 * P:3 * P], ACT.Copy, scale=0.5).then_inc(ghT_copied, 1)
                    act.wait_ge(quarter_used, g * (4 * GX) + (4 * q + 4))
                    for c in (0, 1):
                        nc.scalar.activation(yg[q * SL:(q + 1) * SL, c * CH:(c + 1) * CH], yp[c * SL:(c + 1) * SL, :],
                                             ACT.Copy).then_inc(yg_act, 1)
            act.wait_ge(over_ready, 1)
            act.wait_ge(scattered, GROUPS * 2 * NC + ONE)
            n_over = act.value_load(over_i[0:1, LIST:LIST + 1], min_val=0, max_val=LIST)
            with act.If(n_over > 0):
                with act.Fori(0, n_over) as e:
                    for b in range(TB):
                        act.wait_ge(oh13_ready, e * 2 + (b + 1) + ONE)
                        act.wait_ge(hid_ready, e * 2 + b + ONE)
                        nc.scalar.activation(ehid[:, b, :], pair[b][:, 0, :], ACT.Tanh, scale=half_rstd[:, b:b + 1])\
                            .then_inc(e_exp, 1)
                        act.wait_ge(hidT_ready, e * 2 + (b + 1) + ONE)
                        nc.scalar.activation(hidT[:, b], four[:, 3, :].rearrange("p (k t) -> p k t", k=4), ACT.Copy)\
                            .then_inc(hidT_copied, 1)
            act.wait_ge(resid_done, 1)
            mean_square(0, gates[:, 0, 0:D], resid[:, 0, :], D, 12).then_inc(ms_done, 1)

        @block.tensor
        def _(pe):
            for ahead in (oh13_ready, oy_ready, gathered, swT_ready, ghT_ready, qkT_ready, oT_ready, score_ready,
                          ho_ready, level_mm, mT_ready, hidT_ready):
                pe.sem_inc(ahead, ONE)
            def transpose_rows(src, first):
                for g in range(4):
                    if g % 2 == 0:
                        pe.wait_ge(xn_ready, TB * (g // 2 + 1))
                    if first + g >= 2:
                        pe.wait_ge(xl_ready, first + g - 1)
                    for k in range(4):
                        for b in range(TB):
                            kk = 4 * g + k
                            last = nc.tensor.transpose(levp[:, 4 * (g % 2) + k, b * P:(b + 1) * P],
                                                       src[:, b, kk * P:(kk + 1) * P], ident)
                    last.then_inc(tp_ready, 1)

            pe.wait_ge(id_in, 16)
            transpose_rows(gates, 0)
            def project(dst, u, k, hi=act_hi, lo=act_lo, first=0, end=KD):
                wh, wl = w_hi[:, u % UNITS, k % KU, :], w_lo[:, u % UNITS, k % KU, :]
                for b in range(TB):
                    xh = hi[:, k, b * P:(b + 1) * P]
                    xl = m_lo[:, b, D + k * P:D + (k + 1) * P] if lo is m_lo else lo[:, k, b * P:(b + 1) * P]
                    nc.tensor.matmul(dst[:, b, :], xh, wh, start=(k == first), stop=False)
                    nc.tensor.matmul(dst[:, b, :], xh, wl, start=False, stop=False)
                    last = nc.tensor.matmul(dst[:, b, :], xl, wh, start=False, stop=(k == end - 1))
                if k % KU == KU - 1:
                    last.then_inc(unit_used, 1)

            for n in range(N_PRO):
                c = n // CU
                if n == 2 * CU:
                    pe.wait_ge(pair1_act, 1)
                if n < CU:
                    pe.wait_ge(xl_ready, n + 1)
                if n % 2 == 0:
                    pe.wait_ge(lo_pool, n // 2 + 1)
                else:
                    pe.wait_ge(lo_dve, n // 2 + 1)
                for k in range((n % CU) * KU, (n % CU + 1) * KU):
                    project(pair[(c + 1) % 2], n, k)
                if n == CU - 2:
                    pe.wait_ge(lb_s, 2)
                    pe.wait_ge(c_in, 16 * 3)
                    pe.wait_ge(xl_ready, 3)
                    for a in range(2):
                        last = nc.tensor.transpose(flat4[:, a * HEADS:(a + 1) * HEADS], lbrow[0:HEADS, a, :],
                                                   ident[0:HEADS, 0:HEADS])
                    last.then_inc(lb_t, 1)

            with pe.Fori(0, HEADS) as i:
                def a_transpose():
                    pe.wait_ge(staged, i * 5 + 5)
                    pe.wait_ge(ohT_done, i + ONE)
                    pe.wait_ge(lb_done, 1)
                    for a, src in enumerate((qs, ks)):
                        for b in range(TB):
                            last = nc.tensor.transpose(bank_t[:, a * T + b * P:a * T + (b + 1) * P], src[:, b, :], ident)
                    last.then_inc(qkT_ready, 1)

                def a_scores():
                    pe.wait_ge(qkT_copied, i + 1)
                    pe.wait_ge(lev_read, i + ONE)
                    pe.wait_ge(cross_copied, i + ONE)
                    for h in range(2):
                        r = slice(h * DH, (h + 1) * DH)
                        nc.tensor.matmul(four[:, h, 0:P], qkT[r, 0, 0:P], qkT[r, 1, 0:P], start=True, stop=True)
                        last = nc.tensor.matmul(four[:, h, P:3 * P], qkT[r, 0, P:T], qkT[r, 1, :], start=True, stop=True)
                    last.then_inc(score_ready, 1)

                def a_probT():
                    pe.wait_ge(prob_ready, i * 4 + 4 + ONE)
                    pe.wait_ge(oh_ready, i * 2 + ONE)
                    for h in range(2):
                        bank = (bank_t, bank_o)[h]
                        for k in range(3):
                            last = nc.tensor.transpose(bank[:, k * P:(k + 1) * P], prob[:, h, k * P:(k + 1) * P], ident)
                    last.then_inc(probT_ready, 1)

                def a_values():
                    pe.wait_ge(probT_copied, i * 2 + 2)
                    for h in range(2):
                        o = four[h * DH:(h + 1) * DH, 0, :]
                        nc.tensor.matmul(o[:, P:T], vs[:, 0, :], probT[:, h, P:2 * P], start=True, stop=False)
                        nc.tensor.matmul(o[:, P:T], vs[:, 1, :], probT[:, h, 2 * P:3 * P], start=False, stop=True)
                        last = nc.tensor.matmul(o[:, 0:P], vs[:, 0, :], probT[:, h, 0:P], start=True, stop=True)
                    last.then_inc(oT_ready, 1)

                def h_transpose():
                    pe.wait_ge(hg_rows, i + 1 + ONE)
                    for a, src in enumerate((qrow, es[:, :, HW:2 * HW])):
                        for b in range(TB):
                            last = nc.tensor.transpose(bank_t[:, a * T + b * P:a * T + (b + 1) * P], src[:, b, :], ident)
                    last.then_inc(qfT_ready, 1)

                def h_level(lv):
                    def go():
                        if lv == 0:
                            pe.wait_ge(qT_copied, i + 1)
                            pe.wait_ge(oaT_done, i + 1)
                        pe.wait_ge(level_ops, i * 8 + max(lv, 1))
                        if lv == LEVELS + 1:
                            nc.tensor.matmul(bank_t[:, 0:P], kq[:, 0:P], qp[:, P:T], start=True, stop=True)\
                                .then_inc(level_mm, 1)
                            return
                        for b in range(TB):
                            if lv == LEVELS:
                                last = nc.tensor.matmul(levp[:, lv, b * P:(b + 1) * P], kq[:, b * P:(b + 1) * P],
                                                        qp[:, b * P:(b + 1) * P], start=True, stop=True)
                                continue
                            for h in range(2):
                                t = slice(b * P + h * HB, b * P + (h + 1) * HB)
                                last = nc.tensor.matmul(levh[h * HB:(h + 1) * HB, lv, b * HB:(b + 1) * HB], kq[:, t],
                                                        (qT if lv == 0 else qp)[:, t], start=True, stop=True)
                        last.then_inc(level_mm, 1)
                    return go

                def h_values():
                    pe.wait_ge(hatt_ready, i + 1)
                    pe.wait_ge(cross_copied, i + 1 + ONE)
                    pe.wait_ge(pair0_act, i + 2)
                    o = [bank_o[:, b * HW:(b + 1) * HW] for b in range(TB)]
                    nc.tensor.matmul(o[0], hatt[:, 0:P], irow[:, 0, :], start=True, stop=True)
                    nc.tensor.matmul(o[1], hatt[:, P:T], irow[:, 1, :], start=True, stop=False)
                    nc.tensor.matmul(o[1], crossT, irow[:, 0, :], start=False, stop=True).then_inc(ho_ready, 1)

                def h_outT():
                    pe.wait_ge(oh_ready, i * 2 + 2 + ONE)
                    for b in range(TB):
                        last = nc.tensor.transpose(bank_t[:, b * P:(b + 1) * P], oh[:, b, :], ident)
                    last.then_inc(ohT_ready, 1)

                tasks = {2: [a_transpose], 3: [a_scores], 9: [a_probT], 11: [a_values],
                         KD + 1: [h_transpose], KD + 3: [h_level(0), h_level(1)], KD + 4: [h_level(2)],
                         KD + 5: [h_level(3)], KD + 6: [h_level(4)], KD + 7: [h_level(5)],
                         KD + 8: [h_level(6)], KD + 9: [h_level(7)], KD + 11: [h_level(8)],
                         KD + 12: [h_values]}
                for u in range(HU):
                    if u == 0:
                        pe.wait_ge(pair0_act, i + 1)
                        pe.wait_ge(pair0_dve, i + ONE)
                    if u == CU:
                        pe.wait_ge(pair1_act, i + 2)
                    wait_lo(pe, i, u)
                    for k in range((u % CU) * KU, (u % CU + 1) * KU):
                        project(pair[u // CU], u, k)
                        for task in tasks.get((u // CU) * KD + k, ()):
                            task()
                h_outT()

            def turn_merged(c):
                pe.wait_ge(merged_ready, c + 1)
                pe.wait_ge(m_lo_ready, TB * c)
                for k in range(4):
                    for b in range(TB):
                        last = nc.tensor.transpose(levp[:, k, b * P:(b + 1) * P], merged[:, b, k * P:(k + 1) * P], ident)
                last.then_inc(mT_ready, 1)

            def branch_chunk(c, first):
                for u in range(CU):
                    if first:
                        pe.wait_ge(o_lo_ready, u + 1)
                        if u == 0:
                            pe.wait_ge(pair0_act, HEADS + 1)
                            pe.wait_ge(pair0_dve, HEADS + ONE)
                        if u == CU // 2:
                            pe.wait_ge(pair1_act, HEADS + 2)
                    elif u % 2 == 0:
                        pe.wait_ge(y_read, c * 2 + (u // 2 - 1) + ONE)
                    wait_later_lo(pe, c, u)
                    for k in range(u * KU, (u + 1) * KU):
                        project(pair[u // 2], u, k, first=u // 2 * KS, end=u // 2 * KS + KS)
                    if u == 0 and not first:
                        turn_merged(c - 1)
            branch_chunk(0, True)
            with pe.Fori(1, NC) as c:
                branch_chunk(c, False)
            def h_transpose_chunk(c):
                pe.wait_ge(hg_ready, c + 1)
                pe.wait_ge(tp_copied, 4 + c - 1)
                for k in range(4):
                    for b in range(TB):
                        kk = 4 * c + k
                        last = nc.tensor.transpose(levp[:, 4 * (c % 2) + k, b * P:(b + 1) * P],
                                                   hn[:, b, kk * P:(kk + 1) * P], ident)
                last.then_inc(tp_ready, 1)

            for c in range(NC):
                if c < 2:
                    pe.wait_ge(y_read, 2 * NC - 1 + c + ONE)
                else:
                    pe.wait_ge(h_added, c - 1 + ONE)
                for u in range(CU):
                    if c == 0:
                        pe.wait_ge(m_lo_ready, TB * max(u + 1, NC - 1))
                    wait_later_lo(pe, NC + c, u)
                    for k in range(u * KU, (u + 1) * KU):
                        project(pair[c % 2], u, k, m_hi, m_lo)
                    if c == 0 and u == 0:
                        turn_merged(NC - 1)
                    if c and u == 1:
                        h_transpose_chunk(c - 1)
            def logits(first, end):
                for k in range(first, end):
                    last = nc.tensor.matmul(pair[0][0:NR, 0, 0:T], wr[:, k, :], hT[:, k, :], start=(k == 0), stop=(k == KD - 1))
                return last
            pe.wait_ge(r_in, 16 * 4)
            pe.wait_ge(h_added, NC - 1 + ONE)
            pe.wait_ge(tp_copied, 7)
            logits(0, 6)
            h_transpose_chunk(NC - 1)
            logits(6, 12)
            pe.wait_ge(tp_copied, 8)
            logits(12, KD).then_inc(lgT_ready, 1)
            pe.wait_ge(lgT_copied, 1)
            pe.wait_ge(h_added, NC + ONE)
            for b in range(TB):
                last = nc.tensor.transpose(pair[1][:, b, 0:NR], lgT[:, b * P:(b + 1) * P], ident[0:NR, 0:NR])
            last.then_inc(logit_ready, 1)
            pe.wait_ge(logit_read, 2)
            pe.wait_ge(mask_ready, 1)
            tri, ones = cst[:, K_TRI:K_TRI + P], cst[:, K_ONE:K_ONE + P]
            rank = pair[1][:, 0, 0:3 * NE].rearrange("p (b e) -> p b e", b=3)
            nc.tensor.matmul(rank[:, 0, :], tri, rmask[:, 0, :], start=True, stop=True)
            nc.tensor.matmul(rank[:, 1, :], tri, rmask[:, 1, :], start=True, stop=False)
            nc.tensor.matmul(rank[:, 1, :], ones, rmask[:, 0, :], start=False, stop=True)
            nc.tensor.matmul(rank[:, 2, :], ones, rmask[:, 0, :], start=True, stop=False)
            nc.tensor.matmul(rank[:, 2, :], ones, rmask[:, 1, :], start=False, stop=True).then_inc(rank_ready, 1)
            pe.wait_ge(rank_read, 1)
            with pe.Fori(0, GROUPS) as g:
                pe.wait_ge(onehot_ready, g * 2 + 2)
                pe.wait_ge(scattered, g * (2 * NC) + ONE)
                def gather(half):
                    for k in range(half * KS, (half + 1) * KS):
                        for b in range(TB):
                            last = nc.tensor.matmul(flat4[:, k * P:(k + 1) * P], hn[:, b, k * P:(k + 1) * P],
                                                    gh[:, b, :], start=(b == 0), stop=(b == TB - 1))
                    last.then_inc(gathered, 1)
                gather(0)
                pe.wait_ge(sw_ready, g * 2 + 2)
                pe.wait_ge(yg_act, g * (2 * GX) + ONE)
                pe.wait_ge(yg_dve, g * (2 * GX) + ONE)
                for b in range(TB):
                    last = nc.tensor.transpose(pair[1][:, 0, b * P:(b + 1) * P], sw[:, b, :], ident)
                last.then_inc(swT_ready, 1)
                for q in range(GX):
                    hp = pair[0][:, q % 2, :]
                    yp = pair[1][:, q % 2, :]
                    pe.wait_ge(ghT_copied, g * GX + q + ONE)
                    for half in range(2):
                        if q == 0:
                            pe.wait_ge(xg_copied, g * 2 + (half + 1))
                        for m in range(2):
                            s = 2 * half + m
                            pe.wait_ge(loaded[s], g * (16 * GX) + 16 * (q + 1))
                        for k in range(KS):
                            kk = half * KS + k
                            for c in range(4):
                                last = nc.tensor.matmul(
                                    hp[c * SL:(c + 1) * SL, 0:2 * P], xg[:, kk, q * SL:(q + 1) * SL],
                                    wslot[:, 2 * half:2 * half + 2, k * CH + c * P:k * CH + (c + 1) * P],
                                    start=(kk == 0), stop=(kk == KD - 1))
                        last.then_inc(quarter_used, 1)
                        if q == 0 and half == 0:
                            gather(1)
                    pe.wait_ge(ghid_ready, g * GX + (q + 1) + ONE)
                    nc.tensor.transpose(hp[:, 2 * P:3 * P], ghid, ident).then_inc(ghT_ready, 1)
                    pe.wait_ge(ghT_copied, g * GX + (q + 1) + ONE)
                    pe.wait_ge(swT_copied, g + 1)
                    pe.wait_ge(yg_act, g * (2 * GX) + 2 * q + ONE)
                    pe.wait_ge(yg_dve, g * (2 * GX) + 2 * q + ONE)
                    for k in range(4):
                        if k % 2 == 0:
                            pe.wait_ge(loaded[4 + k // 2], g * (16 * GX) + 16 * (q + 1))
                        for c in range(4):
                            last = nc.tensor.matmul(yp[c * SL:(c + 1) * SL, :], ghT[:, k * SL:(k + 1) * SL],
                                                    slot_w2(4 + k // 2)[:, k % 2, c * CH:(c + 1) * CH],
                                                    start=(k == 0), stop=(k == 3))
                        if k % 2 == 1:
                            last.then_inc(quarter_used, 1)
                pe.wait_ge(yg_act, g * (2 * GX) + 2 * GX + ONE)
                pe.wait_ge(yg_dve, g * (2 * GX) + 2 * GX + ONE)
                for b in range(TB):
                    for c in range(NC):
                        if b == 1:
                            pe.wait_ge(scattered, g * (2 * NC) + (c + 1) + ONE)
                        nc.tensor.matmul(four[:, c, :], swT[:, b * P:(b + 1) * P], yg[:, c * CH:(c + 1) * CH],
                                         start=True, stop=True).then_inc(back_ready, 1)
            pe.wait_ge(over_ready, 1)
            pe.wait_ge(scattered, GROUPS * 2 * NC + ONE)
            n_over = pe.value_load(over_i[0:1, LIST:LIST + 1], min_val=0, max_val=LIST)
            with pe.If(n_over > 0):
                with pe.Fori(0, n_over) as e:
                    for b in range(TB):
                        pe.wait_ge(hid_ready, e * 2 + b + ONE)
                        for half in range(2):
                            for m in range(2):
                                s = 2 * half + m
                                if b == 0:
                                    pe.wait_ge(loaded[s], e * 16 + 16 * (1 + NE))
                                for k in range(KS):
                                    kk = half * KS + k
                                    last = nc.tensor.matmul(pair[b][:, m, :], hT[:, kk, b * P:(b + 1) * P], slot(s)[:, k, :],
                                                            start=(kk == 0), stop=(kk == KD - 1))
                        last.then_inc(oh13_ready, 1)
                    for b in range(TB):
                        pe.wait_ge(hid_ready, e * 2 + (b + 1) + ONE)
                        pe.wait_ge(y_added, e * 8 + b * 4 + ONE)
                        pe.wait_ge(hidT_copied, e * 2 + b + ONE)
                        for k in range(4):
                            last = nc.tensor.transpose(four[:, 3, k * P:(k + 1) * P], hid[:, b, k * P:(k + 1) * P], ident)
                        last.then_inc(hidT_ready, 1)
                        pe.wait_ge(hidT_copied, e * 2 + (b + 1) + ONE)
                        for half in range(2):
                            if b == 0:
                                pe.wait_ge(loaded[4 + half], e * 16 + 16 * (1 + NE))
                        for c in range(NC):
                            for k in range(4):
                                last = nc.tensor.matmul(four[:, c, :], hidT[:, b, k, :],
                                                        slot_w2(4 + k // 2)[:, k % 2, c * CH:(c + 1) * CH],
                                                        start=(k == 0), stop=(k == 3))
                            last.then_inc(oy_ready, 1)

        @block.vector
        def _(dve):
            for ahead in (prob_ready, hg_rows, hid_ready, lev_read, oh_ready, pair0_dve, y_read, h_added, y_added,
                          scattered, ghid_ready, yg_dve):
                dve.sem_inc(ahead, ONE)
            chain = Chain(dve, dve_step)
            link = chain.link

            def mean_square_dve(b, dst, src, col):
                return nc.vector.tensor_tensor_reduce(out=dst, in0=src, in1=src, scale=1.0 / D, scalar=0.0, op0=ALU.mult,
                                                      op1=ALU.add, accum_out=stat[:, col + b:col + b + 1])

            def rstd(v):
                y, t = nwt[:, 0:TB], nwt[:, TB:2 * TB]
                link(nc.vector.tensor_scalar(v, v, EPS, None, ALU.add))
                link(nc.vector.tensor_scalar(y.bitcast(I32), v.bitcast(I32), -0.5, float(0x5F3759DF), ALU.mult, ALU.add))
                for step in range(3):
                    link(nc.vector.tensor_tensor(t, y, y, ALU.mult))
                    link(nc.vector.scalar_tensor_tensor(t, t, -0.5, v, ALU.mult, ALU.mult))
                    link(nc.vector.scalar_tensor_tensor(v if step == 2 else y, t, 1.5, y, ALU.add, ALU.mult))

            dve.wait_ge(x_in[1], 16)
            link(mean_square_dve(1, actT[:, KS:KD, :].rearrange("p a b -> p (a b)"), resid[:, 1, :], 0))
            dve.wait_ge(ms_done, 1)
            dve.wait_ge(g_in, 16)
            rstd(stat[:, 0:2])
            for cols in (slice(0, D // 2), slice(D // 2, D)):
                for b in range(TB):
                    nc.vector.scalar_tensor_tensor(gates[:, b, cols], resid[:, b, cols], stat[:, b:b + 1], norm_g[:, cols],
                                                   ALU.mult, ALU.mult).then_inc(xn_ready, 1)
            def split_lo(n, u):
                dve.wait_ge(hi_ready, n)
                nc.vector.tensor_tensor(w_lo[:, u % UNITS], w_raw[:, u % UNITS], w_hi[:, u % UNITS].bitcast(F32), ALU.subtract)\
                    .then_inc(lo_dve, 1)

            def xl(g):
                dve.wait_ge(tp_copied, g + 1)
                nc.vector.tensor_tensor(act_lo[:, 4 * g:4 * g + 4, :], levp[:, 4 * (g % 2):4 * (g % 2) + 4, :],
                                        act_hi[:, 4 * g:4 * g + 4, :].bitcast(F32), ALU.subtract).then_inc(xl_ready, 1)
            dve.wait_ge(lb_in, 32)
            r0, r1 = lbrow[0:HEADS, 0, :], lbrow[0:HEADS, 1, :]
            top = es[0:HEADS, 0, 0:P]
            link(nc.vector.tensor_tensor(top, r0, r1, ALU.max))
            nc.vector.tensor_tensor(r0, r0, top, ALU.subtract).then_inc(lb_rows, 1)
            nc.vector.tensor_tensor(r1, r1, top, ALU.subtract).then_inc(lb_rows, 1)
            for g in range(4):
                xl(g)
            split_lo(2, 1)
            dve.wait_ge(lb_e, 1)
            link(nc.vector.tensor_tensor(r1, r0, r1, ALU.add))
            link(nc.vector.reciprocal(r1, r1))
            link(nc.vector.tensor_tensor(r0, r0, r1, ALU.mult))
            nc.vector.tensor_scalar(r1, r0, -0.5, 0.5, ALU.mult, ALU.add).then_inc(lb_s, 1)
            nc.vector.tensor_scalar(r0, r0, 0.5, 0.5, ALU.mult, ALU.add).then_inc(lb_s, 1)
            dve.wait_ge(c_in, 16 * 3)
            nc.vector.tensor_scalar(hnorm[:, :], hnorm[:, :], 0.5, None, ALU.mult).then_inc(lb_s, 1)
            for n in range(3, N_PRO, 2):
                split_lo(n + 1, n)
            dve.wait_ge(lb_s, 3)
            dve.wait_ge(lb_done, 1)

            att_mask = cst[:, K_ATT:K_ATT + 3 * P]
            lev_mask = cst[:, K_LEV:K_LEV + LEVELS * HB].rearrange("p (l t) -> p l t", l=LEVELS)
            top_mask = cst[:, K_TOP:K_TOP + P]
            def head(i):
                dve.wait_ge(staged, i * 5 + 5)
                dve.wait_ge(score_ready, i + 1 + ONE)
                for h in range(2):
                    link(nc.vector.tensor_tensor(prob[:, h, :], four[:, h, 0:3 * P], att_mask, ALU.add))
                link(nc.vector.tensor_reduce(mx[:, 0, :], prob[:, :, 0:P], AX.X, ALU.max))
                link(nc.vector.tensor_reduce(mx[:, 1, :], prob[:, :, P:3 * P], AX.X, ALU.max))
                link(nc.vector.tensor_tensor(mx, mx, sk, ALU.max))
                link(nc.vector.tensor_tensor(esink, sk, mx, ALU.subtract))
                nc.vector.tensor_scalar(mneg, mx, -1.0, None, ALU.mult).then_inc(max_ready, 1)
                dve.wait_ge(exp_done, i * 5 + 5)
                link(nc.vector.tensor_tensor(rden, psums, esink, ALU.add))
                link(nc.vector.reciprocal(rden, rden))
                for h in range(2):
                    nc.vector.tensor_scalar(prob[:, h, 0:P], prob[:, h, 0:P], rden[:, 0, h:h + 1], None, ALU.mult)\
                        .then_inc(prob_ready, 1)
                    nc.vector.tensor_scalar(prob[:, h, P:3 * P], prob[:, h, P:3 * P], rden[:, 1, h:h + 1], None, ALU.mult)\
                        .then_inc(prob_ready, 1)
                for u in HEAD_DVE:
                    split_lo(i * HU + (N_PRO + u + 1), u)
                dve.wait_ge(es_ready, i * 2 + 2)
                dve.wait_ge(pair0_act, i + 2)
                link(nc.vector.scalar_tensor_tensor(orow, es[:, :, 2 * HW:3 * HW], 1.0, pair[0][:, :, 3 * HW:4 * HW],
                                                    ALU.add, ALU.mult))
                nc.vector.scalar_tensor_tensor(qrow, es[:, :, 0:HW], 1.0, pair[0][:, :, 0:HW], ALU.add, ALU.mult)\
                    .then_inc(hg_rows, 1)
                nc.vector.tensor_tensor(orow, orow, bc(hnorm[:, :].unsqueeze(1), [P, TB, HW]), ALU.mult).then_inc(pair0_dve, 1)
                settle(dve, c_in)
                link(nc.vector.tensor_copy(lbs, lbT[:, :, bass.ds(i, 1)].rearrange("p a o -> p (a o)")))
                dve.wait_ge(qT_copied, i + 1)
                link(nc.vector.tensor_scalar(fT, bank_t[:, T:2 * T], lbs[:, 1:2], lbs[:, 0:1], ALU.mult, ALU.add))
                link(nc.vector.scalar_tensor_tensor(qp, bank_t[:, 0:T], Q_SCALE, fT, ALU.mult, ALU.mult))
                nc.vector.tensor_scalar(kq, fT, -1.0, 1.0, ALU.mult, ALU.add).then_inc(level_ops, 1)
                totals = fT
                off = 0
                for lv in range(1, LEVELS + 1):
                    size = 1 << (lv - 1)
                    blocks = T // size
                    pairs = totals.rearrange("p (n a) -> p n a", a=2)
                    q_odd = qp.rearrange("p (n a s) -> p n a s", a=2, s=size)[:, :, 1, :]
                    k_even = kq.rearrange("p (n a s) -> p n a s", a=2, s=size)[:, :, 0, :]
                    dve.wait_ge(level_mm, i * 9 + (lv + 1) + ONE)
                    if lv == 1:
                        dve.wait_ge(level_ops, i * 8 + 1)
                    link(nc.vector.tensor_tensor(q_odd, q_odd, bc(pairs[:, :, 0:1], [P, blocks // 2, size]), ALU.mult))
                    if lv < LEVELS:
                        nxt = tot[:, off:off + blocks // 2]
                        link(nc.vector.tensor_tensor(nxt, pairs[:, :, 0], pairs[:, :, 1], ALU.mult))
                        off += blocks // 2
                    nc.vector.tensor_tensor(k_even, k_even, bc(pairs[:, :, 1:2], [P, blocks // 2, size]), ALU.mult)\
                        .then_inc(level_ops, 1)
                    totals = nxt
                    dve.wait_ge(level_ops, i * 8 + (lv + 1))
                    if lv == LEVELS - 1:
                        for b in range(TB):
                            ins = nc.vector.tensor_tensor(lev[:, :, b * HB:(b + 1) * HB], levh[:, :, b * HB:(b + 1) * HB],
                                                          lev_mask, ALU.mult)
                            if b == TB - 1:
                                ins.then_inc(lev_read, 1)
                            else:
                                link(ins)
                dve.wait_ge(lev_read, i + 1 + ONE)
                link(nc.vector.tensor_reduce(diag.rearrange("p b t -> p (b t)"), lev.rearrange("p l t -> p t l"), AX.X, ALU.add))
                att = hatt.rearrange("p (b t) -> p b t", b=TB)
                link(nc.vector.tensor_tensor(att, levp[:, LEVELS, :].rearrange("p (b t) -> p b t", b=TB),
                                             bc(top_mask.unsqueeze(1), [P, TB, P]), ALU.mult))
                for h in range(2):
                    half = slice(h * HB, (h + 1) * HB)
                    ins = nc.vector.tensor_tensor(att[half, :, half], att[half, :, half], diag[half, :, :], ALU.add)
                    if h:
                        ins.then_inc(hatt_ready, 1)
                    else:
                        link(ins)
                dve.wait_ge(ho_sq, i * 2 + 2)
                rstd(stat[:, 4:6])
                for b in range(TB):
                    nc.vector.scalar_tensor_tensor(oh[:, b, :], bank_o[:, b * HW:(b + 1) * HW], stat[:, 4 + b:5 + b],
                                                   orow[:, b, :], ALU.mult, ALU.mult).then_inc(oh_ready, 1)
            with dve.Fori(0, HEADS) as i:
                chain.enter(i, 40)
                head(i)
            chain.leave(HEADS)
            for g in range(4):
                dve.wait_ge(o_hi_ready, g + 1)
                nc.vector.tensor_tensor(act_lo[:, 4 * g:4 * g + 4, :], oT[:, 4 * g:4 * g + 4, :],
                                        act_hi[:, 4 * g:4 * g + 4, :].bitcast(F32), ALU.subtract).then_inc(o_lo_ready, 1)

            def m_split_lo(c):
                dve.wait_ge(mT_done, c + 1 + ONE)
                for b in range(TB):
                    t = slice(b * P, (b + 1) * P)
                    nc.vector.scalar_tensor_tensor(m_lo[:, b, bass.ds(c * CH + D, CH)].rearrange("p (k t) -> p k t", t=P),
                                                   levp[:, 0:4, t], 0.5, m_hi[:, bass.ds(c * 4, 4), t].bitcast(F32),
                                                   ALU.mult, ALU.subtract).then_inc(m_lo_ready, 1)

            def merge_chunk(c, first):
                split_lo(c * CU + (N_UNITS + 3), 2)
                if not first:
                    m_split_lo(c - 1)
                split_lo(c * CU + (N_UNITS + 4), 3)
                for a, m in enumerate((merged, merged2)):
                    dve.wait_ge(unit_used, c * CU + (N_UNITS + CU // 2 * (a + 1)))
                    nc.vector.scalar_tensor_tensor(m, gates[:, :, bass.ds(c * CH + a * D, CH)], 1.0, pair[a][:, :, :],
                                                   ALU.add, ALU.mult).then_inc(y_read, 1)
                dve.wait_ge(y_read, c * 2 + 2 + ONE)
                nc.vector.tensor_tensor(merged, merged, merged2, ALU.add).then_inc(merged_ready, 1)
            dve.wait_ge(pair1_act, HEADS + 2)
            merge_chunk(0, True)
            with dve.Fori(1, NC) as c:
                merge_chunk(c, False)
            split_lo(N_WO + 3, 2)
            m_split_lo(NC - 1)
            split_lo(N_WO + 4, 3)
            dve.wait_ge(g2_in, 16)
            for b in range(TB):
                dve.wait_ge(x_in[b], 32)
            for c in range(NC):
                dve.wait_ge(unit_used, N_WO + CU * (c + 1))
                h_c = resid[:, :, c * CH:(c + 1) * CH]
                nc.vector.tensor_tensor(h_c, h_c, pair[c % 2][:, :, :], ALU.add).then_inc(h_added, 1)
                dve.wait_ge(h_added, c + 1 + ONE)
                nc.vector.tensor_tensor(hn[:, :, c * CH:(c + 1) * CH], h_c,
                                        bc(norm_g[:, c * CH:(c + 1) * CH].unsqueeze(1), [P, TB, CH]), ALU.mult)\
                    .then_inc(hg_ready, 1)
                if c < NC - 1:
                    for u in (2, 3):
                        split_lo(N_WO + (c + 1) * CU + u + 1, u)
            dve.wait_ge(act_step, NC * TB)
            link(nc.vector.tensor_reduce(stat[:, 8:10], msq, AX.X, ALU.add))
            rstd(stat[:, 8:10])
            link(nc.vector.tensor_scalar(half_rstd, stat[:, 8:10], 0.5, None, ALU.mult))
            dve.wait_ge(tp_ready, 8)
            for b in range(TB):
                nc.vector.tensor_scalar(hn[:, b, :], hn[:, b, :], stat[:, 8 + b:9 + b], None, ALU.mult).then_inc(xn_ready, 1)

            off = [NR]

            def rw(*shape):
                n = 1
                for s in shape:
                    n *= s
                ap = rwork[:, off[0]:off[0] + n]
                off[0] += n
                return ap.rearrange("p (a b) -> p a b", a=shape[0]) if len(shape) == 2 else ap
            lg = rw(TB, NR)
            oneg = rw(TB, NG)
            me = rw(TB, NE)
            oh1 = rw(TB, NE)
            oh2 = rw(TB, NE)
            t32 = rw(TB, NE)
            t4 = rw(TB, NG)
            m_g, i_g, m_1, i_1, m_2, i_2, psel, w_1, w_2, s1 = (rw(TB, 1) for _ in range(10))
            iota = cst[:, K_IOTA:K_IOTA + NE]
            dve.wait_ge(logit_ready, 1)
            for b in range(TB):
                nc.vector.scalar_tensor_tensor(lg[:, b, :], pair[1][:, b, 0:NR], stat[:, 8 + b:9 + b], br, ALU.mult, ALU.add)\
                    .then_inc(logit_read, 1)
            dve.wait_ge(logit_read, 2)

            def first_max(v, m, idx, onehot, tmp, n):
                it = bc(iota[:, 0:n].unsqueeze(1), [P, TB, n])
                link(nc.vector.tensor_reduce(m, v, AX.X, ALU.max))
                link(nc.vector.tensor_tensor(tmp, v, bc(m, [P, TB, n]), ALU.is_lt))
                link(nc.vector.scalar_tensor_tensor(tmp, tmp, 1000.0, it, ALU.mult, ALU.add))
                link(nc.vector.tensor_reduce(idx, tmp, AX.X, ALU.min))
                link(nc.vector.tensor_tensor(onehot, it, bc(idx, [P, TB, n]), ALU.is_equal))

            lgg = lg[:, :, 0:NG]
            first_max(lgg, m_g, i_g, oneg, t4, NG)
            ex = small[:, 0:TB * NG].rearrange("p (b g) -> p b g", b=TB)
            gm = bc(oneg.rearrange("p b g -> p (b g)").unsqueeze(2), [P, TB * NG, EG])
            link(nc.vector.tensor_scalar(t32.rearrange("p b (g e) -> p (b g) e", g=NG), gm, 1.0, -NEG, ALU.subtract, ALU.mult))
            link(nc.vector.tensor_tensor(me, lg[:, :, NG:NR], t32, ALU.add))
            first_max(me, m_1, i_1, oh1, t32, NE)
            link(nc.vector.scalar_tensor_tensor(me, oh1, 4 * NEG, me, ALU.mult, ALU.add))
            first_max(me, m_2, i_2, oh2, t32, NE)
            nc.vector.tensor_tensor(rmask, oh1, oh2, ALU.add).then_inc(mask_ready, 1)
            link(nc.vector.tensor_tensor(ex, lgg, bc(m_g, [P, TB, NG]), ALU.subtract))
            d12 = small[:, 8:10].rearrange("p (b o) -> p b o", b=TB)
            nc.vector.tensor_tensor(d12, m_2, m_1, ALU.subtract).then_inc(r_exp_in, 1)
            dve.wait_ge(mask_ready, 1)
            link(nc.vector.tensor_scalar(place, rmask, -BIG, BIG, ALU.mult, ALU.add))
            dve.wait_ge(rank_ready, 1)
            rank = pair[1][:, 0, 0:3 * NE].rearrange("p (b e) -> p b e", b=3)
            over, upto, idx = lrow[0:1, 0:NE], lrow[0:1, NE:2 * NE], lrow[0:1, 2 * NE:2 * NE + LIST + 1]
            link(nc.vector.tensor_tensor(place, place, rank[:, 0:TB, :], ALU.add))
            link(nc.vector.tensor_scalar(late, rank[:, 0:TB, :], CAP - 0.5, BIG, ALU.is_gt, ALU.mult))
            if CAP < SL:
                link(nc.vector.tensor_tensor(place, place, late, ALU.add))
            it4 = bc(iota.unsqueeze(1), [P, GX, SL])

            def onehots(g):
                for b in range(TB):
                    pl = place[:, b, bass.ts(g, GX)]
                    nc.vector.tensor_tensor(gh[:, b, :].rearrange("p (q s) -> p q s", q=GX), it4,
                                            bc(pl.unsqueeze(2), [P, GX, SL]), ALU.is_equal).then_inc(onehot_ready, 1)
            onehots(0)
            nc.vector.tensor_scalar(over, rank[0:1, 2, :], CAP + 0.5, None, ALU.is_gt).then_inc(rank_read, 1)
            dve.wait_ge(r_exp, 1)
            link(nc.vector.tensor_reduce(psel, ex, AX.X, ALU.add))
            link(nc.vector.tensor_scalar(s1, d12, 1.0, None, ALU.add))
            link(nc.vector.tensor_tensor(s1, s1, psel, ALU.mult))
            link(nc.vector.reciprocal(w_1, s1))
            link(nc.vector.tensor_tensor(w_2, w_1, d12, ALU.mult))
            link(nc.vector.tensor_tensor(oh1, oh1, bc(w_1, [P, TB, NE]), ALU.mult))
            link(nc.vector.tensor_tensor(oh2, oh2, bc(w_2, [P, TB, NE]), ALU.mult))
            link(nc.vector.tensor_tensor(coef, oh1, oh2, ALU.add))

            def group(g):
                dve.wait_ge(onehot_ready, g * 2 + 2)
                dve.wait_ge(swT_ready, g + ONE)
                for b in range(TB):
                    cf = coef[:, b, bass.ts(g, GX)]
                    nc.vector.tensor_tensor(sw[:, b, :].rearrange("p (q s) -> p q s", q=GX),
                                            gh[:, b, :].rearrange("p (q s) -> p q s", q=GX),
                                            bc(cf.unsqueeze(2), [P, GX, SL]), ALU.mult).then_inc(sw_ready, 1)
                for q in range(GX):
                    hp = pair[0][:, q % 2, :]
                    yp = pair[1][:, q % 2, :]
                    dve.wait_ge(ge_exp, g * GX + (q + 1))
                    dve.wait_ge(ghT_ready, g * GX + q + ONE)
                    link(nc.vector.scalar_tensor_tensor(ghid, geh, 1.0, hp[:, 0:P], ALU.add, ALU.mult))
                    nc.vector.tensor_tensor(ghid, ghid, hp[:, P:2 * P], ALU.mult).then_inc(ghid_ready, 1)
                    dve.wait_ge(quarter_used, g * (4 * GX) + (4 * q + 4))
                    for c in (2, 3):
                        nc.vector.tensor_copy(yg[q * SL:(q + 1) * SL, c * CH:(c + 1) * CH], yp[c * SL:(c + 1) * SL, :])\
                            .then_inc(yg_dve, 1)
                for b in range(TB):
                    for c in range(NC):
                        dve.wait_ge(back_ready, g * (2 * NC) + (b * NC + c + 1))
                        h_c = resid[:, b, c * CH:(c + 1) * CH]
                        nc.vector.tensor_tensor(h_c, h_c, four[:, c, :], ALU.add).then_inc(scattered, 1)
            with dve.Fori(0, GROUPS - 1) as g:
                chain.enter(g, GX)
                group(g)
                dve.wait_ge(gathered, g * 2 + 2 + ONE)
                dve.wait_ge(sw_ready, g * 2 + 2)
                onehots(g + 1)
            chain.leave(GROUPS - 1)
            dve.wait_ge(rank_read, 1)
            link(nc.vector.tensor_tensor_scan(upto, cst[0:1, K_ONE:K_ONE + NE], over, 0.0, ALU.mult, ALU.add))
            link(nc.vector.tensor_tensor(llist, bc(cst[0:1, K_IOTA + 1:K_IOTA + 1 + LIST].unsqueeze(2), [1, LIST, NE]),
                                         bc(upto.unsqueeze(1), [1, LIST, NE]), ALU.is_equal))
            link(nc.vector.tensor_tensor(over, over, iota[0:1, :], ALU.mult))
            link(nc.vector.tensor_tensor(llist, llist, bc(over.unsqueeze(1), [1, LIST, NE]), ALU.mult))
            link(nc.vector.tensor_reduce(idx[:, 0:LIST], llist, AX.X, ALU.add))
            link(nc.vector.tensor_copy(idx[:, LIST:LIST + 1], upto[:, NE - 1:NE]))
            link(nc.vector.scalar_tensor_tensor(ocoef, late, 1.0 / BIG, coef, ALU.mult, ALU.mult))
            nc.vector.tensor_copy(over_i[0:1, :], idx).then_inc(over_ready, 1)
            group(GROUPS - 1)
            dve.wait_ge(scattered, GROUPS * 2 * NC + ONE)
            dve.wait_ge(over_ready, 1)
            n_over = dve.value_load(over_i[0:1, LIST:LIST + 1], min_val=0, max_val=LIST)
            with dve.If(n_over > 0):
                with dve.Fori(0, n_over) as e:
                    ex_e = dve.value_load(over_i[0:1, bass.ds(e, 1)], min_val=0, max_val=NE - 1)
                    chain_o = Chain(dve, over_step)
                    chain_o.enter(e, 2 * 2 + 1)
                    dve.wait_ge(y_added, e * 2 * NC + ONE)
                    chain_o.link(nc.vector.tensor_scalar(small[:, 16:18].rearrange("p (b o) -> p b o", b=TB),
                                                         ocoef[:, :, bass.ds(ex_e, 1)], 1.0, None, ALU.mult))
                    for b in range(TB):
                        dve.wait_ge(e_exp, e * 2 + (b + 1))
                        dve.wait_ge(hidT_ready, e * 2 + b + ONE)
                        chain_o.link(nc.vector.tensor_scalar(ehid[:, b, :], ehid[:, b, :], 1.0, stat[:, 8 + b:9 + b],
                                                             ALU.add, ALU.mult))
                        chain_o.link(nc.vector.tensor_tensor(hid[:, b, :], ehid[:, b, :], pair[b][:, 0, :], ALU.mult))
                        nc.vector.scalar_tensor_tensor(hid[:, b, :], pair[b][:, 1, :], half_rstd[:, b:b + 1], hid[:, b, :],
                                                       ALU.mult, ALU.mult).then_inc(hid_ready, 1)
                    for b in range(TB):
                        for c in range(NC):
                            dve.wait_ge(oy_ready, e * 8 + (b * 4 + c + 1) + ONE)
                            h_c = resid[:, b, c * CH:(c + 1) * CH]
                            nc.vector.scalar_tensor_tensor(h_c, four[:, c, :], small[:, 16 + b:17 + b], h_c,
                                                           ALU.mult, ALU.add).then_inc(y_added, 1)
            nc.vector.tensor_copy(small[:, 20:21], small[:, 0:1]).then_inc(resid_done, 1)
            dve.wait_ge(resid_done, 1)
            link(mean_square_dve(1, gates[:, 1, 0:D], resid[:, 1, :], 12))
            dve.wait_ge(ms_done, 2)
            dve.wait_ge(g3_in, 16)
            rstd(stat[:, 12:14])
            for b in range(TB):
                for cols in (slice(0, D // 2), slice(D // 2, D)):
                    nc.vector.scalar_tensor_tensor(resid[:, b, cols], resid[:, b, cols], stat[:, 12 + b:13 + b], norm_g[:, cols],
                                                   ALU.mult, ALU.mult).then_inc(o_ready, 1)


_INS = ["x", "w_in", "attn_sinks", "hgrn_lb_logits", "hgrn_norm_g", "w_br_attn", "w_br_hgrn", "w_out",
        "mix_norm_g", "moe_norm_g", "w_router_group", "b_router_group", "w_router_expert",
        "b_router_expert", "w1", "w3", "w2", "final_norm_g"]


def kernel(**inputs):
    import numpy as np
    import concourse.bacc as bacc
    from concourse.bass_utils import run_bass_kernel_spmd as run

    nc = bacc.Bacc("TRN2", target_bir_lowering=False, num_devices=1)
    arrays, args = {}, []
    for name in _INS + ["consts"]:
        a = constants() if name == "consts" else np.ascontiguousarray(inputs[name])
        arrays[f"in_{name}"] = a
        args.append(nc.dram_tensor(f"in_{name}", a.shape, mybir.dt.from_np(a.dtype), kind="ExternalInput").ap())
    res = nc.dram_tensor("result", (1, T, D), F32, kind="ExternalOutput").ap()
    hybrid_block(nc, *args, res)
    r = run(nc, [arrays], core_ids=[0])
    return r.results[0]["result"]
```
